# Optimizing a Trainium2 kernel written in Bass

```python
import jax, jax.numpy as jnp
from jax import lax
import numpy as np

D_MODEL = 1024
BATCH = 1
SEQ = 1024
DEPTH = 1

GRID_W = 64
CTX_LEN = 256
HGRN_HEADS = 4
HGRN_DK = 128
HGRN_DV = 128
HGRN_WIDTH = HGRN_HEADS * HGRN_DK
HGRN_CHUNK = 64
SGU_GROUPS = 4
SGU_CHUNK = 128
SGU_WIDTH = 512
SGU_GROUP_DIM = SGU_WIDTH // SGU_GROUPS
ROWS_PER_SGU_CHUNK = SGU_CHUNK // GRID_W
N_EXPERTS = 16
EXPERT_FF = 2048
CAPACITY_FACTOR = 2
N_MOD = 6
EPS = 1e-6
IN_COLS = 5 * HGRN_WIDTH + 2 * SGU_WIDTH + 2 * D_MODEL


def rmsnorm(x, w):
    xf = x.astype(jnp.float32)
    y = xf * lax.rsqrt(jnp.mean(xf * xf, axis=-1, keepdims=True) + EPS)
    return (y * w.astype(jnp.float32)).astype(x.dtype)

def adaln(cond, w, b):
    m = jax.nn.silu(cond) @ w + b
    m = m.reshape((-1, 1, N_MOD * D_MODEL))
    return jnp.split(m, N_MOD, axis=-1)

def modulate(h, shift, scale):
    return h * (1 + scale) + shift

def split_in(p):
    sizes = (HGRN_WIDTH,) * 5 + (SGU_WIDTH,) * 2 + (D_MODEL,) * 2
    idx = []
    acc = 0
    for s in sizes[:-1]:
        acc += s
        idx.append(acc)
    return jnp.split(p, idx, axis=-1)

def to_heads(a):
    return a.reshape(a.shape[0], a.shape[1], HGRN_HEADS, HGRN_DK)

def hgrn_forget(z, lb):
    f = lb + (1 - lb) * jax.nn.sigmoid(z.astype(jnp.float32))
    return jnp.log(f), 1 - f

def hgrn_chunk_scan(q, k, logf, v, s0):
    B_, T, H, DK = q.shape
    DV = v.shape[-1]
    nc = T // HGRN_CHUNK

    def to_chunks(a):
        return a.astype(jnp.float32).reshape(B_, nc, HGRN_CHUNK, H, a.shape[-1]).transpose(1, 0, 3, 2, 4)

    qc, kc, fc, vc = to_chunks(q), to_chunks(k), to_chunks(logf), to_chunks(v)
    mask = jnp.tril(jnp.ones((HGRN_CHUNK, HGRN_CHUNK), dtype=bool))[None, None, :, :, None]

    def step(S, inp):
        qb, kb, fb, vb = inp
        b = jnp.cumsum(fb, axis=2)
        diff = b[:, :, :, None, :] - b[:, :, None, :, :]
        decay = jnp.exp(jnp.where(mask, diff, -jnp.inf))
        scores = jnp.einsum('bhik,bhijk->bhij', qb, decay * kb[:, :, None, :, :])
        o = jnp.einsum('bhij,bhjv->bhiv', scores, vb) + jnp.einsum('bhik,bhkv->bhiv', qb * jnp.exp(b), S)
        b_last = b[:, :, -1:, :]
        S_new = jnp.exp(b_last[:, :, 0, :])[..., None] * S + jnp.einsum('bhjk,bhjv->bhkv', kb * jnp.exp(b_last - b), vb)
        return S_new, o

    s_fin, o = lax.scan(step, s0.astype(jnp.float32), (qc, kc, fc, vc))
    o = o.transpose(1, 0, 3, 2, 4).reshape(B_, T, H, DV)
    return o, s_fin

def hgrn_final_state(k, logf, v):
    b = jnp.cumsum(logf.astype(jnp.float32), axis=1)
    w = k.astype(jnp.float32) * jnp.exp(b[:, -1:] - b)
    return jnp.einsum('bthk,bthv->bhkv', w, v.astype(jnp.float32))

def sgu(u, v, norm_w, w_s, b_s, n_chunks):
    B_, T, _ = u.shape
    u = jax.nn.gelu(u).reshape(B_, n_chunks, SGU_CHUNK, SGU_GROUPS, SGU_GROUP_DIM)
    v = jax.nn.gelu(v).reshape(B_, T, SGU_GROUPS, SGU_GROUP_DIM)
    v = rmsnorm(v, norm_w.reshape(SGU_GROUPS, SGU_GROUP_DIM))
    v = v.reshape(B_, n_chunks, SGU_CHUNK, SGU_GROUPS, SGU_GROUP_DIM)
    mixed = jnp.einsum('gts,bnsgc->bntgc', w_s, v) + b_s.T[:, :, None]
    return (u * mixed).reshape(B_, T, SGU_WIDTH)

def token_mixer(parts, lb_f, lb_b, hgrn_norm_w, sgu_norm_w, sgu_w, sgu_b,
                w_branch_a, w_branch_b, w_out, s0_f, s0_b, n_sgu_chunks):
    q_p, ff_p, fb_p, v_p, g_p, u_p, sv_p, ga_p, gb_p = parts
    q = jax.nn.silu(to_heads(q_p))
    v = to_heads(v_p)
    logf_f, k_f = hgrn_forget(to_heads(ff_p), lb_f)
    logf_b, k_b = hgrn_forget(to_heads(fb_p), lb_b)
    o_f, s_f = hgrn_chunk_scan(q, k_f, logf_f, v, s0_f)
    o_b, s_b = hgrn_chunk_scan(q[:, ::-1], k_b[:, ::-1], logf_b[:, ::-1], v[:, ::-1], s0_b)
    o = o_f + o_b[:, ::-1]
    o = rmsnorm(o, hgrn_norm_w.reshape(HGRN_HEADS, HGRN_DV)).astype(g_p.dtype)
    o = o.reshape(o.shape[0], o.shape[1], HGRN_WIDTH) * jax.nn.silu(g_p)
    y_a = o @ w_branch_a
    y_b = sgu(u_p, sv_p, sgu_norm_w, sgu_w, sgu_b, n_sgu_chunks) @ w_branch_b
    merged = jax.nn.sigmoid(ga_p) * y_a + jax.nn.sigmoid(gb_p) * y_b
    return merged @ w_out, s_f, s_b

def moe_expert_choice(h, router_w, w_gate, w_up, w_down):
    B_, T, _ = h.shape
    cap = CAPACITY_FACTOR * T // N_EXPERTS
    aff = jax.nn.softmax((h @ router_w).astype(jnp.float32), axis=-1)
    gate, idx = lax.top_k(jnp.swapaxes(aff, 1, 2), cap)
    bidx = jnp.arange(B_)[:, None, None]
    xs = h[bidx, idx]
    hid = jax.nn.silu(jnp.einsum('becd,edf->becf', xs, w_gate)) * jnp.einsum('becd,edf->becf', xs, w_up)
    ye = jnp.einsum('becf,efd->becd', hid, w_down) * gate[..., None].astype(h.dtype)
    return jnp.zeros_like(h).at[bidx, idx].add(ye)

def first_inputs(seed: int = 0) -> dict:
    key = jax.random.key(seed)
    ks = jax.random.split(key, 24)
    f32 = jnp.float32
    nrm = lambda k, shape, s: jax.random.normal(k, shape, f32) * s
    return {
        'x': nrm(ks[0], (BATCH, SEQ, D_MODEL), 1.0),
        'c': nrm(ks[1], (BATCH, D_MODEL), 1.0),
        'ctx': nrm(ks[2], (BATCH, CTX_LEN, D_MODEL), 1.0),
        'c_ctx': nrm(ks[3], (D_MODEL,), 1.0),
        'ada_w': nrm(ks[4], (DEPTH, D_MODEL, N_MOD * D_MODEL), 0.02),
        'ada_b': nrm(ks[5], (DEPTH, N_MOD * D_MODEL), 0.02),
        'norm_mix_w': 1 + nrm(ks[6], (DEPTH, D_MODEL), 0.05),
        'norm_ffn_w': 1 + nrm(ks[7], (DEPTH, D_MODEL), 0.05),
        'w_in': nrm(ks[8], (DEPTH, D_MODEL, IN_COLS), D_MODEL ** -0.5),
        'hgrn_lb_logits': nrm(ks[9], (2, DEPTH + 1, HGRN_WIDTH), 0.5),
        'hgrn_norm_w': 1 + nrm(ks[10], (DEPTH, HGRN_WIDTH), 0.05),
        'sgu_norm_w': 1 + nrm(ks[11], (DEPTH, SGU_WIDTH), 0.05),
        'sgu_w': nrm(ks[12], (DEPTH, SGU_GROUPS, SGU_CHUNK, SGU_CHUNK), SGU_CHUNK ** -0.5),
        'sgu_b': 1 + nrm(ks[13], (DEPTH, SGU_GROUPS, SGU_CHUNK), 0.05),
        'w_branch_a': nrm(ks[14], (DEPTH, HGRN_WIDTH, D_MODEL), HGRN_WIDTH ** -0.5),
        'w_branch_b': nrm(ks[15], (DEPTH, SGU_WIDTH, D_MODEL), SGU_WIDTH ** -0.5),
        'w_out': nrm(ks[16], (DEPTH, D_MODEL, D_MODEL), D_MODEL ** -0.5),
        'router_w': nrm(ks[17], (DEPTH, D_MODEL, N_EXPERTS), D_MODEL ** -0.5),
        'expert_w_gate': nrm(ks[18], (DEPTH, N_EXPERTS, D_MODEL, EXPERT_FF), D_MODEL ** -0.5),
        'expert_w_up': nrm(ks[19], (DEPTH, N_EXPERTS, D_MODEL, EXPERT_FF), D_MODEL ** -0.5),
        'expert_w_down': nrm(ks[20], (DEPTH, N_EXPERTS, EXPERT_FF, D_MODEL), EXPERT_FF ** -0.5),
        'final_norm_w': 1 + nrm(ks[21], (D_MODEL,), 0.05),
    }

def first_block(x, c, ctx, c_ctx, ada_w, ada_b, norm_mix_w, norm_ffn_w, w_in, hgrn_lb_logits,
              hgrn_norm_w, sgu_norm_w, sgu_w, sgu_b, w_branch_a, w_branch_b, w_out, router_w,
              expert_w_gate, expert_w_up, expert_w_down, final_norm_w):
    B_, N, _ = x.shape
    ROWS = N // GRID_W
    n_sgu_lat = ROWS // ROWS_PER_SGU_CHUNK
    n_sgu_ctx = ctx.shape[1] // SGU_CHUNK
    lb_all = jnp.cumsum(jax.nn.softmax(hgrn_lb_logits.astype(jnp.float32), axis=1), axis=1)
    for l in range(DEPTH):
        last = l == DEPTH - 1
        lb_f = lb_all[0, l].reshape(HGRN_HEADS, HGRN_DK)
        lb_b = lb_all[1, l].reshape(HGRN_HEADS, HGRN_DK)
        sh_m, sc_m, g_m, sh_f, sc_f, g_f = adaln(c, ada_w[l], ada_b[l])
        csh_m, csc_m, cg_m, csh_f, csc_f, cg_f = adaln(c_ctx, ada_w[l], ada_b[l])

        h_ctx = modulate(rmsnorm(ctx, norm_mix_w[l]), csh_m, csc_m)
        pc = split_in(h_ctx @ w_in[l])
        if last:
            v_c = to_heads(pc[3])
            logf_f, k_f = hgrn_forget(to_heads(pc[1]), lb_f)
            logf_b, k_b = hgrn_forget(to_heads(pc[2]), lb_b)
            s_f = hgrn_final_state(k_f, logf_f, v_c)
            s_b = hgrn_final_state(k_b[:, ::-1], logf_b[:, ::-1], v_c[:, ::-1])
        else:
            zeros = jnp.zeros((ctx.shape[0], HGRN_HEADS, HGRN_DK, HGRN_DV), jnp.float32)
            y_c, s_f, s_b = token_mixer(pc, lb_f, lb_b, hgrn_norm_w[l], sgu_norm_w[l], sgu_w[l], sgu_b[l],
                                        w_branch_a[l], w_branch_b[l], w_out[l], zeros, zeros, n_sgu_ctx)
            ctx = ctx + cg_m * y_c
            h2c = modulate(rmsnorm(ctx, norm_ffn_w[l]), csh_f, csc_f)
            ctx = ctx + cg_f * moe_expert_choice(h2c, router_w[l], expert_w_gate[l], expert_w_up[l], expert_w_down[l])

        h = modulate(rmsnorm(x, norm_mix_w[l]), sh_m, sc_m)
        pl = split_in(h @ w_in[l])
        y, _, _ = token_mixer(pl, lb_f, lb_b, hgrn_norm_w[l], sgu_norm_w[l], sgu_w[l], sgu_b[l],
                              w_branch_a[l], w_branch_b[l], w_out[l], s_f, s_b, n_sgu_lat)
        x = x + g_m * y
        h2 = modulate(rmsnorm(x, norm_ffn_w[l]), sh_f, sc_f)
        x = x + g_f * moe_expert_choice(h2, router_w[l], expert_w_gate[l], expert_w_up[l], expert_w_down[l])
    return rmsnorm(x, final_norm_w)


N_HEADS = 8
N_KV_HEADS = 2
HEAD_DIM = 64
GQA_GROUP = N_HEADS // N_KV_HEADS
ATTN_WIDTH = N_HEADS * HEAD_DIM
KV_WIDTH = N_KV_HEADS * HEAD_DIM
LRU_WIDTH = D_MODEL - ATTN_WIDTH
LRU_BLOCKS = 8
LRU_BLOCK = LRU_WIDTH // LRU_BLOCKS
LRU_C = 8.0
LRU_CONV_W = 4
D_FF = 3 * D_MODEL
FFN_CONV_W = 3
Q_BLOCK = 128
ROPE_THETA = 10000.0
IN_WIDTH = ATTN_WIDTH + 2 * KV_WIDTH + 2 * LRU_WIDTH


def rms_norm(x, g):
    xf = x.astype(jnp.float32)
    y = xf * lax.rsqrt(jnp.mean(xf * xf, axis=-1, keepdims=True) + EPS)
    return (y * g.astype(jnp.float32)).astype(x.dtype)

def depthwise_conv(x, w, b, left, right):
    y = lax.conv_general_dilated(
        x, w[:, None, :].astype(x.dtype), window_strides=(1,), padding=[(left, right)],
        dimension_numbers=("NWC", "WIO", "NWC"), feature_group_count=x.shape[-1])
    return y + b.astype(x.dtype)

def rope_1d(x, pos):
    d = x.shape[-1]
    inv_freq = 1.0 / (ROPE_THETA ** (jnp.arange(0, d, 2, dtype=jnp.float32) / d))
    ang = pos.astype(jnp.float32)[:, None] * inv_freq[None, :]
    cos = jnp.cos(ang)[None, :, None, :]
    sin = jnp.sin(ang)[None, :, None, :]
    xf = x.astype(jnp.float32)
    x1, x2 = xf[..., : d // 2], xf[..., d // 2:]
    return jnp.concatenate([x1 * cos - x2 * sin, x2 * cos + x1 * sin], axis=-1).astype(x.dtype)

def axial_rope(x, row, col):
    half = x.shape[-1] // 2
    return jnp.concatenate([rope_1d(x[..., :half], row), rope_1d(x[..., half:], col)], axis=-1)

def block_attention(q, k, v):
    B, S = q.shape[0], q.shape[1]
    nb = S // Q_BLOCK
    qg = q.reshape(B, nb, Q_BLOCK, N_KV_HEADS, GQA_GROUP, HEAD_DIM).transpose(1, 0, 2, 3, 4, 5)

    def one_block(qb):
        s = jnp.einsum("bqkgd,bskd->bkgqs", qb, k).astype(jnp.float32)
        p = jax.nn.softmax(s, axis=-1).astype(v.dtype)
        return jnp.einsum("bkgqs,bskd->bqkgd", p, v)

    o = lax.map(one_block, qg)
    return o.transpose(1, 0, 2, 3, 4, 5).reshape(B, S, ATTN_WIDTH)

def _linear_combine(left, right):
    a1, b1 = left
    a2, b2 = right
    return a1 * a2, a2 * b1 + b2

def rg_lru(xc, wa, ba, wx, bx, lam, reverse):
    B, S, _ = xc.shape
    xf = xc.astype(jnp.float32)
    xb = xf.reshape(B, S, LRU_BLOCKS, LRU_BLOCK)
    r = jax.nn.sigmoid(jnp.einsum("bshi,hij->bshj", xb, wa.astype(jnp.float32)) + ba.astype(jnp.float32))
    i = jax.nn.sigmoid(jnp.einsum("bshi,hij->bshj", xb, wx.astype(jnp.float32)) + bx.astype(jnp.float32))
    r = r.reshape(B, S, LRU_WIDTH)
    i = i.reshape(B, S, LRU_WIDTH)
    log_a = LRU_C * r * jax.nn.log_sigmoid(lam.astype(jnp.float32))
    a = jnp.exp(log_a)
    mult = jnp.sqrt(-jnp.expm1(2.0 * log_a))
    start = S - 1 if reverse else 0
    mult = jnp.where((jnp.arange(S) == start)[None, :, None], 1.0, mult)
    b = mult * i * xf
    _, h = lax.associative_scan(_linear_combine, (a, b), reverse=reverse, axis=1)
    return h

def second_inputs(seed: int = 0) -> dict:
    key = jax.random.key(seed)
    ks = jax.random.split(key, 32)
    f32 = jnp.float32

    def nrm(k, shape, scale):
        return jax.random.normal(k, shape, f32) * scale

    def gain(k, shape):
        return 1.0 + 0.02 * jax.random.normal(k, shape, f32)

    def lam_init(k):
        u = jax.random.uniform(k, (DEPTH, LRU_WIDTH), f32, 0.9, 0.999)
        a = u ** (1.0 / LRU_C)
        return jnp.log(a) - jnp.log1p(-a)

    L = DEPTH
    return {
        "x": jax.random.normal(ks[0], (BATCH, SEQ, D_MODEL), f32),
        "norm1_g": gain(ks[1], (L, D_MODEL)),
        "w_in": nrm(ks[2], (L, D_MODEL, IN_WIDTH), D_MODEL ** -0.5),
        "q_norm_g": gain(ks[3], (L, HEAD_DIM)),
        "k_norm_g": gain(ks[4], (L, HEAD_DIM)),
        "lru_conv_w": nrm(ks[5], (L, LRU_CONV_W, LRU_WIDTH), LRU_CONV_W ** -0.5),
        "lru_conv_b": nrm(ks[6], (L, LRU_WIDTH), 0.01),
        "wa_f": nrm(ks[7], (L, LRU_BLOCKS, LRU_BLOCK, LRU_BLOCK), LRU_BLOCK ** -0.5),
        "ba_f": nrm(ks[8], (L, LRU_BLOCKS, LRU_BLOCK), 0.01),
        "wx_f": nrm(ks[9], (L, LRU_BLOCKS, LRU_BLOCK, LRU_BLOCK), LRU_BLOCK ** -0.5),
        "bx_f": nrm(ks[10], (L, LRU_BLOCKS, LRU_BLOCK), 0.01),
        "lam_f": lam_init(ks[11]),
        "wa_b": nrm(ks[12], (L, LRU_BLOCKS, LRU_BLOCK, LRU_BLOCK), LRU_BLOCK ** -0.5),
        "ba_b": nrm(ks[13], (L, LRU_BLOCKS, LRU_BLOCK), 0.01),
        "wx_b": nrm(ks[14], (L, LRU_BLOCKS, LRU_BLOCK, LRU_BLOCK), LRU_BLOCK ** -0.5),
        "bx_b": nrm(ks[15], (L, LRU_BLOCKS, LRU_BLOCK), 0.01),
        "lam_b": lam_init(ks[16]),
        "w_out": nrm(ks[17], (L, D_MODEL, D_MODEL), D_MODEL ** -0.5),
        "norm2_g": gain(ks[18], (L, D_MODEL)),
        "w_up": nrm(ks[19], (L, D_MODEL, 2 * D_FF), D_MODEL ** -0.5),
        "up_conv_w": nrm(ks[20], (L, FFN_CONV_W, 2 * D_FF), FFN_CONV_W ** -0.5),
        "up_conv_b": nrm(ks[21], (L, 2 * D_FF), 0.01),
        "w_down": nrm(ks[22], (L, D_FF, D_MODEL), D_FF ** -0.5),
        "final_g": gain(ks[23], (D_MODEL,)),
    }

def second_block(x, norm1_g, w_in, q_norm_g, k_norm_g, lru_conv_w, lru_conv_b,
              wa_f, ba_f, wx_f, bx_f, lam_f, wa_b, ba_b, wx_b, bx_b, lam_b,
              w_out, norm2_g, w_up, up_conv_w, up_conv_b, w_down, final_g):
    B, S, _ = x.shape
    rows = S // GRID_W
    row = jnp.repeat(jnp.arange(rows, dtype=jnp.int32), GRID_W)
    col = jnp.tile(jnp.arange(GRID_W, dtype=jnp.int32), rows)
    splits = [ATTN_WIDTH, ATTN_WIDTH + KV_WIDTH, ATTN_WIDTH + 2 * KV_WIDTH,
              ATTN_WIDTH + 2 * KV_WIDTH + LRU_WIDTH]

    for l in range(DEPTH):
        h = rms_norm(x, norm1_g[l])
        z = h @ w_in[l]
        q, k, v, xr, yr = jnp.split(z, splits, axis=-1)

        q = rms_norm(q.reshape(B, S, N_HEADS, HEAD_DIM), q_norm_g[l])
        k = rms_norm(k.reshape(B, S, N_KV_HEADS, HEAD_DIM), k_norm_g[l])
        q = axial_rope(q, row, col) * (HEAD_DIM ** -0.5)
        k = axial_rope(k, row, col)
        v = v.reshape(B, S, N_KV_HEADS, HEAD_DIM)
        attn_out = block_attention(q, k, v)

        xc = depthwise_conv(xr, lru_conv_w[l], lru_conv_b[l], 2, 1)
        h_fwd = rg_lru(xc, wa_f[l], ba_f[l], wx_f[l], bx_f[l], lam_f[l], False)
        h_bwd = rg_lru(xc, wa_b[l], ba_b[l], wx_b[l], bx_b[l], lam_b[l], True)
        lru_out = ((h_fwd + h_bwd) * jax.nn.gelu(yr.astype(jnp.float32))).astype(x.dtype)

        mixed = jnp.concatenate([attn_out, lru_out], axis=-1) @ w_out[l]
        x = x + mixed

        h = rms_norm(x, norm2_g[l])
        u = depthwise_conv(h @ w_up[l], up_conv_w[l], up_conv_b[l], 1, 1)
        gate, val = jnp.split(u, 2, axis=-1)
        x = x + (jax.nn.gelu(gate) * val) @ w_down[l]

    return rms_norm(x, final_g)


def setup_inputs(seed=0):
    out = dict(first_inputs(seed))
    for name, value in second_inputs(seed + 1).items():
        if name != "x":
            out[name + "_2"] = value
    return out


def reference(
    x, c, ctx, c_ctx, ada_w, ada_b, norm_mix_w, norm_ffn_w, w_in, hgrn_lb_logits, hgrn_norm_w,
    sgu_norm_w, sgu_w, sgu_b, w_branch_a, w_branch_b, w_out, router_w, expert_w_gate,
    expert_w_up, expert_w_down, final_norm_w, norm1_g_2, w_in_2, q_norm_g_2, k_norm_g_2,
    lru_conv_w_2, lru_conv_b_2, wa_f_2, ba_f_2, wx_f_2, bx_f_2, lam_f_2, wa_b_2, ba_b_2, wx_b_2,
    bx_b_2, lam_b_2, w_out_2, norm2_g_2, w_up_2, up_conv_w_2, up_conv_b_2, w_down_2, final_g_2,
):
    x = first_block(
        x, c, ctx, c_ctx, ada_w, ada_b, norm_mix_w, norm_ffn_w, w_in, hgrn_lb_logits,
        hgrn_norm_w, sgu_norm_w, sgu_w, sgu_b, w_branch_a, w_branch_b, w_out, router_w,
        expert_w_gate, expert_w_up, expert_w_down, final_norm_w,
    )
    return second_block(
        x, norm1_g_2, w_in_2, q_norm_g_2, k_norm_g_2, lru_conv_w_2, lru_conv_b_2, wa_f_2,
        ba_f_2, wx_f_2, bx_f_2, lam_f_2, wa_b_2, ba_b_2, wx_b_2, bx_b_2, lam_b_2, w_out_2,
        norm2_g_2, w_up_2, up_conv_w_2, up_conv_b_2, w_down_2, final_g_2,
    )


_drawn_inputs = setup_inputs


def setup_inputs(seed=0):
    import zlib

    import numpy as np

    out = dict(_drawn_inputs(seed))
    spreads = {}
    factors = {'ctx': 8.0,
     'c_ctx': 8.0,
     'norm_ffn_w': 2.911,
     'hgrn_lb_logits': 6.973,
     'hgrn_norm_w': 3.864,
     'sgu_norm_w': 4.526,
     'sgu_b': 5.022,
     'norm1_g_2': 3.525,
     'q_norm_g_2': 8.0,
     'k_norm_g_2': 8.0,
     'ba_f_2': 64.0,
     'bx_f_2': 41.237,
     'ba_b_2': 64.0,
     'bx_b_2': 48.202,
     'norm2_g_2': 11.834,
     'up_conv_b_2': 24.032,
     'final_g_2': 8.071,
     'lru_conv_b_2': 3.806}
    for name, (base, spread) in spreads.items():
        noise = np.random.default_rng([zlib.crc32(name.encode()), seed]).standard_normal(out[name].shape)
        drawn = base * np.exp(spread * noise) if base else spread * noise
        out[name] = __import__('jax').numpy.asarray(drawn.astype(out[name].dtype))
    for name, factor in factors.items():
        out[name] = (out[name] * factor).astype(out[name].dtype)
    return out
```

```python
import numpy as np

import concourse.bass as bass
from concourse import mybir

F32 = mybir.dt.float32
U32 = mybir.dt.uint32
U8 = mybir.dt.uint8
ALU = mybir.AluOpType
ACT = mybir.ActivationFunctionType
AX = mybir.AxisListType

P = 128
D = 1024
T = 1024
DT = D // P
TT = T // P
BANK = 512
EPS = 1e-6

CTX = 256
HEADS = 4
WIDTH = 512
CHUNK = 128
LEVELS = [1, 2, 4, 8, 16, 32, 64]
NCH = T // CHUNK
GROUPS = 4
COL_Q, COL_FF, COL_FB, COL_V, COL_G, COL_U, COL_SV = (i * WIDTH for i in range(7))
COL_GA, COL_GB = 7 * WIDTH, 7 * WIDTH + D

NE = 16
CAP = 2 * T // NE
FF = 2048
ARENA = 51600
NEG = -1.0

QH, KVH, HD = 8, 2, 64
AW = QH * HD
KW = KVH * HD
LW = D - AW
LT = LW // P
CC_XR = AW + 2 * KW
CC_YR = CC_XR + LW
DFF = 3 * D
FT = DFF // P
LRU_C = 8.0


class Lane:

    def __init__(self, nc, engine, name, in_turn):
        self.nc, self.engine, self.name, self.in_turn = nc, engine, name, in_turn
        self.seen = {}
        self.sem, self.count, self.latest = None, 0, None

    def stage(self, name):
        self.label = f"{self.name}_{name}"
        self.sem, self.count = self.nc.alloc_semaphore(self.label), 0

    def after(self, *events):
        for event in events:
            if event is None:
                continue
            if isinstance(event, list):
                self.after(*event)
                continue
            sem, value, name = event
            if value > self.seen.get(name, 0):
                self.engine.wait_ge(sem, value)
                self.seen[name] = value
        return self.engine

    def mark(self, instruction):
        self.count += 1
        instruction.then_inc(self.sem, 1)
        self.latest = (self.sem, self.count, self.label)
        return self.latest

    def run(self, issue, *events):
        self.after(*events)
        if self.in_turn:
            self.after(self.latest)
        return self.mark(issue(self.engine))


class Transfers:

    def __init__(self, nc, name):
        self.sem, self.count, self.name = nc.alloc_semaphore(name), 0, name

    def start(self, lane, out, in_, *events):
        lane.after(*events).dma_start(out, in_).then_inc(self.sem, 16)
        self.count += 16
        return self.done()

    def done(self):
        return (self.sem, self.count, self.name)


class Ring:

    def __init__(self, nc, lane, name, slots, loads, free):
        self.lane, self.slots, self.loads = lane, slots, loads
        self.transfers = [Transfers(nc, f"{name}{i}") for i in range(len(slots))]
        self.issued = self.taken = 0
        for i in range(min(len(free), len(loads))):
            self.load(free[i])

    def load(self, *events):
        if self.issued < len(self.loads):
            i = self.issued % len(self.slots)
            out, in_ = self.loads[self.issued](self.slots[i])
            self.issued += 1
            self.transfers[i].start(self.lane, out, in_, *events)

    def take(self):
        assert self.taken < self.issued
        i = self.taken % len(self.slots)
        self.taken += 1
        return self.slots[i], self.transfers[i].done()

    def release(self, event):
        self.load(event)


class Core:

    def __init__(self, nc):
        self.nc = nc
        self.pe = Lane(nc, nc.tensor, "pe", False)
        self.dve = Lane(nc, nc.vector, "dve", True)
        self.act = Lane(nc, nc.scalar, "act", True)
        self.pool = Lane(nc, nc.gpsimd, "pool", True)
        self.sp = Lane(nc, nc.sync, "sp", False)
        self.ident = self.sb("ident", P)
        self.ones = self.sb("ones", P)
        self.masks = self.sb("masks", 15 * P, U8)
        self.vec = self.sb("vec", 4 * P)
        self.mod = self.sb("mod", 96)
        self.small = self.sb("small", 192)
        self.arena = self.sb("arena", ARENA)
        self.psum = nc.alloc_psum_tensor("psum", [P, 8 * BANK], F32)
        self.bank_free = [None] * 8
        self.where = {}

    def sb(self, name, n, dt=F32):
        return self.nc.alloc_sbuf_tensor(name, [P, n], dt)

    def stage(self, name):
        for lane in (self.pe, self.dve, self.act, self.pool):
            lane.stage(name)

    def everything(self):
        return [lane.latest for lane in (self.pe, self.dve, self.act, self.pool)]

    def view(self, at, n):
        assert at + n <= ARENA, (at, n)
        return self.arena[:, at:at + n]

    def bank(self, b, n=BANK):
        return self.psum[:, b * BANK:b * BANK + n]

    def col(self, name, i=0, n=1):
        return self.vec[:, self.where[name] + i:self.where[name] + i + n]

    def claim(self, b, n=1):
        self.pe.after(*self.bank_free[b:b + n])

    def freed(self, b, n, event):
        for i in range(b, b + n):
            self.bank_free[i] = event
        return event

    def matmuls(self, out, pairs, *events, step=None):
        self.pe.after(*events)
        for n, (lhsT, rhs) in enumerate(pairs):
            mm = self.pe.engine.matmul(out, lhsT, rhs, start=(n == 0), stop=(n == len(pairs) - 1))
        return self.pe.mark(mm)

    def turns(self, outs_ins, *events):
        self.pe.after(*events)
        for out, in_ in outs_ins:
            tr = self.pe.engine.transpose(out, in_, self.ident[0:in_.shape[0], 0:in_.shape[0]])
        return self.pe.mark(tr)


def tiled(slot, k):
    return slot.rearrange("p (k n) -> p k n", k=k)


def feature_tile(w, at, width=P):
    k = w.shape[0] // P
    src = w.rearrange("(k p) n -> p k n", p=P)[:, :, at:at + width]
    return lambda slot: (tiled(slot[:, 0:k * width], k), src)


def shape_constants():
    j, i = np.meshgrid(np.arange(P), np.arange(P), indexing="ij")
    masks = [j == i]
    for h in LEVELS:
        same = j // (2 * h) == i // (2 * h)
        masks.append(same & (j // h % 2 == 0) & (i // h % 2 == 1))
    for h in LEVELS:
        same = j // (2 * h) == i // (2 * h)
        masks.append(same & (j // h % 2 == 1) & (i // h % 2 == 0))
    masks = np.stack(masks, 1).astype(np.float32).reshape(P, -1)
    quarter = HD // 4
    inverse = (np.float32(1.0) / np.float32(10000.0) ** (np.arange(0, HD // 2, 2, dtype=np.float32)
                                                         / np.float32(HD // 2))).astype(np.float32)
    token = np.arange(T)
    angles = np.stack([(token // 64).astype(np.float32)[:, None] * inverse,
                       (token % 64).astype(np.float32)[:, None] * inverse], 1).astype(np.float32)
    rope = np.stack([np.cos(angles), np.sin(angles)], 1).astype(np.float32)
    rope = rope.reshape(TT, P, 4 * quarter).transpose(1, 0, 2).reshape(P, -1)
    return {
        "identity": np.eye(P, dtype=np.float32),
        "pair_masks": masks,
        "rope_table": np.ascontiguousarray(rope),
    }


def row_scale(core, sums, n, *events):
    a = core.dve.run(lambda e: e.tensor_scalar(sums, sums, 1.0 / n, EPS, ALU.mult, ALU.add), *events)
    b = core.act.run(lambda e: e.activation(sums, sums, ACT.Sqrt), a)
    return core.dve.run(lambda e: e.reciprocal(sums, sums), b)


def norm_rows(core, tok, n_tiles, sums, junk, landed):
    for t in range(n_tiles):
        ev = core.act.run(lambda e: e.activation(junk, tok[:, t, :], ACT.Square, accum_out=sums[:, t:t + 1]),
                          landed[t])
    ready = row_scale(core, sums, D, ev)
    return [core.dve.run(lambda e: e.tensor_scalar(tok[:, t, :], tok[:, t, :], sums[:, t:t + 1], None, ALU.mult),
                         ready) for t in range(n_tiles)]


def turn_and_modulate(core, tok, n_tiles, j, b, out, scale, shift, *events):
    core.claim(b, 2)
    turned = core.turns([(core.bank(b, D)[:, t * P:(t + 1) * P], tok[:, t, j * P:(j + 1) * P])
                         for t in range(n_tiles)], *events)
    ev = core.act.run(lambda e: e.activation(out, core.bank(b, n_tiles * P), ACT.Identity, bias=shift, scale=scale),
                      turned)
    return core.freed(b, 2, ev)


HT, RING_A, WIDE, OT, YB = 0, 8192, 16384, 20480, 24576
VV, RAW, UNIT, KRT, SALL, VCTX = 28672, 32768, 39936, 46080, 47104, 48128
BSB, WST, S0, KC = 49152, 49664, 50176, 50432
MERGED, WOUT = UNIT, VV
GM_ROW, GF_ROW, XT = BSB, VCTX, YB


def start(core, ins):
    nc, pe, dve, act, sp = core.nc, core.pe, core.dve, core.act, core.sp
    core.stage("start")
    rows = core.view(38912, 4 * P).rearrange("p (n c) -> p n c", n=4)
    cleared = dve.run(lambda e: e.memset(core.view(38912, 4 * P), 0.0))
    core.ones_set = dve.run(lambda e: e.memset(core.ones[:, :], 1.0))
    core.eps = core.small[:, 184:185]
    core.eps_set = dve.run(lambda e: e.memset(core.eps, EPS))
    first = Transfers(nc, "dma_constants")
    first.start(sp, core.ident[:, :], ins["identity"])
    masks_f = core.view(RING_A, 15 * P)
    first.start(sp, masks_f, ins["pair_masks"])
    by_rows = lambda name: ins[name].rearrange("a (r p) -> (a r) p", p=P)
    pairs_of_blocks = lambda name: ins[name].rearrange("a (r h) j -> (a r) (h j)", h=2)
    vectors = [
        (0, "c", by_rows("c")), (0, "c_ctx", ins["c_ctx"].rearrange("(r p) -> r p", p=P)),
        (0, "norm_mix", by_rows("norm_mix_w")), (0, "ada_b", by_rows("ada_b")),
        (0, "lb", ins["hgrn_lb_logits"].rearrange("a b (r p) -> (a b r) p", p=P)),
        (0, "hgrn_norm", by_rows("hgrn_norm_w")), (0, "sgu_norm", by_rows("sgu_norm_w")),
        (0, "norm_ffn", by_rows("norm_ffn_w")), (1, "norm1", by_rows("norm1_g_2")),
        (1, "lru_conv_w", ins["lru_conv_w_2"].rearrange("a w (r p) -> (a w r) p", p=P)),
        (1, "lru_conv_b", by_rows("lru_conv_b_2")), (1, "ba_f", pairs_of_blocks("ba_f_2")),
        (1, "bx_f", pairs_of_blocks("bx_f_2")), (1, "ba_b", pairs_of_blocks("ba_b_2")),
        (1, "bx_b", pairs_of_blocks("bx_b_2")), (1, "lam_f", by_rows("lam_f_2")),
        (1, "lam_b", by_rows("lam_b_2")), (1, "norm2", by_rows("norm2_g_2")),
        (1, "up_conv_b", by_rows("up_conv_b_2")),
        (2, "up_conv_w01", ins["up_conv_w_2"][:, 0:2, :].rearrange("a w (r p) -> (a w r) p", p=P)),
        (3, "up_conv_w2", ins["up_conv_w_2"][:, 2:3, :].rearrange("a w (r p) -> (a w r) p", p=P)),
    ]
    used = [0] * 4
    for t, name, src in vectors:
        n = src.shape[0]
        first.start(sp, rows[used[t]:used[t] + n, t, :], src, cleared)
        core.where[name] = t * P + used[t]
        used[t] += n
        assert used[t] <= P
    x_tok = core.view(VV, TT * D).rearrange("p (t d) -> p t d", t=TT)
    ctx_tok = core.view(36864, 2 * D).rearrange("p (t d) -> p t d", t=2)
    ctx_in = Transfers(nc, "dma_ctx").start(sp, ctx_tok, ins["ctx"].rearrange("a (t p) d -> p (a t) d", p=P))
    x_dram = ins["x"].rearrange("a (t p) d -> p (a t) d", p=P)
    x_in = [Transfers(nc, f"dma_x{i}").start(sp, x_tok[:, 4 * i:4 * i + 4, :], x_dram[:, 4 * i:4 * i + 4, :])
            for i in range(2)]
    w_in = ins["w_in"][0]
    ada_slots = [core.view(at, 4096) for at in (RING_A + 4096, YB, 40960, 45056)]
    ada = Ring(nc, sp, "dma_ada", ada_slots, [feature_tile(ins["ada_w"][0], c * BANK, BANK) for c in range(4)],
               [None] * 4)
    wide_loads = [feature_tile(w_in, COL_V, BANK), feature_tile(w_in, COL_SV, BANK)]
    wide_loads += [feature_tile(ins["ada_w"][0], c * BANK, BANK) for c in range(4, 12)]
    core.wide = Ring(nc, sp, "dma_wide", [core.view(WIDE, 4096)], wide_loads, [None])
    order = []
    for h in range(HEADS):
        order += [COL_Q + h * P, COL_FF + h * P, COL_FB + h * P]
    order += [COL_U + g * P for g in range(GROUPS)] + [COL_G + h * P for h in range(HEADS)]
    loads = [feature_tile(w_in, at) for at in order]
    for j in range(DT):
        loads += [feature_tile(w_in, COL_GA + j * P), feature_tile(ins["w_branch_a"][0], j * P),
                  feature_tile(w_in, COL_GB + j * P), feature_tile(ins["w_branch_b"][0], j * P)]

    turned = core.turns([(core.bank(0)[:, t * P:(t + 1) * P], rows[:, t, :]) for t in range(4)], first.done())
    core.vec_ok = dve.run(lambda e: e.tensor_copy(core.vec[:, :], core.bank(0)), turned)
    core.freed(0, 1, core.vec_ok)
    core.masks_ok = dve.run(lambda e: e.tensor_copy(core.masks[:, :], masks_f))

    silu_c = core.small[:, 0:16].rearrange("p (k s) -> p k s", s=2)
    act.run(lambda e: e.activation(silu_c[:, :, 0], core.col("c", 0, 8), ACT.Silu), core.vec_ok)
    core.silu_ok = act.run(lambda e: e.activation(silu_c[:, :, 1], core.col("c_ctx", 0, 8), ACT.Silu))
    core.silu_c = silu_c
    core.ada_rows_free = None
    core.mod_v = core.mod[:, :].rearrange("p (j s) -> p j s", s=2)

    junk = core.view(39424, D)
    ctx_n = norm_rows(core, ctx_tok, 2, core.small[:, 16:18], junk, [ctx_in] * 2)
    x_n = norm_rows(core, x_tok, TT, core.small[:, 24:32], junk, [x_in[0]] * 4 + [x_in[1]] * 4)
    for c in range(4):
        for _ in ada_chunk(core, ada, c, c % 2):
            pass
    mix_scale = core.small[:, 32:48].rearrange("p (j s) -> p j s", s=2)
    for s in range(2):
        a = dve.run(lambda e: e.tensor_scalar(mix_scale[:, :, s], core.mod_v[:, 8:16, s], 1.0, None, ALU.add))
        ok = dve.run(lambda e: e.tensor_tensor(mix_scale[:, :, s], mix_scale[:, :, s], core.col("norm_mix", 0, 8),
                                               ALU.mult), a)
    core.hT = core.view(HT, DT * T).rearrange("p (j t) -> p j t", j=DT)
    core.hcT = core.view(YB, DT * CTX).rearrange("p (j t) -> p j t", j=DT)
    for j in range(DT):
        core.hc_ok = turn_and_modulate(core, ctx_tok, 2, j, 2 + 2 * (j % 3), core.hcT[:, j, :],
                                       mix_scale[:, j, 1:2], core.mod_v[:, j, 1:2], ctx_n, ok)
    for j in range(DT):
        core.h_ok = turn_and_modulate(core, x_tok, TT, j, 2 + 2 * (j % 3), core.hT[:, j, :],
                                      mix_scale[:, j, 0:1], core.mod_v[:, j, 0:1], x_n, ok)

    low, e0, e1 = core.small[:, 48:56], core.small[:, 56:64], core.small[:, 64:72]
    core.low, core.span = low, core.small[:, 72:80]
    for d in range(2):
        l0, l1, sl = core.col("lb", 8 * d, 4), core.col("lb", 8 * d + 4, 4), slice(4 * d, 4 * d + 4)
        dve.run(lambda e: e.tensor_tensor(low[:, sl], l0, l1, ALU.max))
        dve.run(lambda e: e.tensor_tensor(e0[:, sl], l0, low[:, sl], ALU.subtract))
        a = dve.run(lambda e: e.tensor_tensor(e1[:, sl], l1, low[:, sl], ALU.subtract))
    b = act.run(lambda e: e.activation(core.small[:, 56:72], core.small[:, 56:72], ACT.Exp), a)
    dve.run(lambda e: e.tensor_tensor(low, e0, e1, ALU.add), b)
    dve.run(lambda e: e.reciprocal(low, low))
    dve.run(lambda e: e.tensor_tensor(low, low, e0, ALU.mult))
    core.low_ok = dve.run(lambda e: e.tensor_scalar(core.span, low, -1.0, 1.0, ALU.mult, ALU.add))

    core.score = [core.view(UNIT + 3072 * d + 2048, NCH * CHUNK) for d in range(2)]
    for d in range(2):
        core.score_free = dve.run(lambda e: e.memset(core.score[d], 0.0), core.pe.latest, act.latest)

    sgu_rows = core.view(UNIT, GROUPS * P).rearrange("p (g s) -> p g s", g=GROUPS)
    core.sgu_wT = core.view(WST, GROUPS * P).rearrange("p (g t) -> p g t", g=GROUPS)
    core.sgu_bias = core.view(BSB, GROUPS * P)
    dma_sgu = Transfers(nc, "dma_sgu")
    dma_sgu.start(sp, sgu_rows, ins["sgu_w"][0].rearrange("g t s -> t g s"), core.everything())
    landed = dma_sgu.start(sp, core.sgu_bias, ins["sgu_b"].rearrange("a g t -> (a g t)").partition_broadcast(P))
    slots = [core.view(RING_A + 1024 * i, 1024) for i in range(8)]
    core.feat = Ring(nc, sp, "dma_feature", slots, loads, [core.masks_ok] * 4 + [core.pe.latest] * 4)
    core.claim(0)
    turned = core.turns([(core.bank(0)[:, g * P:(g + 1) * P], sgu_rows[:, g, :]) for g in range(GROUPS)], landed)
    ev = dve.run(lambda e: e.tensor_copy(core.view(WST, GROUPS * P), core.bank(0)), turned, landed)
    core.freed(0, 1, ev)
    core.sgu_ok = ev


def ada_chunk(core, ring, c, b):
    slot, landed = ring.take()
    w = tiled(slot, DT)
    core.pe.after(landed, core.silu_ok)
    core.claim(b)
    for k in range(DT):
        mm = core.pe.engine.matmul(core.bank(b)[0:2, :], core.silu_c[:, k, :], w[:, k, :], start=(k == 0),
                                   stop=(k == DT - 1))
        if k < DT - 1:
            yield
    summed = core.pe.mark(mm)
    ring.release(summed)
    rows = core.view(KC, BANK)[0:2, :]
    ev = core.dve.run(lambda e: e.tensor_copy(rows, core.bank(b)[0:2, :]), summed, core.ada_rows_free)
    yield
    out = core.bank(b, 8).rearrange("p (m s) -> p m s", s=2)
    core.ada_rows_free = turned = core.turns([(out[:, m, :], rows[:, m * P:(m + 1) * P]) for m in range(4)], ev)
    for s in range(2):
        ev = core.dve.run(lambda e: e.tensor_tensor(core.mod_v[:, 4 * c:4 * c + 4, s], out[:, :, s],
                                                    core.col("ada_b", 4 * c, 4), ALU.add), turned)
    core.freed(b, 1, ev)
    core.mod_ok = ev
    yield


def values(core):
    core.v = core.view(VV, TT * WIDTH).rearrange("p (t n) -> p t n", t=TT)
    core.vctx = core.view(VCTX, 2 * WIDTH).rearrange("p (t n) -> p t n", t=2)
    slot, landed = core.wide.take()
    w = tiled(slot, DT)
    x_free = core.everything()
    for t in range(TT + 2):
        src, out = (core.hT, core.v[:, t, :]) if t < TT else (core.hcT, core.vctx[:, t - TT, :])
        at = (t % TT if t < TT else t - TT) * P
        b = t % 4
        core.claim(b)
        mm = core.matmuls(core.bank(b), [(src[:, k, at:at + P], w[:, k, :]) for k in range(DT)], landed,
                          core.h_ok)
        lane = core.act if t % 2 else core.dve
        if t % 2:
            ev = core.act.run(lambda e: e.activation(out, core.bank(b), ACT.Copy), mm, x_free)
        else:
            ev = core.dve.run(lambda e: e.tensor_copy(out, core.bank(b)), mm, x_free)
        core.freed(b, 1, ev)
    core.wide.release(mm)
    core.v_ok = [core.act.latest, core.dve.latest]


def feature_halves(core, slot, landed, finish, k_of=None, banks=(6, 7)):
    src = core.hT if k_of is None else k_of
    n = src.shape[1]
    w = tiled(slot[:, 0:n * P], n)
    for half in range(2):
        b = banks[half]
        core.claim(b)
        core.pe.after(landed)
        for k in range(n):
            mm = core.pe.engine.matmul(core.bank(b), w[:, k, :], src[:, k, half * BANK:(half + 1) * BANK],
                                       start=(k == 0), stop=(k == n - 1))
            if k < n - 1:
                yield
        ev = core.pe.mark(mm)
        core.freed(b, 1, finish(half, b, ev))
        yield


def raw_head(core, h):
    r = RAW + 3584 * (h % 2)
    free = core.raw_free[h % 2]
    q = core.view(r, T)
    slot, landed = core.feat.take()
    yield from feature_halves(core, slot, landed, lambda half, b, ev: core.act.run(
        lambda e: e.activation(q[:, half * BANK:(half + 1) * BANK], core.bank(b), ACT.Silu), ev, free))
    core.feat.release(core.pe.latest)
    core.q_ok[h] = core.act.latest
    for d in range(2):
        f, fc = core.view(r + T * (d + 1), T), core.view(r + 3 * T + CTX * d, CTX)
        slot, landed = core.feat.take()
        w = tiled(slot, DT)
        low, span = core.low[:, 4 * d + h:4 * d + h + 1], core.span[:, 4 * d + h:4 * d + h + 1]

        def gate(out, b, n, ev):
            s = core.act.run(lambda e: e.activation(out, core.bank(b, n), ACT.Sigmoid), ev, free)
            core.f_ok[h] = core.pool.run(lambda e: e.tensor_scalar(out, out, span, low, ALU.mult, ALU.add),
                                         s, core.low_ok)
            return s
        yield from feature_halves(core, slot, landed, lambda half, b, ev: gate(
            f[:, half * BANK:(half + 1) * BANK], b, BANK, ev))
        b = 6
        core.claim(b)
        for k in range(DT):
            mm = core.pe.engine.matmul(core.bank(b, CTX), w[:, k, :], core.hcT[:, k, :], start=(k == 0),
                                       stop=(k == DT - 1))
            if k < DT - 1:
                yield
        ev = core.pe.mark(mm)
        core.feat.release(ev)
        core.freed(b, 1, gate(fc, b, CTX, ev))
        yield


def halves(ap, h):
    return ap.rearrange("p (n s h) -> p n s h", s=2, h=h)


def decay_step(core, lane, way, h, decay, key, query, *events):
    d = halves(decay, h)
    ends = h - 1 if way == 0 else 0
    old, new = (0, 1) if way == 0 else (1, 0)
    n = d.shape[1]
    k = halves(key, h)
    ev = lane.run(lambda e: e.tensor_tensor(k[:, :, old, :], k[:, :, old, :],
                                            d[:, :, new, ends:ends + 1].broadcast_to([P, n, h]), ALU.mult), *events)
    if query is not None:
        q = halves(query, h)
        ev = lane.run(lambda e: e.tensor_tensor(q[:, :, new, :], q[:, :, new, :],
                                                d[:, :, old, ends:ends + 1].broadcast_to([P, n, h]), ALU.mult))
    at = d[:, :, new, ends:ends + 1]
    return lane.run(lambda e: e.tensor_tensor(at, at, d[:, :, old, ends:ends + 1], ALU.mult), ev)


def head_scan(core, h, fill):
    pe, dve, act, pool = core.pe, core.dve, core.act, core.pool
    r = RAW + 3584 * (h % 2)
    q = core.view(r, T)
    f = [core.view(r + T * (d + 1), T) for d in range(2)]
    fc = [core.view(r + 3 * T + CTX * d, CTX) for d in range(2)]
    key = [core.view(UNIT + 3072 * d, T) for d in range(2)]
    query = [core.view(UNIT + 3072 * d + 1024, T) for d in range(2)]
    key_c = [core.view(KC + CTX * d, CTX) for d in range(2)]
    krt = core.view(KRT, NCH * P).rearrange("p (c k) -> p c k", c=NCH)
    states = core.view(SALL, NCH * P).rearrange("p (c v) -> p c v", c=NCH)
    s0 = [core.view(S0 + P * d, P) for d in range(2)]
    head_cols = slice(h * P, (h + 1) * P)
    ready, ready_c = [None] * 2, [None] * 2
    for d in range(2):
        dve.run(lambda e: e.tensor_scalar(key[d], f[d], -1.0, 1.0, ALU.mult, ALU.add), core.f_ok[h],
                core.unit_free[d])
        ready[d] = dve.run(lambda e: e.tensor_tensor(query[d], q, f[d], ALU.mult), core.q_ok[h])
    for d in range(2):
        ev = pool.run(lambda e: e.tensor_scalar(key_c[d], fc[d], -1.0, 1.0, ALU.mult, ALU.add), core.kc_free)
        for lv in LEVELS:
            ev = decay_step(core, pool, d, lv, fc[d], key_c[d], None, ev)
        ready_c[d] = ev
    for n in range(len(LEVELS) + 1):
        for d in range(2):
            b = 2 * d
            core.claim(b, 2)
            pe.after(ready[d])
            rhs = q if n == 0 else query[d]
            for c in range(NCH):
                at = slice(c * CHUNK, (c + 1) * CHUNK)
                mm = pe.engine.matmul(core.bank(b, T)[:, at], key[d][:, at], rhs[:, at], start=True, stop=True)
            paired = pe.mark(mm)
            m = 0 if n == 0 else n + (len(LEVELS) if d else 0)
            mask = core.masks[:, m * P:(m + 1) * P].rearrange("p (a i) -> p a i", a=1).broadcast_to([P, NCH, P])
            ev = dve.run(lambda e: e.copy_predicated(
                core.score[d].rearrange("p (c i) -> p c i", c=NCH), mask,
                core.bank(b, T).rearrange("p (c i) -> p c i", c=NCH)), paired, core.score_free)
            core.freed(b, 2, ev)
            if n > 0:
                ready[d] = decay_step(core, dve, d, LEVELS[n - 1], f[d], key[d], query[d], paired)
            fill(3)
    core.claim(4, 2)
    order_c = [[0, 1], [1, 0]]
    turned = core.turns([(core.bank(4)[:, (2 * d + c) * P:(2 * d + c + 1) * P], key_c[d][:, c * P:(c + 1) * P])
                         for d in range(2) for c in range(2)], ready_c[1], ready_c[0])
    core.kc_free = turned
    kr_ok = act.run(lambda e: e.activation(core.view(KRT, 4 * P), core.bank(4), ACT.Copy), turned, core.krt_free)
    core.freed(4, 1, kr_ok)
    fill(2)
    pe.after(kr_ok, core.v_ok)
    for d in range(2):
        for c in range(2):
            mm = pe.engine.matmul(core.bank(5)[:, (2 * d + c) * P:(2 * d + c + 1) * P], krt[:, 2 * d + c, :],
                                  core.vctx[:, c, head_cols], start=True, stop=True)
    u_ok = pe.mark(mm)
    for d in range(2):
        a, z = order_c[d]
        part = lambda c: core.bank(5)[:, (2 * d + c) * P:(2 * d + c + 1) * P]
        dve.run(lambda e: e.tensor_copy(s0[d], part(a)), u_ok)
        last = z * P + (P - 1 if d == 0 else 0)
        ev = dve.run(lambda e: e.scalar_tensor_tensor(out=s0[d], in0=s0[d], scalar=fc[d][:, last:last + 1],
                                                      in1=part(z), op0=ALU.mult, op1=ALU.add), ready_c[d])
    core.freed(5, 1, ev)
    fill(2)
    oT = core.view(OT + T * h, T)
    for d in range(2):
        core.claim(4, 2)
        turned = core.turns([(core.bank(4, T)[:, c * P:(c + 1) * P], key[d][:, c * P:(c + 1) * P])
                             for c in range(NCH)], ready[d])
        ev = act.run(lambda e: e.activation(core.view(KRT, T), core.bank(4, T), ACT.Copy), turned, u_ok)
        core.freed(4, 2, ev)
        fill(3)
        core.claim(4, 2)
        pe.after(ev)
        for c in range(NCH):
            mm = pe.engine.matmul(core.bank(4, T)[:, c * P:(c + 1) * P], krt[:, c, :], core.v[:, c, head_cols],
                                  start=True, stop=True)
        u_ok = pe.mark(mm)
        seq = list(range(NCH)) if d == 0 else list(range(NCH))[::-1]
        ev = dve.run(lambda e: e.tensor_copy(states[:, seq[0], :], s0[d]), core.states_free)
        for c, nxt in zip(seq, seq[1:]):
            last = c * P + (P - 1 if d == 0 else 0)
            ev = dve.run(lambda e: e.scalar_tensor_tensor(
                out=states[:, nxt, :], in0=states[:, c, :], scalar=f[d][:, last:last + 1],
                in1=core.bank(4, T)[:, c * P:(c + 1) * P], op0=ALU.mult, op1=ALU.add), u_ok)
        core.freed(4, 2, ev)
        fill(4)
        b = 2 * d
        core.claim(b, 2)
        pe.after(ev)
        for c in range(NCH):
            at = slice(c * CHUNK, (c + 1) * CHUNK)
            pe.engine.matmul(core.bank(b, T)[:, at], core.v[:, c, head_cols], core.score[d][:, at], start=True,
                             stop=False)
            mm = pe.engine.matmul(core.bank(b, T)[:, at], states[:, c, :], query[d][:, at], start=False, stop=True)
        done = pe.mark(mm)
        core.states_free = core.krt_free = done
        core.unit_free[d] = done
        if d == 0:
            ev = act.run(lambda e: e.activation(oT, core.bank(b, T), ACT.Copy), done)
        else:
            ev = dve.run(lambda e: e.tensor_tensor(oT, oT, core.bank(b, T), ALU.add), done, ev0)
        ev0 = ev
        core.freed(b, 2, ev)
    core.score_free = done
    core.raw_free[h % 2] = [done, dve.latest, pool.latest]
    square = query[1]
    sq = act.run(lambda e: e.activation(square, oT, ACT.Square), ev)
    core.claim(4, 2)
    pe.after(sq)
    for c in range(NCH):
        mm = pe.engine.matmul(core.bank(4)[:, c:c + 1], square[:, c * P:(c + 1) * P], core.ones[:, 0:1], start=True,
                              stop=True)
    summed = pe.mark(mm)
    rs = core.small[:, 80:88]
    ev = dve.run(lambda e: e.tensor_copy(rs, core.bank(4, NCH)), summed)
    core.freed(4, 1, ev)
    ev = row_scale(core, rs, P, ev)
    fill(4)
    diag = key[1]
    ev = dve.run(lambda e: e.tensor_tensor(
        diag.rearrange("p (c i) -> p c i", c=NCH),
        core.ident[:, :].rearrange("p (a i) -> p a i", a=1).broadcast_to([P, NCH, P]),
        rs.rearrange("p (c a) -> p c a", a=1).broadcast_to([P, NCH, P]), ALU.mult), ev, core.unit_free[1])
    core.claim(4, 2)
    pe.after(ev)
    for half in range(2):
        mm = pe.engine.matmul(core.bank(4 + half), core.ones[:, :], diag[:, half * BANK:(half + 1) * BANK],
                              start=True, stop=True)
    spread = pe.mark(mm)
    core.unit_free[1] = spread
    ev = dve.run(lambda e: e.tensor_tensor(oT, oT, core.bank(4, T), ALU.mult), spread)
    core.freed(4, 2, ev)


def hgrn(core):
    core.stage("hgrn")
    core.raw_free = [core.everything(), core.everything()]
    core.unit_free = [core.everything(), core.everything()]
    core.q_ok, core.f_ok = {}, {}
    core.kc_free = core.krt_free = core.states_free = core.everything()
    for _ in raw_head(core, 0):
        pass
    for h in range(HEADS):
        other = raw_head(core, h + 1) if h + 1 < HEADS else sgu_gates(core)

        def fill(n):
            for _ in range(n):
                next(other, None)
        head_scan(core, h, fill)
        for _ in other:
            pass


def sgu_gates(core):
    core.uT = core.view(YB, GROUPS * T).rearrange("p (g t) -> p g t", g=GROUPS)
    for g in range(GROUPS):
        slot, landed = core.feat.take()
        yield from feature_halves(core, slot, landed, lambda half, b, ev: core.act.run(
            lambda e: e.activation(core.uT[:, g, half * BANK:(half + 1) * BANK], core.bank(b), ACT.Gelu_apprx_tanh),
            ev))
        core.feat.release(core.pe.latest)



def sgu_values(core):
    nw = lambda g: core.col("sgu_norm", g)
    slot, landed = core.wide.take()
    w = tiled(slot, DT)
    gv, squares = core.view(RAW, WIDTH), core.view(RAW + WIDTH, WIDTH)
    sums = core.small[:, 88:92]
    by_group = lambda ap: ap.rearrange("p (g c) -> p g c", g=GROUPS)
    gv_free = core.raw_free[0]
    for t in range(TT):
        core.claim(6)
        core.pe.after(landed)
        for k in range(DT):
            mm = core.pe.engine.matmul(core.bank(6), core.hT[:, k, t * P:(t + 1) * P], w[:, k, :], start=(k == 0),
                                       stop=(k == DT - 1))
            if k < DT - 1:
                yield
        ev = core.pe.mark(mm)
        if t == TT - 1:
            core.wide.release(ev)
        ev = core.act.run(lambda e: e.activation(gv, core.bank(6), ACT.Gelu_apprx_tanh), ev, gv_free)
        core.freed(6, 1, ev)
        sq = core.act.run(lambda e: e.activation(squares, gv, ACT.Square))
        ev = core.dve.run(lambda e: e.tensor_reduce(sums, by_group(squares), AX.X, ALU.add), sq)
        ev = row_scale(core, sums, P, ev)
        ev = core.dve.run(lambda e: e.tensor_tensor(
            by_group(squares), by_group(gv), sums.rearrange("p (g a) -> p g a", a=1).broadcast_to([P, GROUPS, P]),
            ALU.mult))
        yield
        core.claim(7)
        core.pe.after(ev, core.sgu_ok)
        for g in range(GROUPS):
            mm = core.pe.engine.matmul(core.bank(7)[:, g * P:(g + 1) * P], squares[:, g * P:(g + 1) * P],
                                       core.sgu_wT[:, g, :], start=True, stop=True)
        mixed = core.pe.mark(mm)
        gv_free = [mixed, ev]
        tmp = core.view(RAW + 2 * WIDTH, WIDTH)
        for g in range(GROUPS):
            core.dve.run(lambda e: e.scalar_tensor_tensor(
                out=tmp[:, g * P:(g + 1) * P], in0=core.bank(7)[:, g * P:(g + 1) * P], scalar=nw(g),
                in1=core.sgu_bias[:, g * P:(g + 1) * P], op0=ALU.mult, op1=ALU.add), mixed)
        core.freed(7, 1, core.dve.latest)
        ut = core.uT[:, :, t * P:(t + 1) * P]
        core.sgu_done = core.dve.run(lambda e: e.tensor_tensor(ut, ut, by_group(tmp), ALU.mult), core.u_ok)
        yield


def hgrn_gates(core):
    tmp = core.view(RAW + 3 * WIDTH, BANK)
    for h in range(HEADS):
        slot, landed = core.feat.take()

        def gate(half, b, ev):
            s = core.act.run(lambda e: e.activation(tmp, core.bank(b), ACT.Silu), ev, core.gate_free)
            o = core.view(OT + T * h + half * BANK, BANK)
            core.gate_free = core.dve.run(lambda e: e.scalar_tensor_tensor(
                out=o, in0=o, scalar=core.col("hgrn_norm", h), in1=tmp, op0=ALU.mult, op1=ALU.mult), s)
            return s
        yield from feature_halves(core, slot, landed, gate)
        core.feat.release(core.pe.latest)


def merge(core, ins):
    core.stage("merge")
    oT = core.view(OT, HEADS * T).rearrange("p (k t) -> p k t", k=HEADS)
    core.merged = core.view(MERGED, DT * T).rearrange("p (j t) -> p j t", j=DT)
    tmp_free = [[core.wide.transfers[0].done(), core.everything()]] * 2
    unit_free = core.everything()
    for j in range(DT):
        terms = []
        for n, (src, branch) in enumerate(((oT, "a"), (core.uT, "b"))):
            tmp = core.view(WIDE + 2048 * (j % 2) + 1024 * n, T)
            for what in ("gate", "branch"):
                slot, landed = core.feat.take()
                pair = 4 * (n % 2) + (0 if what == "gate" else 2)
                if what == "gate":
                    run = feature_halves(core, slot, landed, lambda half, b, ev: core.act.run(
                        lambda e: e.activation(tmp[:, half * BANK:(half + 1) * BANK], core.bank(b), ACT.Sigmoid), ev,
                        tmp_free[j % 2]), banks=(pair, pair + 1))
                else:
                    sig = core.act.latest
                    core.pe.after(core.sgu_done, core.gate_free)
                    run = feature_halves(core, slot, landed, lambda half, b, ev: core.dve.run(
                        lambda e: e.tensor_tensor(tmp[:, half * BANK:(half + 1) * BANK],
                                                  tmp[:, half * BANK:(half + 1) * BANK], core.bank(b), ALU.mult),
                        ev, sig), k_of=src, banks=(pair, pair + 1))
                for _ in run:
                    pass
                core.feat.release(core.pe.latest)
            terms.append(tmp)
        core.merged_ok = core.pool.run(lambda e: e.tensor_tensor(core.merged[:, j, :], terms[0], terms[1], ALU.add),
                                       core.dve.latest, unit_free)
        tmp_free = list(tmp_free)
        tmp_free[j % 2] = core.merged_ok


def gain_rows(core, ins):
    nc = core.nc
    scratch = nc.dram_tensor("gain_rows", (2, D), F32, kind="Internal").ap()
    rows = core.view(GM_ROW + 1024, 256)[0:DT, :].rearrange("p (n c) -> p n c", n=2)
    core.claim(0)
    turned = core.turns([(core.bank(0)[0:DT, n * P:(n + 1) * P], core.mod_v[:, at:at + DT, 0])
                         for n, at in enumerate((2 * DT, 5 * DT))], core.mod_ok)
    ev = core.dve.run(lambda e: e.tensor_copy(core.view(GM_ROW + 1024, 256)[0:DT, :], core.bank(0)[0:DT, 0:256]),
                      turned)
    core.freed(0, 1, ev)
    stored = Transfers(nc, "dma_gain_store").start(core.sp, scratch.rearrange("n (j c) -> j n c", c=P), rows, ev)
    core.gm_row, core.gf_row = core.view(GM_ROW, D), core.view(GF_ROW, D)
    back = Transfers(nc, "dma_gain_rows")
    back.start(core.sp, core.gm_row, scratch[0].partition_broadcast(P), stored, core.everything())
    core.gains_ok = back.start(core.sp, core.gf_row, scratch[1].partition_broadcast(P))
    core.ffn_scale = core.small[:, 96:104]
    a = core.dve.run(lambda e: e.tensor_scalar(core.ffn_scale, core.mod_v[:, 4 * DT:5 * DT, 0], 1.0, None, ALU.add))
    core.ffn_ok = core.dve.run(lambda e: e.tensor_tensor(core.ffn_scale, core.ffn_scale, core.col("norm_ffn", 0, 8),
                                                         ALU.mult), a)


def project_out(core, ins, w_out_ok, w_out):
    nc, pe, dve, act, sp = core.nc, core.pe, core.dve, core.act, core.sp
    core.x_dram = nc.dram_tensor("x_after_mixer", (T, D), F32, kind="Internal").ap()
    core.xn_dram = nc.dram_tensor("x_normed", (T, D), F32, kind="Internal").ap()
    x_src = ins["x"].rearrange("a (t p) d -> (a t) p d", p=P)
    core.xn = core.view(HT, TT * D).rearrange("p (t d) -> p t d", t=TT)
    xt = [core.view(XT + 1024 * i, D) for i in range(2)]
    ht_free = core.everything()
    dma_x = [Transfers(nc, f"dma_x_again{i}") for i in range(2)]
    dma_st = [Transfers(nc, f"dma_x_store{i}") for i in range(2)]
    core.xn_stored = Transfers(nc, "dma_xn_store")
    landed = [dma_x[i].start(sp, xt[i], x_src[i], ht_free) for i in range(2)]
    sums = core.small[:, 104:112]
    for t in range(TT):
        xn = core.xn[:, t, :]
        for half in range(2):
            b = (2 * t + half) % 8
            cols = slice(half * BANK, (half + 1) * BANK)
            core.claim(b)
            mm = core.matmuls(core.bank(b), [(core.merged[:, k, t * P:(t + 1) * P], w_out[:, k, cols])
                                             for k in range(DT)], w_out_ok, core.merged_ok)
            ev = dve.run(lambda e: e.tensor_tensor(xn[:, cols], core.bank(b), core.gm_row[:, cols], ALU.mult), mm,
                         core.gains_ok, ht_free)
            core.freed(b, 1, ev)
        x1 = dve.run(lambda e: e.tensor_tensor(xt[t % 2], xt[t % 2], xn, ALU.add), landed[t % 2])
        st = dma_st[t % 2].start(sp, core.x_dram[t * P:(t + 1) * P, :], xt[t % 2], x1)
        sq = act.run(lambda e: e.activation(xn, xt[t % 2], ACT.Square, accum_out=sums[:, t:t + 1]), x1)
        ev = row_scale(core, sums[:, t:t + 1], D, sq)
        core.xn_ok = dve.run(lambda e: e.tensor_scalar(xn, xt[t % 2], sums[:, t:t + 1], None, ALU.mult), ev)
        core.xn_stored.start(sp, core.xn_dram[t * P:(t + 1) * P, :], xn, core.xn_ok)
        if t + 2 < TT:
            landed[t % 2] = dma_x[t % 2].start(sp, xt[t % 2], x_src[t + 2], st, core.xn_ok)
    core.x_stored = [d.done() for d in dma_st]


SLOTS = [8192 + 4096 * i for i in range(9)]
XS, XST, HID, HIDT, YE = 0, 2048, 4096, 6144, 45056
TOPK = 50176


def expert_loads(ins):
    gate, up, down = (ins[f"expert_w_{n}"][0] for n in ("gate", "up", "down"))
    loads = []
    for e in range(NE):
        for c in range(FF // BANK):
            loads += [feature_tile(gate[e], c * BANK, BANK), feature_tile(up[e], c * BANK, BANK)]
        for c in range(4):
            src = down[e].rearrange("(c k p) n -> c p k n", p=P, k=4)[c]
            loads.append(lambda slot, src=src: (tiled(slot, 4), src))
    w_in, w_out = ins["w_in_2"][0], ins["w_out_2"][0]
    loads += [feature_tile(w_in, 0, AW), feature_tile(w_in, AW, 2 * KW), feature_tile(w_in, CC_XR, LW),
              feature_tile(w_in, CC_YR, LW), feature_tile(w_out, 0, BANK), feature_tile(w_out, BANK, BANK)]
    return loads


def route(core, ins, router, router_ok):
    pe, dve, act, pool = core.pe, core.dve, core.act, core.pool
    core.stage("route")
    shift = core.mod_v[:, 3 * DT:4 * DT, 0]
    h2 = [core.view(YE + 1024 * i, T) for i in range(2)]
    h2_free = [core.everything()] * 2
    core.claim(6, 2)
    for j in range(DT):
        ev = turn_and_modulate(core, core.xn, TT, j, 2 * (j % 3), h2[j % 2], core.ffn_scale[:, j:j + 1],
                               shift[:, j:j + 1], core.xn_ok, core.ffn_ok, h2_free[j % 2])
        pe.after(ev, router_ok)
        for half in range(2):
            mm = pe.engine.matmul(core.bank(6 + half)[0:NE, :], router[:, j, :],
                                  h2[j % 2][:, half * BANK:(half + 1) * BANK], start=(j == 0), stop=(j == DT - 1))
        h2_free = list(h2_free)
        h2_free[j % 2] = pe.mark(mm)
    work = core.view(47104, T)[0:NE, :]
    logits = dve.run(lambda e: e.tensor_copy(work, core.bank(6, T)[0:NE, :]), pe.latest)
    core.freed(6, 2, logits)
    core.claim(0)
    turned = core.turns([(core.bank(0)[:, t * NE:(t + 1) * NE], work[:, t * P:(t + 1) * P]) for t in range(TT)],
                        logits)
    aff = core.view(TOPK + 416, TT * NE)
    by_token = lambda ap: ap.rearrange("p (t e) -> p t e", t=TT)
    lo = core.bank(0, TT * NE)
    peak = core.small[:, 112:120]
    wide = lambda ap: ap.rearrange("p (t a) -> p t a", a=1).broadcast_to([P, TT, NE])
    ev = dve.run(lambda e: e.tensor_reduce(peak, by_token(lo), AX.X, ALU.max), turned)
    ev = dve.run(lambda e: e.tensor_tensor(by_token(aff), by_token(lo), wide(peak), ALU.subtract))
    core.freed(0, 1, ev)
    ev = act.run(lambda e: e.activation(aff, aff, ACT.Exp), ev)
    dve.run(lambda e: e.tensor_reduce(peak, by_token(aff), AX.X, ALU.add), ev)
    dve.run(lambda e: e.reciprocal(peak, peak))
    ev = dve.run(lambda e: e.tensor_tensor(by_token(aff), by_token(aff), wide(peak), ALU.mult))
    core.claim(0, 2)
    turned = core.turns([(core.bank(0, T)[0:NE, t * P:(t + 1) * P], by_token(aff)[:, t, :]) for t in range(TT)], ev)
    ev = dve.run(lambda e: e.tensor_copy(work, core.bank(0, T)[0:NE, :]), turned)
    core.freed(0, 2, ev)
    best = core.view(TOPK, CAP)[0:NE, :]
    which = core.arena[:, TOPK + 128:TOPK + 256].bitcast(U32)[0:NE, :]
    as_float = core.view(TOPK + 256, CAP)[0:NE, :]
    for r in range(CAP // 8):
        eight = slice(8 * r, 8 * r + 8)
        dve.run(lambda e: e.max(best[:, eight], work))
        dve.run(lambda e: e.max_index(which[:, eight], best[:, eight], work))
        dve.run(lambda e: e.match_replace(work, best[:, eight], work, NEG))
    ev = dve.run(lambda e: e.tensor_copy(as_float, which))
    core.claim(2)
    turned = core.turns([(core.bank(2)[:, 0:NE], best), (core.bank(2)[:, NE:2 * NE], as_float)], ev)
    core.gate = core.view(TOPK + 384, NE)
    core.index = core.arena[:, TOPK + 400:TOPK + 416].bitcast(U32)
    dve.run(lambda e: e.tensor_copy(core.gate, core.bank(2)[:, 0:NE]), turned)
    core.routed = dve.run(lambda e: e.tensor_copy(core.index, core.bank(2)[:, NE:2 * NE]))
    core.freed(2, 1, core.routed)


def experts(core, ins):
    nc, pe, dve, act, pool = core.nc, core.pe, core.dve, core.act, core.pool
    core.stage("experts")
    shift = core.mod_v[:, 3 * DT:4 * DT, 0]
    area_free = core.everything()
    dma_xs = [Transfers(nc, f"dma_gather{i}") for i in range(2)]
    dma_ye = [Transfers(nc, f"dma_scatter{i}") for i in range(2)]
    xs = [core.view(XS + 1024 * i, D) for i in range(2)]
    xsT = [core.view(XST + 1024 * i, D).rearrange("p (k c) -> p k c", k=DT) for i in range(2)]
    hid = core.view(HID, FF)
    hidT = core.view(HIDT, FF).rearrange("p (k c) -> p k c", k=FF // P)
    ye = [core.view(YE + 1024 * i, D) for i in range(2)]
    xs_free, xsT_free, ye_free = [area_free] * 2, [area_free] * 2, [area_free] * 2
    xsT_ok, gathered = [None] * 2, [None] * 2
    hid_free, hidT_free = area_free, area_free
    scattered = core.x_stored

    def gather(x):
        i = x % 2
        pool.after(core.routed, core.xn_stored.done(), xs_free[i])
        nc.gpsimd.indirect_dma_start(xs[i], None, core.xn_dram,
                                     bass.IndirectOffsetOnAxis(ap=core.index[:, x:x + 1], axis=0)
                                     ).then_inc(dma_xs[i].sem, 16)
        dma_xs[i].count += 16
        gathered[i] = dma_xs[i].done()

    def turn_inputs(x):
        i = x % 2
        core.claim(4, 2)
        turned = core.turns([(core.bank(4, D)[:, j * P:(j + 1) * P], xs[i][:, j * P:(j + 1) * P])
                             for j in range(DT)], gathered[i])
        xs_free[i] = turned
        for j in range(DT):
            part = core.bank(4, D)[:, j * P:(j + 1) * P]
            if j >= DT // 2:
                ev = dve.run(lambda e: e.tensor_scalar(xsT[i][:, j, :], part, core.ffn_scale[:, j:j + 1],
                                                       shift[:, j:j + 1], ALU.mult, ALU.add), turned, xsT_free[i])
            else:
                ev = act.run(lambda e: e.activation(xsT[i][:, j, :], part, ACT.Identity, bias=shift[:, j:j + 1],
                                                    scale=core.ffn_scale[:, j:j + 1]), turned, xsT_free[i])
        core.freed(4, 2, [dve.latest, act.latest])
        xsT_ok[i] = [dve.latest, act.latest]

    def turn_hidden(c, ready):
        nonlocal hidT_free
        b = 4 + c % 2
        core.claim(b)
        turned = core.turns([(core.bank(b)[:, k * P:(k + 1) * P], hid[:, (4 * c + k) * P:(4 * c + k + 1) * P])
                             for k in range(4)], ready)
        out = core.view(HIDT + 4 * P * c, 4 * P)
        if c % 2:
            ev = dve.run(lambda e: e.tensor_copy(out, core.bank(b)), turned, hidT_free)
        else:
            ev = act.run(lambda e: e.activation(out, core.bank(b), ACT.Copy), turned, hidT_free)
        core.freed(b, 1, ev)
        return ev

    gather(0)
    gather(1)
    turn_inputs(0)
    for x in range(NE):
        i = x % 2
        hid_ok, hidT_ok = [None] * 4, [None] * 4
        for c in range(FF // BANK):
            cols = slice(c * BANK, (c + 1) * BANK)
            made = []
            for n in range(2):
                slot, landed = core.expert.take()
                w = tiled(slot, DT)
                b = 2 * (c % 2) + n
                core.claim(b)
                mm = core.matmuls(core.bank(b), [(xsT[i][:, k, :], w[:, k, :]) for k in range(DT)], landed, xsT_ok[i])
                core.expert.release(mm)
                made.append(mm)
            s = act.run(lambda e: e.activation(hid[:, cols], core.bank(2 * (c % 2)), ACT.Silu), made[0], hid_free)
            core.freed(2 * (c % 2), 1, s)
            hid_ok[c] = dve.run(lambda e: e.tensor_tensor(hid[:, cols], hid[:, cols], core.bank(2 * (c % 2) + 1),
                                                          ALU.mult), s, made[1])
            core.freed(2 * (c % 2) + 1, 1, hid_ok[c])
            if c:
                hidT_ok[c - 1] = turn_hidden(c - 1, hid_ok[c - 1])
        xsT_free[i] = mm
        if x + 1 < NE:
            turn_inputs(x + 1)
        if x + 2 < NE:
            gather(x + 2)
        core.claim(6, 2)
        for c in range(4):
            if c == 3:
                hidT_ok[3] = turn_hidden(3, hid_ok[3])
                hid_free = [pe.latest]
            slot, landed = core.expert.take()
            w = tiled(slot, 4)
            pe.after(landed, hidT_ok[c])
            for k in range(4):
                for half in range(2):
                    mm = pe.engine.matmul(core.bank(6 + half), hidT[:, 4 * c + k, :],
                                          w[:, k, half * BANK:(half + 1) * BANK], start=(c == 0 and k == 0),
                                          stop=(c == 3 and k == 3))
            ev = pe.mark(mm)
            core.expert.release(ev)
        hidT_free = ev
        for half in range(2):
            cols = slice(half * BANK, (half + 1) * BANK)
            out = dve.run(lambda e: e.scalar_tensor_tensor(
                out=ye[i][:, cols], in0=core.bank(6 + half), scalar=core.gate[:, x:x + 1], in1=core.gf_row[:, cols],
                op0=ALU.mult, op1=ALU.mult), ev, ye_free[i], core.gains_ok)
        core.freed(6, 2, out)
        pool.after(out, scattered)
        nc.gpsimd.indirect_dma_start(core.x_dram, bass.IndirectOffsetOnAxis(ap=core.index[:, x:x + 1], axis=0),
                                     ye[i], None, compute_op=ALU.add).then_inc(dma_ye[i].sem, 16)
        dma_ye[i].count += 16
        scattered = ye_free[i] = dma_ye[i].done()
    core.scattered = scattered



H1, X2, QKT, VB, LRUT, JUNK = 0, 8192, 8192, 13312, 14336, 16384
BLOCKS, LRU_TMP = 18432, 20480
PROB, PROBT, OATT = 18432, 20480, 22528
XN3, X3T = 18432, 26624
QK, SQ, ROPED, R1, R2 = 45056, 45696, 46336, 46976, 47296
FINAL_ROW, GAIN, ROPE = 47616, 48640, 49280
ACTT, UP_RING, CONV, G_ROW = 8192, 32768, 40960, 49152


def second_start(core, ins):
    nc, pe, dve, act, sp = core.nc, core.pe, core.dve, core.act, core.sp
    core.stage("second")
    gone = core.everything()
    x2 = core.view(X2, TT * D).rearrange("p (t d) -> p t d", t=TT)
    core.xb_dram = nc.dram_tensor("x_second", (T, D), F32, kind="Internal").ap()
    final_row = core.view(FINAL_ROW, D)
    rows = Transfers(nc, "dma_second_rows")
    rows.start(sp, final_row, ins["final_norm_w"].partition_broadcast(P), gone)
    core.gain_row = core.view(GAIN, (QH + KVH) * HD)
    gains = core.gain_row.rearrange("p (h c) -> p h c", c=HD)
    for h in range(QH + KVH):
        rows.start(sp, gains[:, h, :], ins["q_norm_g_2" if h < QH else "k_norm_g_2"][0].partition_broadcast(P))
    core.rope = core.view(ROPE, TT * HD)
    core.rows_in = rows.start(sp, core.rope, ins["rope_table"])
    core.blocks = core.view(BLOCKS, 16 * P).rearrange("p (w m j) -> p w m j", w=4, m=LT)
    cleared = dve.run(lambda e: e.memset(core.view(BLOCKS, 16 * P), 0.0), gone)
    blocks = Transfers(nc, "dma_blocks")
    for n, name in enumerate(("wa_f_2", "wx_f_2", "wa_b_2", "wx_b_2")):
        src = ins[name][0].rearrange("(m s) i j -> s i m j", s=2)
        for s in range(2):
            core.blocks_in = blocks.start(sp, core.blocks[s * 64:(s + 1) * 64, n, :, s * 64:(s + 1) * 64], src[s],
                                          cleared)
    dma_x2 = [Transfers(nc, f"dma_x2_{i}") for i in range(2)]
    x2_src = core.x_dram.rearrange("(t p) d -> p t d", p=P)
    x2_in = [dma_x2[i].start(sp, x2[:, 4 * i:4 * i + 4, :], x2_src[:, 4 * i:4 * i + 4, :], core.scattered, gone)
             for i in range(2)]
    sums = core.small[:, 120:128]
    sums2 = core.small[:, 128:136]
    junk = core.view(JUNK, D)
    core.xb_stored = Transfers(nc, "dma_xb_store")
    for i in range(2):
        tiles = range(4 * i, 4 * i + 4)
        part, part2 = sums[:, 4 * i:4 * i + 4], sums2[:, 4 * i:4 * i + 4]
        for t in tiles:
            ev = act.run(lambda e: e.activation(junk, x2[:, t, :], ACT.Square, accum_out=sums[:, t:t + 1]), x2_in[i],
                         gone)
        row_scale(core, part, D, ev)
        for t in tiles:
            ev = dve.run(lambda e: e.scalar_tensor_tensor(out=x2[:, t, :], in0=x2[:, t, :], scalar=sums[:, t:t + 1],
                                                          in1=final_row, op0=ALU.mult, op1=ALU.mult), core.rows_in)
            core.xb_stored.start(sp, core.xb_dram[t * P:(t + 1) * P, :], x2[:, t, :], ev)
            ev = act.run(lambda e: e.activation(junk, x2[:, t, :], ACT.Square, accum_out=sums2[:, t:t + 1]), ev)
        row_scale(core, part2, D, ev)
        for t in tiles:
            ready = dve.run(lambda e: e.tensor_scalar(x2[:, t, :], x2[:, t, :], sums2[:, t:t + 1], None, ALU.mult),
                            core.xb_stored.done())
    core.h1T = core.view(H1, DT * T).rearrange("p (j t) -> p j t", j=DT)
    for j in range(DT):
        core.h1_ok = turn_and_modulate(core, x2, TT, j, 2 * (j % 4), core.h1T[:, j, :], core.col("norm1", j), 0.0,
                                       ready, gone)


def second_heads(core, ins):
    nc, pe, dve, act = core.nc, core.pe, core.dve, core.act
    n_heads = QH + KVH
    (wq, q_in), (wkv, kv_in) = core.expert.take(), core.expert.take()
    wq, wkv = tiled(wq, DT), tiled(wkv[:, 0:DT * 2 * KW], DT)
    core.qkT = core.view(QKT, 5 * T).rearrange("p (i t) -> p i t", i=5)
    core.vb = core.view(VB, TT * KW).rearrange("p (t n) -> p t n", t=TT)
    qk, sq, roped = core.view(QK, 640), core.view(SQ, 640), core.view(ROPED, 640)
    r1, r2 = core.view(R1, 320), core.view(R2, 320)
    sums = core.small[:, 136:146]
    ev_gain = dve.run(lambda e: e.tensor_scalar(core.gain_row[:, 0:AW], core.gain_row[:, 0:AW], HD ** -0.5, None,
                                                ALU.mult), core.rows_in)
    by_head = lambda ap: ap.rearrange("p (h c) -> p h c", c=HD)
    parts = lambda ap: ap.rearrange("p (h a s c) -> p h a s c", a=2, s=2, c=HD // 4)
    flat = lambda ap: ap.rearrange("p (h a c) -> p h a c", a=2, c=HD // 4)
    roped_free = None
    turns_free = [core.h1_ok]
    for t in range(TT):
        tok = slice(t * P, (t + 1) * P)
        b = 2 * (t % 2)
        core.claim(b, 2)
        core.matmuls(core.bank(b), [(core.h1T[:, k, tok], wq[:, k, :]) for k in range(DT)], q_in, core.h1_ok)
        mm = core.matmuls(core.bank(b + 1, 2 * KW), [(core.h1T[:, k, tok], wkv[:, k, :]) for k in range(DT)], kv_in)
        both = core.bank(b, n_heads * HD)
        ev = act.run(lambda e: e.activation(sq, both, ACT.Square), mm)
        act.run(lambda e: e.activation(core.vb[:, t, :], core.bank(b + 1)[:, KW:2 * KW], ACT.Copy), turns_free)
        ev = dve.run(lambda e: e.tensor_reduce(sums, by_head(sq), AX.X, ALU.add), ev)
        ev = row_scale(core, sums, HD, ev)
        dve.run(lambda e: e.tensor_tensor(
            by_head(qk), by_head(both), sums.rearrange("p (h a) -> p h a", a=1).broadcast_to([P, n_heads, HD]),
            ALU.mult), ev)
        core.freed(b, 2, [dve.latest, act.latest])
        ev = dve.run(lambda e: e.tensor_tensor(qk, qk, core.gain_row, ALU.mult), ev_gain)
        table = core.rope[:, t * HD:(t + 1) * HD].rearrange("p (f a c) -> p f a c", f=2, a=2)
        paired = roped[:, 0:AW].rearrange("p (i s a z c) -> p s i a z c", s=2, a=2, z=2, c=HD // 4)
        keys = roped[:, AW:AW + KW].rearrange("p (s a z c) -> p s a z c", a=2, z=2, c=HD // 4)
        for a in range(2):
            angle = lambda f: table[:, f, a, :].rearrange("p (o c) -> p o c", o=1).broadcast_to(
                [P, n_heads, HD // 4])
            lo, hi = parts(qk)[:, :, a, 0, :], parts(qk)[:, :, a, 1, :]
            t1, t2 = flat(r1)[:, :, a, :], flat(r2)[:, :, a, :]
            queries = lambda ap: ap[:, 0:QH, :].rearrange("p (s i) c -> p s i c", s=2)
            for z, first, second, op in ((0, lo, hi, ALU.subtract), (1, hi, lo, ALU.add)):
                dve.run(lambda e: e.tensor_tensor(t1, first, angle(0), ALU.mult))
                dve.run(lambda e: e.tensor_tensor(t2, second, angle(1), ALU.mult))
                dve.run(lambda e: e.tensor_tensor(paired[:, :, :, a, z, :], queries(t1), queries(t2), op), roped_free)
                ready = dve.run(lambda e: e.tensor_tensor(keys[:, :, a, z, :], t1[:, QH:, :], t2[:, QH:, :], op))
        core.claim(4, 2)
        turned = core.turns([(core.bank(4, T)[:, i * P:(i + 1) * P], roped[:, i * P:(i + 1) * P]) for i in range(5)],
                            ready)
        roped_free = turned
        core.qk_ok = act.run(lambda e: e.activation(core.qkT[:, :, tok], core.bank(4, 5 * P).rearrange(
            "p (i t) -> p i t", i=5), ACT.Copy), turned)
        core.freed(4, 2, core.qk_ok)


def lru_rates(core):
    dve, act = core.dve, core.act
    lam = core.small[:, 0:8]
    rate, minus, z, s, s2 = (core.small[:, 8 * n:8 * n + 8] for n in (1, 2, 3, 4, 5))
    for d, name in enumerate(("lam_f", "lam_b")):
        dve.run(lambda e: e.tensor_copy(lam[:, 4 * d:4 * d + 4], core.col(name, 0, 4)))
    ev = dve.run(lambda e: e.tensor_scalar(z, lam, -1.0, None, ALU.mult))
    ev = dve.run(lambda e: e.tensor_tensor(z, z, lam, ALU.max))
    ev = act.run(lambda e: e.activation(z, z, ACT.Exp, scale=-1.0), ev)
    dve.run(lambda e: e.tensor_scalar(s, z, 2.0, None, ALU.add), ev)
    dve.run(lambda e: e.reciprocal(s, s))
    dve.run(lambda e: e.tensor_tensor(s, s, z, ALU.mult))
    dve.run(lambda e: e.tensor_tensor(s2, s, s, ALU.mult))
    dve.run(lambda e: e.memset(z, 1.0 / 19))
    for n in range(17, 0, -2):
        dve.run(lambda e: e.tensor_tensor(z, z, s2, ALU.mult))
        dve.run(lambda e: e.tensor_scalar(z, z, 1.0 / n, None, ALU.add))
    dve.run(lambda e: e.tensor_tensor(z, z, s, ALU.mult))
    dve.run(lambda e: e.tensor_scalar(z, z, 2.0, None, ALU.mult))
    dve.run(lambda e: e.tensor_scalar(rate, lam, 0.0, None, ALU.min))
    dve.run(lambda e: e.tensor_tensor(rate, rate, z, ALU.subtract))
    dve.run(lambda e: e.tensor_scalar(rate, rate, LRU_C, None, ALU.mult))
    core.rates_ok = dve.run(lambda e: e.tensor_scalar(minus, rate, -1.0, None, ALU.mult))
    core.rate, core.minus_rate = rate, minus


def lru(core):
    pe, dve, act, pool = core.pe, core.dve, core.act, core.pool
    core.stage("lru")
    gone = core.everything()
    (wx, wx_in), (wy, wy_in) = core.expert.take(), core.expert.take()
    wx, wy = tiled(wx, DT), tiled(wy, DT)
    tile = lambda n: core.view(LRU_TMP + T * n, T)
    xc_of, yr_of = [tile(0), tile(1)], [tile(2), tile(3)]
    a, tanh, b, h = (tile(n) for n in (4, 5, 6, 7))
    core.lruT = core.view(LRUT, LT * T).rearrange("p (c t) -> p c t", c=LT)
    xc_free, yr_free, xc_ok, yr_ok = [gone] * 2, [gone] * 2, [None] * 2, [None] * 2

    def project(c):
        i = c % 2
        cols = slice(c * P, (c + 1) * P)
        for w, landed, pair in ((wx, wx_in, 0), (wy, wy_in, 2)):
            core.claim(pair, 2)
            for half in range(2):
                mm = core.matmuls(core.bank(pair + half), [(w[:, k, cols], core.h1T[:, k, half * BANK:(half + 1) * BANK])
                                                           for k in range(DT)], landed, core.h1_ok)
            if pair == 0:
                xc, x = xc_of[i], core.bank(0, T)
                tap = lambda n: core.col("lru_conv_w", 4 * n + c)
                ev = act.run(lambda e: e.activation(xc, x, ACT.Identity, bias=core.col("lru_conv_b", c), scale=tap(2)),
                             mm, xc_free[i])
                for n, shift in ((0, 2), (1, 1)):
                    dve.run(lambda e: e.scalar_tensor_tensor(out=xc[:, shift:T], in0=x[:, 0:T - shift], scalar=tap(n),
                                                             in1=xc[:, shift:T], op0=ALU.mult, op1=ALU.add), ev)
                xc_ok[i] = dve.run(lambda e: e.scalar_tensor_tensor(
                    out=xc[:, 0:T - 1], in0=x[:, 1:T], scalar=tap(3), in1=xc[:, 0:T - 1], op0=ALU.mult, op1=ALU.add))
                core.freed(0, 2, xc_ok[i])
            else:
                yr_ok[i] = act.run(lambda e: e.activation(yr_of[i], core.bank(2, T), ACT.Gelu_apprx_tanh), mm,
                                   yr_free[i])
                core.freed(2, 2, yr_ok[i])

    def recur(c):
        i = c % 2
        xc, out = xc_of[i], core.lruT[:, c, :]
        for d in range(2):
            for n, pair in ((0, 4), (1, 6)):
                core.claim(pair, 2)
                pe.after(xc_ok[i], core.blocks_in)
                for half in range(2):
                    mm = pe.engine.matmul(core.bank(pair + half), core.blocks[:, 2 * d + n, c, :],
                                          xc[:, half * BANK:(half + 1) * BANK], start=True, stop=True)
                gate = pe.mark(mm)
                bias = core.col(("ba_", "bx_")[n] + "fb"[d], c)
                ev = act.run(lambda e: e.activation((tanh, b)[n], core.bank(pair, T), ACT.Sigmoid, bias=bias), gate,
                             dve.latest)
                core.freed(pair, 2, ev)
            at = 4 * d + c
            act.run(lambda e: e.activation(a, tanh, ACT.Exp, scale=core.rate[:, at:at + 1]), core.rates_ok)
            ev = act.run(lambda e: e.activation(tanh, tanh, ACT.Tanh, scale=core.minus_rate[:, at:at + 1]))
            dve.run(lambda e: e.tensor_tensor(b, b, xc, ALU.mult), ev)
            dve.run(lambda e: e.tensor_tensor(h, a, a, ALU.mult))
            ev = dve.run(lambda e: e.scalar_tensor_tensor(out=tanh, in0=h, scalar=1.0, in1=tanh, op0=ALU.add,
                                                          op1=ALU.mult))
            act.run(lambda e: e.activation(tanh, tanh, ACT.Sqrt), ev)
            first = 0 if d == 0 else T - 1
            dve.run(lambda e: e.memset(tanh[:, first:first + 1], 1.0), act.latest)
            dve.run(lambda e: e.tensor_tensor(b, b, tanh, ALU.mult))
            if d == 0:
                dve.run(lambda e: e.tensor_tensor_scan(out, a, b, 0.0, ALU.mult, ALU.add), gone)
            else:
                dve.run(lambda e: e.tensor_tensor_scan(h[:, ::-1], a[:, ::-1], b[:, ::-1], 0.0, ALU.mult, ALU.add))
        dve.run(lambda e: e.tensor_tensor(out, out, h, ALU.add))
        core.lru_ok = yr_free[i] = dve.run(lambda e: e.tensor_tensor(out, out, yr_of[i], ALU.mult), yr_ok[i])
        xc_free[i] = [core.lru_ok, pe.latest]

    lru_rates(core)
    project(0)
    for c in range(LT):
        if c + 1 < LT:
            project(c + 1)
        recur(c)


def attention(core):
    pe, dve, act = core.pe, core.dve, core.act
    core.stage("attention")
    gone = core.everything()
    prob = [core.view(PROB + T * i, T) for i in range(2)]
    probT = [core.view(PROBT + T * i, T).rearrange("p (k q) -> p k q", k=TT) for i in range(2)]
    o = core.view(OATT, TT * AW).rearrange("p (t n) -> p t n", t=TT)
    units = [(t, h) for t in range(TT) for h in range(QH)]
    peak = [core.small[:, 48 + i:49 + i] for i in range(2)]
    total = [core.small[:, 50 + i:51 + i] for i in range(4)]
    prob_free, probT_free, exp_ok, probT_ok = [gone] * 2, [gone] * 2, [None] * 2, [None] * 2

    def scores(n):
        t, h = units[n]
        i, lo = n % 2, HD * (h // 4)
        tile = h % 4
        core.claim(2 * i, 2)
        pe.after(core.qk_ok)
        for half in range(2):
            mm = pe.engine.matmul(core.bank(2 * i + half), core.qkT[lo:lo + HD, tile, t * P:(t + 1) * P],
                                  core.qkT[lo:lo + HD, 4, half * BANK:(half + 1) * BANK], start=True, stop=True)
        ev = pe.mark(mm)
        dve.run(lambda e: e.tensor_reduce(peak[i], core.bank(2 * i, T), AX.X, ALU.max), ev, exp_ok[i])
        ev = dve.run(lambda e: e.tensor_scalar(peak[i], peak[i], -1.0, None, ALU.mult))
        exp_ok[i] = act.run(lambda e: e.activation(prob[i], core.bank(2 * i, T), ACT.Exp, bias=peak[i],
                                                   accum_out=total[n % 4]), ev, prob_free[i])
        core.freed(2 * i, 2, exp_ok[i])

    def turn(n):
        i = n % 2
        core.claim(4, 2)
        turned = core.turns([(core.bank(4, T)[:, k * P:(k + 1) * P], prob[i][:, k * P:(k + 1) * P])
                             for k in range(TT)], exp_ok[i])
        prob_free[i] = turned
        half = lambda k: core.view(PROBT + T * i + BANK * k, BANK)
        a = act.run(lambda e: e.activation(half(0), core.bank(4), ACT.Copy), turned, probT_free[i])
        b = dve.run(lambda e: e.tensor_copy(half(1), core.bank(5)), turned, probT_free[i])
        core.freed(4, 1, a)
        core.freed(5, 1, b)
        probT_ok[i] = [a, b]

    def mix(n):
        t, h = units[n]
        i, g = n % 2, h // 4
        b = 6 + i
        core.claim(b)
        pe.after(probT_ok[i])
        for k in range(TT):
            mm = pe.engine.matmul(core.bank(b, HD), probT[i][:, k, :], core.vb[:, k, g * HD:(g + 1) * HD],
                                  start=(k == 0), stop=(k == TT - 1))
        ev = probT_free[i] = pe.mark(mm)
        dve.run(lambda e: e.reciprocal(total[n % 4], total[n % 4]), exp_ok[i])
        core.o_ok = dve.run(lambda e: e.tensor_scalar(o[:, t, h * HD:(h + 1) * HD], core.bank(b, HD), total[n % 4],
                                                      None, ALU.mult), ev)
        core.freed(b, 1, core.o_ok)

    scores(0)
    for n in range(len(units)):
        if n + 1 < len(units):
            scores(n + 1)
        if n:
            mix(n - 1)
        turn(n)
    mix(len(units) - 1)
    core.attT = core.view(H1, 4 * T).rearrange("p (j t) -> p j t", j=4)
    for j in range(4):
        b = 2 * (j % 2)
        core.claim(b, 2)
        turned = core.turns([(core.bank(b, T)[:, t * P:(t + 1) * P], o[:, t, j * P:(j + 1) * P]) for t in range(TT)],
                            core.o_ok)
        core.att_ok = act.run(lambda e: e.activation(core.attT[:, j, :], core.bank(b, T), ACT.Copy), turned)
        core.freed(b, 2, core.att_ok)


def second_out(core):
    nc, pe, dve, act, sp = core.nc, core.pe, core.dve, core.act, core.sp
    core.stage("second_out")
    gone = core.everything()
    halves_w = [core.expert.take() for _ in range(2)]
    core.x3_dram = nc.dram_tensor("x_third", (T, D), F32, kind="Internal").ap()
    xn3 = core.view(XN3, TT * D).rearrange("p (t d) -> p t d", t=TT)
    xt = [core.view(X3T + 1024 * i, D) for i in range(2)]
    dma_x = [Transfers(nc, f"dma_xb{i}") for i in range(2)]
    dma_st = [Transfers(nc, f"dma_x3_store{i}") for i in range(2)]
    sums = core.small[:, 56:64]
    landed = [dma_x[i].start(sp, xt[i], core.xb_dram[i * P:(i + 1) * P, :], gone, core.xb_stored.done())
              for i in range(2)]
    for t in range(TT):
        tok = slice(t * P, (t + 1) * P)
        for half, (w, w_in) in enumerate(halves_w):
            w = tiled(w, DT)
            b = (2 * t + half) % 8
            cols = slice(half * BANK, (half + 1) * BANK)
            src = lambda k: core.attT[:, k, tok] if k < 4 else core.lruT[:, k - 4, tok]
            core.claim(b)
            mm = core.matmuls(core.bank(b), [(src(k), w[:, k, :]) for k in range(DT)], w_in, core.att_ok, core.lru_ok)
            ev = dve.run(lambda e: e.tensor_tensor(xt[t % 2][:, cols], xt[t % 2][:, cols], core.bank(b), ALU.add), mm,
                         landed[t % 2])
            core.freed(b, 1, ev)
        st = dma_st[t % 2].start(sp, core.x3_dram[tok, :], xt[t % 2], ev)
        xn = xn3[:, t, :]
        sq = act.run(lambda e: e.activation(xn, xt[t % 2], ACT.Square, accum_out=sums[:, t:t + 1]), ev, gone)
        ev = row_scale(core, sums[:, t:t + 1], D, sq)
        ready = dve.run(lambda e: e.tensor_scalar(xn, xt[t % 2], sums[:, t:t + 1], None, ALU.mult), ev)
        if t + 2 < TT:
            landed[t % 2] = dma_x[t % 2].start(sp, xt[t % 2], core.xb_dram[(t + 2) * P:(t + 3) * P, :], st, ready)
    core.x3_stored = [d.done() for d in dma_st]
    core.h3T = core.view(H1, DT * T).rearrange("p (j t) -> p j t", j=DT)
    mixed = pe.latest
    for j in range(DT):
        core.h3_ok = turn_and_modulate(core, xn3, TT, j, 2 * (j % 4), core.h3T[:, j, :], core.col("norm2", j), 0.0,
                                       ready, mixed)
    core.h3_mixed = mixed


def ffn_loads(ins):
    up, down = ins["w_up_2"][0], ins["w_down_2"][0]
    loads = []
    for f in range(FT):
        loads += [feature_tile(up, f * P), feature_tile(up, DFF + f * P)]
    for half in range(2):
        for k in range(0, FT, 2):
            src = down[k * P:(k + 2) * P, half * BANK:(half + 1) * BANK].rearrange("(k p) n -> p k n", p=P)
            loads.append(lambda slot, src=src: (tiled(slot, 2), src))
    return loads


def ffn(core, ins, out):
    nc, pe, dve, act, pool, sp = core.nc, core.pe, core.dve, core.act, core.pool, core.sp
    core.stage("ffn")
    gone = core.everything()
    core.actT = core.view(ACTT, FT * T).rearrange("p (f t) -> p f t", f=FT)
    conv = [core.view(CONV + T * i, T) for i in range(4)]
    conv_free = [gone] * 4
    rows = Transfers(nc, "dma_final_row")
    g_row = core.view(G_ROW, D)
    rows_in = rows.start(sp, g_row, ins["final_g_2"].partition_broadcast(P), gone)
    for f in range(FT):
        made = []
        for n in range(2):
            i, pair = 2 * (f % 2) + n, 4 * (f % 2) + 2 * n
            slot, landed = core.ffn.take()
            w = tiled(slot, DT)
            core.claim(pair, 2)
            for half in range(2):
                mm = core.matmuls(core.bank(pair + half), [(w[:, k, :], core.h3T[:, k, half * BANK:(half + 1) * BANK])
                                                           for k in range(DT)], landed, core.h3_ok)
            core.ffn.release(mm)
            u, c, at = core.bank(pair, T), conv[i], n * FT + f
            ev = act.run(lambda e: e.activation(c, u, ACT.Identity, bias=core.col("up_conv_b", at),
                                                scale=core.col("up_conv_w01", 2 * FT + at)), mm, conv_free[i])
            dve.run(lambda e: e.scalar_tensor_tensor(out=c[:, 1:T], in0=u[:, 0:T - 1],
                                                     scalar=core.col("up_conv_w01", at), in1=c[:, 1:T], op0=ALU.mult,
                                                     op1=ALU.add), ev)
            ev = dve.run(lambda e: e.scalar_tensor_tensor(out=c[:, 0:T - 1], in0=u[:, 1:T],
                                                          scalar=core.col("up_conv_w2", at), in1=c[:, 0:T - 1],
                                                          op0=ALU.mult, op1=ALU.add))
            core.freed(pair, 2, ev)
            if n == 0:
                ev = act.run(lambda e: e.activation(c, c, ACT.Gelu_apprx_tanh), ev)
            made.append((ev, c))
        ev = pool.run(lambda e: e.tensor_tensor(core.actT[:, f, :], made[0][1], made[1][1], ALU.mult), made[0][0],
                      made[1][0])
        conv_free[2 * (f % 2)] = conv_free[2 * (f % 2) + 1] = ev
    act_ok = ev
    core.stage("down")
    x3 = core.view(H1, TT * D).rearrange("p (t d) -> p t d", t=TT)
    x3_in = Transfers(nc, "dma_x3").start(sp, x3, core.x3_dram.rearrange("(t p) d -> p t d", p=P), core.x3_stored,
                                          mm)
    sums = core.small[:, 64:72]
    y = [core.view(CONV + T * i, D) for i in range(2)]
    dma_out = [Transfers(nc, f"dma_out{i}") for i in range(2)]
    y_free = [act_ok] * 2
    for half in range(2):
        cols = slice(half * BANK, (half + 1) * BANK)
        ends = [None] * TT
        for kk in range(FT // 2):
            slot, landed = core.ffn.take()
            w = tiled(slot, 2)
            pe.after(landed, act_ok)
            last = kk == FT // 2 - 1
            steps = [(k, t) for t in range(TT) for k in range(2)] if last else [(k, t) for k in range(2)
                                                                                  for t in range(TT)]
            for k, t in steps:
                if kk == 0 and k == 0:
                    core.claim(t)
                mm = pe.engine.matmul(core.bank(t), core.actT[:, 2 * kk + k, t * P:(t + 1) * P], w[:, k, :],
                                      start=(kk == 0 and k == 0), stop=(last and k == 1))
                if last and k == 1:
                    ends[t] = pe.mark(mm)
            if not last:
                ends[0] = pe.mark(mm)
            core.ffn.release(pe.latest)
        for t in range(TT):
            ev = dve.run(lambda e: e.tensor_tensor(x3[:, t, cols], x3[:, t, cols], core.bank(t), ALU.add), ends[t],
                         x3_in)
            core.freed(t, 1, ev)
            if half:
                yt = y[t % 2]
                sq = act.run(lambda e: e.activation(yt, x3[:, t, :], ACT.Square, accum_out=sums[:, t:t + 1]), ev,
                             y_free[t % 2])
                ev = row_scale(core, sums[:, t:t + 1], D, sq)
                ev = dve.run(lambda e: e.scalar_tensor_tensor(out=yt, in0=x3[:, t, :], scalar=sums[:, t:t + 1],
                                                              in1=g_row, op0=ALU.mult, op1=ALU.mult), rows_in)
                y_free[t % 2] = dma_out[t % 2].start(sp, out[0, t * P:(t + 1) * P, :], yt, ev)
    sp.after(y_free)


def build_block_pair(nc, ins, out, upto=99):
    core = Core(nc)
    core.gate_free = None
    start(core, ins)
    if upto <= 1:
        return core
    core.stage("values")
    values(core)
    hgrn(core)
    if upto <= 2:
        return core
    core.u_ok = core.act.latest
    core.gate_free = core.raw_free[0]
    core.stage("sgu")
    for part in [sgu_values(core)] + [ada_chunk(core, core.wide, c, 4 + c % 2) for c in range(4, 12)] + [
            hgrn_gates(core)]:
        for _ in part:
            pass
    merge(core, ins)
    core.stage("out")
    w_out = core.view(WOUT, DT * D).rearrange("p (k n) -> p k n", k=DT)
    w_out_ok = Transfers(nc, "dma_w_out").start(core.sp, w_out, ins["w_out"][0].rearrange("(k p) n -> p k n", p=P),
                                                core.everything())
    gain_rows(core, ins)
    core.expert = Ring(nc, core.sp, "dma_expert", [core.view(at, 4096) for at in SLOTS], expert_loads(ins),
                       [core.everything()] * 4)
    router = core.view(TOPK + 544, DT * NE).rearrange("p (k e) -> p k e", k=DT)
    router_ok = Transfers(nc, "dma_router").start(core.sp, router,
                                                  ins["router_w"][0].rearrange("(k p) e -> p k e", p=P))
    project_out(core, ins, w_out_ok, w_out)
    if upto <= 3:
        core.sp.after(core.x_stored, core.xn_stored.done())
        return core
    area_free = [core.everything(), core.x_stored]
    for _ in range(5):
        core.expert.load(area_free)
    route(core, ins, router, router_ok)
    if upto <= 4:
        return core
    experts(core, ins)
    if upto <= 5:
        core.sp.after(core.scattered)
        return core
    second_start(core, ins)
    second_heads(core, ins)
    if upto <= 6:
        return core
    lru(core)
    if upto <= 7:
        return core
    attention(core)
    gone = core.everything()
    if upto <= 8:
        return core
    second_out(core)
    core.ffn = Ring(nc, core.sp, "dma_ffn", [core.view(UP_RING + 1024 * i, 1024) for i in range(8)], ffn_loads(ins),
                    [[gone, core.pe.latest]] * 8)
    if upto <= 9:
        return core
    ffn(core, ins, out)
    return core


def kernel(**inputs):
    import concourse.bacc as bacc
    from concourse.bass_utils import run_bass_kernel_spmd

    nc = bacc.Bacc("TRN2", target_bir_lowering=False, num_devices=1)
    arrays, ins = {}, {}
    for name, a in list(inputs.items()) + list(shape_constants().items()):
        a = np.ascontiguousarray(a)
        arrays[f"in_{name}"] = a
        ins[name] = nc.dram_tensor(f"in_{name}", a.shape, mybir.dt.from_np(a.dtype), kind="ExternalInput").ap()
    out = nc.dram_tensor("out", (1, T, D), F32, kind="ExternalOutput").ap()
    build_block_pair(nc, ins, out)
    r = run_bass_kernel_spmd(nc, [arrays], core_ids=[0])
    return r.results[0]["out"]
```

```python
import numpy as np

import concourse.bass as bass
from concourse import mybir

F32 = mybir.dt.float32
F32R = mybir.dt.float32r
U32 = mybir.dt.uint32
U8 = mybir.dt.uint8
ALU = mybir.AluOpType
ACT = mybir.ActivationFunctionType
AX = mybir.AxisListType

P = 128
D = 1024
T = 1024
DT = D // P
TT = T // P
BANK = 512
EPS = 1e-6

CTX = 256
HEADS = 4
WIDTH = 512
CHUNK = 128
LEVELS = [1, 2, 4, 8, 16, 32, 64]
NCH = T // CHUNK
GROUPS = 4
COL_Q, COL_FF, COL_FB, COL_V, COL_G, COL_U, COL_SV = (i * WIDTH for i in range(7))
COL_GA, COL_GB = 7 * WIDTH, 7 * WIDTH + D

NE = 16
CAP = 2 * T // NE
FF = 2048
ARENA = 51660
NEG = -1.0

QH, KVH, HD = 8, 2, 64
AW = QH * HD
KW = KVH * HD
LW = D - AW
LT = LW // P
CC_XR = AW + 2 * KW
CC_YR = CC_XR + LW
DFF = 3 * D
FT = DFF // P
LRU_C = 8.0


class Lane:

    def __init__(self, nc, engine, name, in_turn):
        self.nc, self.engine, self.name, self.in_turn = nc, engine, name, in_turn
        self.seen = {}
        self.sem, self.count, self.latest = None, 0, None

    def stage(self, name):
        self.label = f"{self.name}_{name}"
        self.sem, self.count = self.nc.alloc_semaphore(self.label), 0

    def after(self, *events):
        for event in events:
            if event is None:
                continue
            if isinstance(event, list):
                self.after(*event)
                continue
            sem, value, name = event
            if value > self.seen.get(name, 0):
                self.engine.wait_ge(sem, value)
                self.seen[name] = value
        return self.engine

    def mark(self, instruction):
        self.count += 1
        instruction.then_inc(self.sem, 1)
        self.latest = (self.sem, self.count, self.label)
        return self.latest

    def run(self, issue, *events):
        self.after(*events)
        if self.in_turn:
            self.after(self.latest)
        return self.mark(issue(self.engine))


class Transfers:

    def __init__(self, nc, name):
        self.sem, self.count, self.name = nc.alloc_semaphore(name), 0, name

    def start(self, lane, out, in_, *events):
        lane.after(*events).dma_start(out, in_).then_inc(self.sem, 16)
        self.count += 16
        return self.done()

    def done(self):
        return (self.sem, self.count, self.name)


class Ring:

    def __init__(self, nc, lane, name, slots, loads, free):
        self.lane, self.slots, self.loads = lane, slots, loads
        self.transfers = [Transfers(nc, f"{name}{i}") for i in range(len(slots))]
        self.issued = self.taken = 0
        for i in range(min(len(free), len(loads))):
            self.load(free[i])

    def load(self, *events):
        if self.issued < len(self.loads):
            i = self.issued % len(self.slots)
            out, in_ = self.loads[self.issued](self.slots[i])
            self.issued += 1
            self.transfers[i].start(self.lane, out, in_, *events)

    def take(self):
        assert self.taken < self.issued
        i = self.taken % len(self.slots)
        self.taken += 1
        return self.slots[i], self.transfers[i].done()

    def release(self, event):
        self.load(event)


class Core:

    def __init__(self, nc):
        self.nc = nc
        self.pe = Lane(nc, nc.tensor, "pe", False)
        self.dve = Lane(nc, nc.vector, "dve", True)
        self.act = Lane(nc, nc.scalar, "act", True)
        self.pool = Lane(nc, nc.gpsimd, "pool", True)
        self.sp = Lane(nc, nc.sync, "sp", False)
        self.ident = self.sb("ident", P)
        self.ones = self.sb("ones", P)
        self.masks = self.sb("masks", 15 * P, U8)
        self.vec = self.sb("vec", 4 * P)
        self.mod = self.sb("mod", 96)
        self.small = self.sb("small", 192)
        self.arena_at = nc.sbuf_base
        self.arena = self.sb("arena", ARENA)
        self.psum = nc.alloc_psum_tensor("psum", [P, 8 * BANK], F32)
        self.bank_free = [None] * 8
        self.where = {}

    def sb(self, name, n, dt=F32):
        return self.nc.alloc_sbuf_tensor(name, [P, n], dt)

    def stage(self, name):
        for lane in (self.pe, self.dve, self.act, self.pool):
            lane.stage(name)

    def everything(self):
        return [lane.latest for lane in (self.pe, self.dve, self.act, self.pool)]

    def view(self, at, n):
        assert at + n <= ARENA, (at, n)
        return self.arena[:, at:at + n]

    def rounded(self, name, at, n):
        assert at + n <= ARENA, (at, n)
        return self.nc.alloc_sbuf_tensor_at(name, [P, n], F32R, offset=self.arena_at + 4 * at)[:, :]

    def split(self, name, at, n, apart=None):
        return Parts(self.rounded(f"{name}_high", at, n),
                     self.rounded(f"{name}_low", at + n if apart is None else apart, n))

    def split_tiles(self, name, at, count, n):
        return [self.split(f"{name}{i}", at + i * n, n, apart=at + (count + i) * n) for i in range(count)]

    def cut(self, parts, value, high_lane, low_lane, *events):
        if high_lane is self.act:
            high = self.act.run(lambda e: e.activation(parts.high, value, ACT.Copy), *events)
        else:
            high = high_lane.run(lambda e: e.tensor_copy(parts.high, value), *events)
        low = low_lane.run(lambda e: e.tensor_tensor(parts.low, value, parts.high.bitcast(F32), ALU.subtract), high)
        return [high, low]

    def bank(self, b, n=BANK):
        return self.psum[:, b * BANK:b * BANK + n]

    def col(self, name, i=0, n=1):
        return self.vec[:, self.where[name] + i:self.where[name] + i + n]

    def claim(self, b, n=1):
        self.pe.after(*self.bank_free[b:b + n])

    def freed(self, b, n, event):
        for i in range(b, b + n):
            self.bank_free[i] = event
        return event

    def matmuls(self, out, pairs, *events, step=None):
        self.pe.after(*events)
        for n, (lhsT, rhs) in enumerate(pairs):
            mm = self.pe.engine.matmul(out, lhsT, rhs, start=(n == 0), stop=(n == len(pairs) - 1))
        return self.pe.mark(mm)

    def products(self, out, pairs, first=True, last=True):
        for n, (a, b) in enumerate(pairs):
            for m, (x, y) in enumerate(((a.high, b.high), (a.low, b.high), (a.high, b.low))):
                mm = self.pe.engine.matmul(out, x, y, start=(first and n == 0 and m == 0),
                                           stop=(last and n == len(pairs) - 1 and m == 2))
        return mm

    def turns(self, outs_ins, *events):
        self.pe.after(*events)
        for out, in_ in outs_ins:
            tr = self.pe.engine.transpose(out, in_, self.ident[0:in_.shape[0], 0:in_.shape[0]])
        return self.pe.mark(tr)


class Parts:

    def __init__(self, high, low):
        self.high, self.low = high, low

    def __getitem__(self, at):
        return Parts(self.high[at], self.low[at])

    def rearrange(self, pattern, **sizes):
        return Parts(self.high.rearrange(pattern, **sizes), self.low.rearrange(pattern, **sizes))


class SplitRing:

    def __init__(self, core, ring, parts, lanes, limit, free):
        self.core, self.ring, self.parts, self.lanes, self.limit = core, ring, parts, lanes, limit
        self.cuts, self.ready, self.taken = 0, [None] * len(parts), 0
        for _ in range(len(parts)):
            self.prepare(free)

    def prepare(self, *free):
        if self.cuts < self.limit:
            i = self.cuts % len(self.parts)
            high_lane, low_lane = self.lanes[self.cuts % len(self.lanes)]
            slot, landed = self.ring.take()
            n = self.parts[i].high.shape[1]
            self.ready[i] = self.core.cut(self.parts[i], slot[:, 0:n], high_lane, low_lane, landed, *free)
            self.ring.release(self.ready[i])
            self.cuts += 1

    def take(self):
        i = self.taken % len(self.parts)
        self.taken += 1
        return self.parts[i], self.ready[i]

    def release(self, event):
        self.prepare(event)


def tiled(slot, k):
    return slot.rearrange("p (k n) -> p k n", k=k)


def feature_tile(w, at, width=P):
    k = w.shape[0] // P
    src = w.rearrange("(k p) n -> p k n", p=P)[:, :, at:at + width]
    return lambda slot: (tiled(slot[:, 0:k * width], k), src)


def shape_constants():
    j, i = np.meshgrid(np.arange(P), np.arange(P), indexing="ij")
    masks = [j == i]
    for h in LEVELS:
        same = j // (2 * h) == i // (2 * h)
        masks.append(same & (j // h % 2 == 0) & (i // h % 2 == 1))
    for h in LEVELS:
        same = j // (2 * h) == i // (2 * h)
        masks.append(same & (j // h % 2 == 1) & (i // h % 2 == 0))
    masks = np.stack(masks, 1).astype(np.float32).reshape(P, -1)
    quarter = HD // 4
    inverse = (np.float32(1.0) / np.float32(10000.0) ** (np.arange(0, HD // 2, 2, dtype=np.float32)
                                                         / np.float32(HD // 2))).astype(np.float32)
    token = np.arange(T)
    angles = np.stack([(token // 64).astype(np.float32)[:, None] * inverse,
                       (token % 64).astype(np.float32)[:, None] * inverse], 1).astype(np.float32)
    rope = np.stack([np.cos(angles), np.sin(angles)], 1).astype(np.float32)
    rope = rope.reshape(TT, P, 4 * quarter).transpose(1, 0, 2).reshape(P, -1)
    return {
        "identity": np.eye(P, dtype=np.float32),
        "pair_masks": masks,
        "rope_table": np.ascontiguousarray(rope),
    }


def row_scale(core, sums, n, *events):
    a = core.dve.run(lambda e: e.tensor_scalar(sums, sums, 1.0 / n, EPS, ALU.mult, ALU.add), *events)
    b = core.act.run(lambda e: e.activation(sums, sums, ACT.Sqrt), a)
    return core.dve.run(lambda e: e.reciprocal(sums, sums), b)


def norm_rows(core, tok, n_tiles, sums, junk, landed):
    for t in range(n_tiles):
        ev = core.act.run(lambda e: e.activation(junk, tok[:, t, :], ACT.Square, accum_out=sums[:, t:t + 1]),
                          landed[t])
    ready = row_scale(core, sums, D, ev)
    return [core.dve.run(lambda e: e.tensor_scalar(tok[:, t, :], tok[:, t, :], sums[:, t:t + 1], None, ALU.mult),
                         ready) for t in range(n_tiles)]


def turn_and_modulate(core, tok, n_tiles, j, b, out, scale, shift, *events):
    core.claim(b, 2)
    turned = core.turns([(core.bank(b, D)[:, t * P:(t + 1) * P], tok[:, t, j * P:(j + 1) * P])
                         for t in range(n_tiles)], *events)
    ev = core.act.run(lambda e: e.activation(out, core.bank(b, n_tiles * P), ACT.Identity, bias=shift, scale=scale),
                      turned)
    return core.freed(b, 2, ev)


def turn_and_cut(core, tok, j, b, out, scale, *events):
    core.claim(b, 2)
    turned = core.turns([(core.bank(b, T)[:, t * P:(t + 1) * P], tok[:, t, j * P:(j + 1) * P]) for t in range(TT)],
                        *events)
    ev = core.act.run(lambda e: e.activation(out.high, core.bank(b, T), ACT.Copy, scale=scale), turned)
    ev = core.dve.run(lambda e: e.scalar_tensor_tensor(out=out.low, in0=core.bank(b, T), scalar=scale,
                                                       in1=out.high.bitcast(F32), op0=ALU.mult, op1=ALU.subtract), ev)
    return core.freed(b, 2, ev)


HT, RING_A, WIDE, OT, YB = 0, 8192, 16384, 20480, 24576
VV, RAW, UNIT, KRT, SALL, VCTX = 28672, 32768, 39936, 46080, 47104, 48128
BSB, WST, S0, KC = 49152, 49664, 50176, 50432
MERGED, WOUT = UNIT, VV
GM_ROW, GF_ROW, XT = BSB, VCTX, YB


def start(core, ins):
    nc, pe, dve, act, sp = core.nc, core.pe, core.dve, core.act, core.sp
    core.stage("start")
    rows = core.view(38912, 4 * P).rearrange("p (n c) -> p n c", n=4)
    cleared = dve.run(lambda e: e.memset(core.view(38912, 4 * P), 0.0))
    core.ones_set = dve.run(lambda e: e.memset(core.ones[:, :], 1.0))
    core.eps = core.small[:, 184:185]
    core.eps_set = dve.run(lambda e: e.memset(core.eps, EPS))
    first = Transfers(nc, "dma_constants")
    first.start(sp, core.ident[:, :], ins["identity"])
    masks_f = core.view(RING_A, 15 * P)
    first.start(sp, masks_f, ins["pair_masks"])
    by_rows = lambda name: ins[name].rearrange("a (r p) -> (a r) p", p=P)
    pairs_of_blocks = lambda name: ins[name].rearrange("a (r h) j -> (a r) (h j)", h=2)
    vectors = [
        (0, "c", by_rows("c")), (0, "c_ctx", ins["c_ctx"].rearrange("(r p) -> r p", p=P)),
        (0, "norm_mix", by_rows("norm_mix_w")), (0, "ada_b", by_rows("ada_b")),
        (0, "lb", ins["hgrn_lb_logits"].rearrange("a b (r p) -> (a b r) p", p=P)),
        (0, "hgrn_norm", by_rows("hgrn_norm_w")), (0, "sgu_norm", by_rows("sgu_norm_w")),
        (0, "norm_ffn", by_rows("norm_ffn_w")), (1, "norm1", by_rows("norm1_g_2")),
        (1, "lru_conv_w", ins["lru_conv_w_2"].rearrange("a w (r p) -> (a w r) p", p=P)),
        (1, "lru_conv_b", by_rows("lru_conv_b_2")), (1, "ba_f", pairs_of_blocks("ba_f_2")),
        (1, "bx_f", pairs_of_blocks("bx_f_2")), (1, "ba_b", pairs_of_blocks("ba_b_2")),
        (1, "bx_b", pairs_of_blocks("bx_b_2")), (1, "lam_f", by_rows("lam_f_2")),
        (1, "lam_b", by_rows("lam_b_2")), (1, "norm2", by_rows("norm2_g_2")),
        (1, "up_conv_b", by_rows("up_conv_b_2")),
        (2, "up_conv_w01", ins["up_conv_w_2"][:, 0:2, :].rearrange("a w (r p) -> (a w r) p", p=P)),
        (3, "up_conv_w2", ins["up_conv_w_2"][:, 2:3, :].rearrange("a w (r p) -> (a w r) p", p=P)),
    ]
    used = [0] * 4
    for t, name, src in vectors:
        n = src.shape[0]
        first.start(sp, rows[used[t]:used[t] + n, t, :], src, cleared)
        core.where[name] = t * P + used[t]
        used[t] += n
        assert used[t] <= P
    x_tok = core.view(VV, TT * D).rearrange("p (t d) -> p t d", t=TT)
    ctx_tok = core.view(36864, 2 * D).rearrange("p (t d) -> p t d", t=2)
    ctx_in = Transfers(nc, "dma_ctx").start(sp, ctx_tok, ins["ctx"].rearrange("a (t p) d -> p (a t) d", p=P))
    x_dram = ins["x"].rearrange("a (t p) d -> p (a t) d", p=P)
    x_in = [Transfers(nc, f"dma_x{i}").start(sp, x_tok[:, 4 * i:4 * i + 4, :], x_dram[:, 4 * i:4 * i + 4, :])
            for i in range(2)]
    w_in = ins["w_in"][0]
    ada_slots = [core.view(at, 4096) for at in (RING_A + 4096, YB, 40960, 45056)]
    ada = Ring(nc, sp, "dma_ada", ada_slots, [feature_tile(ins["ada_w"][0], c * BANK, BANK) for c in range(4)],
               [None] * 4)
    wide_loads = [feature_tile(w_in, COL_V, BANK), feature_tile(w_in, COL_SV, BANK)]
    wide_loads += [feature_tile(ins["ada_w"][0], c * BANK, BANK) for c in range(4, 12)]
    core.wide = Ring(nc, sp, "dma_wide", [core.view(WIDE, 4096)], wide_loads, [None])
    order = []
    for h in range(HEADS):
        order += [COL_Q + h * P, COL_FF + h * P, COL_FB + h * P]
    order += [COL_U + g * P for g in range(GROUPS)] + [COL_G + h * P for h in range(HEADS)]
    loads = [feature_tile(w_in, at) for at in order]
    for j in range(DT):
        loads += [feature_tile(w_in, COL_GA + j * P), feature_tile(ins["w_branch_a"][0], j * P),
                  feature_tile(w_in, COL_GB + j * P), feature_tile(ins["w_branch_b"][0], j * P)]

    turned = core.turns([(core.bank(0)[:, t * P:(t + 1) * P], rows[:, t, :]) for t in range(4)], first.done())
    core.vec_ok = dve.run(lambda e: e.tensor_copy(core.vec[:, :], core.bank(0)), turned)
    core.freed(0, 1, core.vec_ok)
    core.masks_ok = dve.run(lambda e: e.tensor_copy(core.masks[:, :], masks_f))

    silu_c = core.small[:, 0:16].rearrange("p (k s) -> p k s", s=2)
    act.run(lambda e: e.activation(silu_c[:, :, 0], core.col("c", 0, 8), ACT.Silu), core.vec_ok)
    core.silu_ok = act.run(lambda e: e.activation(silu_c[:, :, 1], core.col("c_ctx", 0, 8), ACT.Silu))
    core.silu_c = silu_c
    core.ada_rows_free = None
    core.mod_v = core.mod[:, :].rearrange("p (j s) -> p j s", s=2)

    junk = core.view(39424, D)
    ctx_n = norm_rows(core, ctx_tok, 2, core.small[:, 16:18], junk, [ctx_in] * 2)
    x_n = norm_rows(core, x_tok, TT, core.small[:, 24:32], junk, [x_in[0]] * 4 + [x_in[1]] * 4)
    for c in range(4):
        for _ in ada_chunk(core, ada, c, c % 2):
            pass
    mix_scale = core.small[:, 32:48].rearrange("p (j s) -> p j s", s=2)
    for s in range(2):
        a = dve.run(lambda e: e.tensor_scalar(mix_scale[:, :, s], core.mod_v[:, 8:16, s], 1.0, None, ALU.add))
        ok = dve.run(lambda e: e.tensor_tensor(mix_scale[:, :, s], mix_scale[:, :, s], core.col("norm_mix", 0, 8),
                                               ALU.mult), a)
    core.hT = core.view(HT, DT * T).rearrange("p (j t) -> p j t", j=DT)
    core.hcT = core.view(YB, DT * CTX).rearrange("p (j t) -> p j t", j=DT)
    for j in range(DT):
        core.hc_ok = turn_and_modulate(core, ctx_tok, 2, j, 2 + 2 * (j % 3), core.hcT[:, j, :],
                                       mix_scale[:, j, 1:2], core.mod_v[:, j, 1:2], ctx_n, ok)
    for j in range(DT):
        core.h_ok = turn_and_modulate(core, x_tok, TT, j, 2 + 2 * (j % 3), core.hT[:, j, :],
                                      mix_scale[:, j, 0:1], core.mod_v[:, j, 0:1], x_n, ok)

    low, e0, e1 = core.small[:, 48:56], core.small[:, 56:64], core.small[:, 64:72]
    core.low, core.span = low, core.small[:, 72:80]
    for d in range(2):
        l0, l1, sl = core.col("lb", 8 * d, 4), core.col("lb", 8 * d + 4, 4), slice(4 * d, 4 * d + 4)
        dve.run(lambda e: e.tensor_tensor(low[:, sl], l0, l1, ALU.max))
        dve.run(lambda e: e.tensor_tensor(e0[:, sl], l0, low[:, sl], ALU.subtract))
        a = dve.run(lambda e: e.tensor_tensor(e1[:, sl], l1, low[:, sl], ALU.subtract))
    b = act.run(lambda e: e.activation(core.small[:, 56:72], core.small[:, 56:72], ACT.Exp), a)
    dve.run(lambda e: e.tensor_tensor(low, e0, e1, ALU.add), b)
    dve.run(lambda e: e.reciprocal(low, low))
    dve.run(lambda e: e.tensor_tensor(low, low, e0, ALU.mult))
    core.low_ok = dve.run(lambda e: e.tensor_scalar(core.span, low, -1.0, 1.0, ALU.mult, ALU.add))

    core.score = [core.view(UNIT + 3072 * d + 2048, NCH * CHUNK) for d in range(2)]
    for d in range(2):
        core.score_free = dve.run(lambda e: e.memset(core.score[d], 0.0), core.pe.latest, act.latest)

    sgu_rows = core.view(UNIT, GROUPS * P).rearrange("p (g s) -> p g s", g=GROUPS)
    core.sgu_wT = core.view(WST, GROUPS * P).rearrange("p (g t) -> p g t", g=GROUPS)
    core.sgu_bias = core.view(BSB, GROUPS * P)
    dma_sgu = Transfers(nc, "dma_sgu")
    dma_sgu.start(sp, sgu_rows, ins["sgu_w"][0].rearrange("g t s -> t g s"), core.everything())
    landed = dma_sgu.start(sp, core.sgu_bias, ins["sgu_b"].rearrange("a g t -> (a g t)").partition_broadcast(P))
    slots = [core.view(RING_A + 1024 * i, 1024) for i in range(8)]
    core.feat = Ring(nc, sp, "dma_feature", slots, loads, [core.masks_ok] * 4 + [core.pe.latest] * 4)
    core.claim(0)
    turned = core.turns([(core.bank(0)[:, g * P:(g + 1) * P], sgu_rows[:, g, :]) for g in range(GROUPS)], landed)
    ev = dve.run(lambda e: e.tensor_copy(core.view(WST, GROUPS * P), core.bank(0)), turned, landed)
    core.freed(0, 1, ev)
    core.sgu_ok = ev


def ada_chunk(core, ring, c, b):
    slot, landed = ring.take()
    w = tiled(slot, DT)
    core.pe.after(landed, core.silu_ok)
    core.claim(b)
    for k in range(DT):
        mm = core.pe.engine.matmul(core.bank(b)[0:2, :], core.silu_c[:, k, :], w[:, k, :], start=(k == 0),
                                   stop=(k == DT - 1))
        if k < DT - 1:
            yield
    summed = core.pe.mark(mm)
    ring.release(summed)
    rows = core.view(KC, BANK)[0:2, :]
    ev = core.dve.run(lambda e: e.tensor_copy(rows, core.bank(b)[0:2, :]), summed, core.ada_rows_free)
    yield
    out = core.bank(b, 8).rearrange("p (m s) -> p m s", s=2)
    core.ada_rows_free = turned = core.turns([(out[:, m, :], rows[:, m * P:(m + 1) * P]) for m in range(4)], ev)
    for s in range(2):
        ev = core.dve.run(lambda e: e.tensor_tensor(core.mod_v[:, 4 * c:4 * c + 4, s], out[:, :, s],
                                                    core.col("ada_b", 4 * c, 4), ALU.add), turned)
    core.freed(b, 1, ev)
    core.mod_ok = ev
    yield


def values(core):
    core.v = core.view(VV, TT * WIDTH).rearrange("p (t n) -> p t n", t=TT)
    core.vctx = core.view(VCTX, 2 * WIDTH).rearrange("p (t n) -> p t n", t=2)
    slot, landed = core.wide.take()
    w = tiled(slot, DT)
    x_free = core.everything()
    for t in range(TT + 2):
        src, out = (core.hT, core.v[:, t, :]) if t < TT else (core.hcT, core.vctx[:, t - TT, :])
        at = (t % TT if t < TT else t - TT) * P
        b = t % 4
        core.claim(b)
        mm = core.matmuls(core.bank(b), [(src[:, k, at:at + P], w[:, k, :]) for k in range(DT)], landed,
                          core.h_ok)
        lane = core.act if t % 2 else core.dve
        if t % 2:
            ev = core.act.run(lambda e: e.activation(out, core.bank(b), ACT.Copy), mm, x_free)
        else:
            ev = core.dve.run(lambda e: e.tensor_copy(out, core.bank(b)), mm, x_free)
        core.freed(b, 1, ev)
    core.wide.release(mm)
    core.v_ok = [core.act.latest, core.dve.latest]


def feature_halves(core, slot, landed, finish, k_of=None, banks=(6, 7)):
    src = core.hT if k_of is None else k_of
    n = src.shape[1]
    w = tiled(slot[:, 0:n * P], n)
    for half in range(2):
        b = banks[half]
        core.claim(b)
        core.pe.after(landed)
        for k in range(n):
            mm = core.pe.engine.matmul(core.bank(b), w[:, k, :], src[:, k, half * BANK:(half + 1) * BANK],
                                       start=(k == 0), stop=(k == n - 1))
            if k < n - 1:
                yield
        ev = core.pe.mark(mm)
        core.freed(b, 1, finish(half, b, ev))
        yield


def raw_head(core, h):
    r = RAW + 3584 * (h % 2)
    free = core.raw_free[h % 2]
    q = core.view(r, T)
    slot, landed = core.feat.take()
    yield from feature_halves(core, slot, landed, lambda half, b, ev: core.act.run(
        lambda e: e.activation(q[:, half * BANK:(half + 1) * BANK], core.bank(b), ACT.Silu), ev, free))
    core.feat.release(core.pe.latest)
    core.q_ok[h] = core.act.latest
    for d in range(2):
        f, fc = core.view(r + T * (d + 1), T), core.view(r + 3 * T + CTX * d, CTX)
        slot, landed = core.feat.take()
        w = tiled(slot, DT)
        low, span = core.low[:, 4 * d + h:4 * d + h + 1], core.span[:, 4 * d + h:4 * d + h + 1]

        def gate(out, b, n, ev):
            s = core.act.run(lambda e: e.activation(out, core.bank(b, n), ACT.Sigmoid), ev, free)
            core.f_ok[h] = core.pool.run(lambda e: e.tensor_scalar(out, out, span, low, ALU.mult, ALU.add),
                                         s, core.low_ok)
            return s
        yield from feature_halves(core, slot, landed, lambda half, b, ev: gate(
            f[:, half * BANK:(half + 1) * BANK], b, BANK, ev))
        b = 6
        core.claim(b)
        for k in range(DT):
            mm = core.pe.engine.matmul(core.bank(b, CTX), w[:, k, :], core.hcT[:, k, :], start=(k == 0),
                                       stop=(k == DT - 1))
            if k < DT - 1:
                yield
        ev = core.pe.mark(mm)
        core.feat.release(ev)
        core.freed(b, 1, gate(fc, b, CTX, ev))
        yield


def halves(ap, h):
    return ap.rearrange("p (n s h) -> p n s h", s=2, h=h)


def decay_step(core, lane, way, h, decay, key, query, *events):
    d = halves(decay, h)
    ends = h - 1 if way == 0 else 0
    old, new = (0, 1) if way == 0 else (1, 0)
    n = d.shape[1]
    k = halves(key, h)
    ev = lane.run(lambda e: e.tensor_tensor(k[:, :, old, :], k[:, :, old, :],
                                            d[:, :, new, ends:ends + 1].broadcast_to([P, n, h]), ALU.mult), *events)
    if query is not None:
        q = halves(query, h)
        ev = lane.run(lambda e: e.tensor_tensor(q[:, :, new, :], q[:, :, new, :],
                                                d[:, :, old, ends:ends + 1].broadcast_to([P, n, h]), ALU.mult))
    at = d[:, :, new, ends:ends + 1]
    return lane.run(lambda e: e.tensor_tensor(at, at, d[:, :, old, ends:ends + 1], ALU.mult), ev)


def head_scan(core, h, fill):
    pe, dve, act, pool = core.pe, core.dve, core.act, core.pool
    r = RAW + 3584 * (h % 2)
    q = core.view(r, T)
    f = [core.view(r + T * (d + 1), T) for d in range(2)]
    fc = [core.view(r + 3 * T + CTX * d, CTX) for d in range(2)]
    key = [core.view(UNIT + 3072 * d, T) for d in range(2)]
    query = [core.view(UNIT + 3072 * d + 1024, T) for d in range(2)]
    key_c = [core.view(KC + CTX * d, CTX) for d in range(2)]
    krt = core.view(KRT, NCH * P).rearrange("p (c k) -> p c k", c=NCH)
    states = core.view(SALL, NCH * P).rearrange("p (c v) -> p c v", c=NCH)
    s0 = [core.view(S0 + P * d, P) for d in range(2)]
    head_cols = slice(h * P, (h + 1) * P)
    ready, ready_c = [None] * 2, [None] * 2
    for d in range(2):
        dve.run(lambda e: e.tensor_scalar(key[d], f[d], -1.0, 1.0, ALU.mult, ALU.add), core.f_ok[h],
                core.unit_free[d])
        ready[d] = dve.run(lambda e: e.tensor_tensor(query[d], q, f[d], ALU.mult), core.q_ok[h])
    for d in range(2):
        ev = pool.run(lambda e: e.tensor_scalar(key_c[d], fc[d], -1.0, 1.0, ALU.mult, ALU.add), core.kc_free)
        for lv in LEVELS:
            ev = decay_step(core, pool, d, lv, fc[d], key_c[d], None, ev)
        ready_c[d] = ev
    for n in range(len(LEVELS) + 1):
        for d in range(2):
            b = 2 * d
            core.claim(b, 2)
            pe.after(ready[d])
            rhs = q if n == 0 else query[d]
            for c in range(NCH):
                at = slice(c * CHUNK, (c + 1) * CHUNK)
                mm = pe.engine.matmul(core.bank(b, T)[:, at], key[d][:, at], rhs[:, at], start=True, stop=True)
            paired = pe.mark(mm)
            m = 0 if n == 0 else n + (len(LEVELS) if d else 0)
            mask = core.masks[:, m * P:(m + 1) * P].rearrange("p (a i) -> p a i", a=1).broadcast_to([P, NCH, P])
            ev = dve.run(lambda e: e.copy_predicated(
                core.score[d].rearrange("p (c i) -> p c i", c=NCH), mask,
                core.bank(b, T).rearrange("p (c i) -> p c i", c=NCH)), paired, core.score_free)
            core.freed(b, 2, ev)
            if n > 0:
                ready[d] = decay_step(core, dve, d, LEVELS[n - 1], f[d], key[d], query[d], paired)
            fill(3)
    core.claim(4, 2)
    order_c = [[0, 1], [1, 0]]
    turned = core.turns([(core.bank(4)[:, (2 * d + c) * P:(2 * d + c + 1) * P], key_c[d][:, c * P:(c + 1) * P])
                         for d in range(2) for c in range(2)], ready_c[1], ready_c[0])
    core.kc_free = turned
    kr_ok = act.run(lambda e: e.activation(core.view(KRT, 4 * P), core.bank(4), ACT.Copy), turned, core.krt_free)
    core.freed(4, 1, kr_ok)
    fill(2)
    pe.after(kr_ok, core.v_ok)
    for d in range(2):
        for c in range(2):
            mm = pe.engine.matmul(core.bank(5)[:, (2 * d + c) * P:(2 * d + c + 1) * P], krt[:, 2 * d + c, :],
                                  core.vctx[:, c, head_cols], start=True, stop=True)
    u_ok = pe.mark(mm)
    for d in range(2):
        a, z = order_c[d]
        part = lambda c: core.bank(5)[:, (2 * d + c) * P:(2 * d + c + 1) * P]
        dve.run(lambda e: e.tensor_copy(s0[d], part(a)), u_ok)
        last = z * P + (P - 1 if d == 0 else 0)
        ev = dve.run(lambda e: e.scalar_tensor_tensor(out=s0[d], in0=s0[d], scalar=fc[d][:, last:last + 1],
                                                      in1=part(z), op0=ALU.mult, op1=ALU.add), ready_c[d])
    core.freed(5, 1, ev)
    fill(2)
    oT = core.view(OT + T * h, T)
    for d in range(2):
        core.claim(4, 2)
        turned = core.turns([(core.bank(4, T)[:, c * P:(c + 1) * P], key[d][:, c * P:(c + 1) * P])
                             for c in range(NCH)], ready[d])
        ev = act.run(lambda e: e.activation(core.view(KRT, T), core.bank(4, T), ACT.Copy), turned, u_ok)
        core.freed(4, 2, ev)
        fill(3)
        core.claim(4, 2)
        pe.after(ev)
        for c in range(NCH):
            mm = pe.engine.matmul(core.bank(4, T)[:, c * P:(c + 1) * P], krt[:, c, :], core.v[:, c, head_cols],
                                  start=True, stop=True)
        u_ok = pe.mark(mm)
        seq = list(range(NCH)) if d == 0 else list(range(NCH))[::-1]
        ev = dve.run(lambda e: e.tensor_copy(states[:, seq[0], :], s0[d]), core.states_free)
        for c, nxt in zip(seq, seq[1:]):
            last = c * P + (P - 1 if d == 0 else 0)
            ev = dve.run(lambda e: e.scalar_tensor_tensor(
                out=states[:, nxt, :], in0=states[:, c, :], scalar=f[d][:, last:last + 1],
                in1=core.bank(4, T)[:, c * P:(c + 1) * P], op0=ALU.mult, op1=ALU.add), u_ok)
        core.freed(4, 2, ev)
        fill(4)
        b = 2 * d
        core.claim(b, 2)
        pe.after(ev)
        for c in range(NCH):
            at = slice(c * CHUNK, (c + 1) * CHUNK)
            pe.engine.matmul(core.bank(b, T)[:, at], core.v[:, c, head_cols], core.score[d][:, at], start=True,
                             stop=False)
            mm = pe.engine.matmul(core.bank(b, T)[:, at], states[:, c, :], query[d][:, at], start=False, stop=True)
        done = pe.mark(mm)
        core.states_free = core.krt_free = done
        core.unit_free[d] = done
        if d == 0:
            ev = act.run(lambda e: e.activation(oT, core.bank(b, T), ACT.Copy), done)
        else:
            ev = dve.run(lambda e: e.tensor_tensor(oT, oT, core.bank(b, T), ALU.add), done, ev0)
        ev0 = ev
        core.freed(b, 2, ev)
    core.score_free = done
    core.raw_free[h % 2] = [done, dve.latest, pool.latest]
    square = query[1]
    sq = act.run(lambda e: e.activation(square, oT, ACT.Square), ev)
    core.claim(4, 2)
    pe.after(sq)
    for c in range(NCH):
        mm = pe.engine.matmul(core.bank(4)[:, c:c + 1], square[:, c * P:(c + 1) * P], core.ones[:, 0:1], start=True,
                              stop=True)
    summed = pe.mark(mm)
    rs = core.small[:, 80:88]
    ev = dve.run(lambda e: e.tensor_copy(rs, core.bank(4, NCH)), summed)
    core.freed(4, 1, ev)
    ev = row_scale(core, rs, P, ev)
    fill(4)
    diag = key[1]
    ev = dve.run(lambda e: e.tensor_tensor(
        diag.rearrange("p (c i) -> p c i", c=NCH),
        core.ident[:, :].rearrange("p (a i) -> p a i", a=1).broadcast_to([P, NCH, P]),
        rs.rearrange("p (c a) -> p c a", a=1).broadcast_to([P, NCH, P]), ALU.mult), ev, core.unit_free[1])
    core.claim(4, 2)
    pe.after(ev)
    for half in range(2):
        mm = pe.engine.matmul(core.bank(4 + half), core.ones[:, :], diag[:, half * BANK:(half + 1) * BANK],
                              start=True, stop=True)
    spread = pe.mark(mm)
    core.unit_free[1] = spread
    ev = dve.run(lambda e: e.tensor_tensor(oT, oT, core.bank(4, T), ALU.mult), spread)
    core.freed(4, 2, ev)


def hgrn(core):
    core.stage("hgrn")
    core.raw_free = [core.everything(), core.everything()]
    core.unit_free = [core.everything(), core.everything()]
    core.q_ok, core.f_ok = {}, {}
    core.kc_free = core.krt_free = core.states_free = core.everything()
    for _ in raw_head(core, 0):
        pass
    for h in range(HEADS):
        other = raw_head(core, h + 1) if h + 1 < HEADS else sgu_gates(core)

        def fill(n):
            for _ in range(n):
                next(other, None)
        head_scan(core, h, fill)
        for _ in other:
            pass


def sgu_gates(core):
    core.uT = core.view(YB, GROUPS * T).rearrange("p (g t) -> p g t", g=GROUPS)
    for g in range(GROUPS):
        slot, landed = core.feat.take()
        yield from feature_halves(core, slot, landed, lambda half, b, ev: core.act.run(
            lambda e: e.activation(core.uT[:, g, half * BANK:(half + 1) * BANK], core.bank(b), ACT.Gelu_apprx_tanh),
            ev))
        core.feat.release(core.pe.latest)



def sgu_values(core):
    nw = lambda g: core.col("sgu_norm", g)
    slot, landed = core.wide.take()
    w = tiled(slot, DT)
    gv, squares = core.view(RAW, WIDTH), core.view(RAW + WIDTH, WIDTH)
    sums = core.small[:, 88:92]
    by_group = lambda ap: ap.rearrange("p (g c) -> p g c", g=GROUPS)
    gv_free = core.raw_free[0]
    for t in range(TT):
        core.claim(6)
        core.pe.after(landed)
        for k in range(DT):
            mm = core.pe.engine.matmul(core.bank(6), core.hT[:, k, t * P:(t + 1) * P], w[:, k, :], start=(k == 0),
                                       stop=(k == DT - 1))
            if k < DT - 1:
                yield
        ev = core.pe.mark(mm)
        if t == TT - 1:
            core.wide.release(ev)
        ev = core.act.run(lambda e: e.activation(gv, core.bank(6), ACT.Gelu_apprx_tanh), ev, gv_free)
        core.freed(6, 1, ev)
        sq = core.act.run(lambda e: e.activation(squares, gv, ACT.Square))
        ev = core.dve.run(lambda e: e.tensor_reduce(sums, by_group(squares), AX.X, ALU.add), sq)
        ev = row_scale(core, sums, P, ev)
        ev = core.dve.run(lambda e: e.tensor_tensor(
            by_group(squares), by_group(gv), sums.rearrange("p (g a) -> p g a", a=1).broadcast_to([P, GROUPS, P]),
            ALU.mult))
        yield
        core.claim(7)
        core.pe.after(ev, core.sgu_ok)
        for g in range(GROUPS):
            mm = core.pe.engine.matmul(core.bank(7)[:, g * P:(g + 1) * P], squares[:, g * P:(g + 1) * P],
                                       core.sgu_wT[:, g, :], start=True, stop=True)
        mixed = core.pe.mark(mm)
        gv_free = [mixed, ev]
        tmp = core.view(RAW + 2 * WIDTH, WIDTH)
        for g in range(GROUPS):
            core.dve.run(lambda e: e.scalar_tensor_tensor(
                out=tmp[:, g * P:(g + 1) * P], in0=core.bank(7)[:, g * P:(g + 1) * P], scalar=nw(g),
                in1=core.sgu_bias[:, g * P:(g + 1) * P], op0=ALU.mult, op1=ALU.add), mixed)
        core.freed(7, 1, core.dve.latest)
        ut = core.uT[:, :, t * P:(t + 1) * P]
        core.sgu_done = core.dve.run(lambda e: e.tensor_tensor(ut, ut, by_group(tmp), ALU.mult), core.u_ok)
        yield


def hgrn_gates(core):
    tmp = core.view(RAW + 3 * WIDTH, BANK)
    for h in range(HEADS):
        slot, landed = core.feat.take()

        def gate(half, b, ev):
            s = core.act.run(lambda e: e.activation(tmp, core.bank(b), ACT.Silu), ev, core.gate_free)
            o = core.view(OT + T * h + half * BANK, BANK)
            core.gate_free = core.dve.run(lambda e: e.scalar_tensor_tensor(
                out=o, in0=o, scalar=core.col("hgrn_norm", h), in1=tmp, op0=ALU.mult, op1=ALU.mult), s)
            return s
        yield from feature_halves(core, slot, landed, gate)
        core.feat.release(core.pe.latest)


def merge(core, ins):
    core.stage("merge")
    oT = core.view(OT, HEADS * T).rearrange("p (k t) -> p k t", k=HEADS)
    core.merged = core.view(MERGED, DT * T).rearrange("p (j t) -> p j t", j=DT)
    tmp_free = [[core.wide.transfers[0].done(), core.everything()]] * 2
    unit_free = core.everything()
    for j in range(DT):
        terms = []
        for n, (src, branch) in enumerate(((oT, "a"), (core.uT, "b"))):
            tmp = core.view(WIDE + 2048 * (j % 2) + 1024 * n, T)
            for what in ("gate", "branch"):
                slot, landed = core.feat.take()
                pair = 4 * (n % 2) + (0 if what == "gate" else 2)
                if what == "gate":
                    run = feature_halves(core, slot, landed, lambda half, b, ev: core.act.run(
                        lambda e: e.activation(tmp[:, half * BANK:(half + 1) * BANK], core.bank(b), ACT.Sigmoid), ev,
                        tmp_free[j % 2]), banks=(pair, pair + 1))
                else:
                    sig = core.act.latest
                    core.pe.after(core.sgu_done, core.gate_free)
                    run = feature_halves(core, slot, landed, lambda half, b, ev: core.dve.run(
                        lambda e: e.tensor_tensor(tmp[:, half * BANK:(half + 1) * BANK],
                                                  tmp[:, half * BANK:(half + 1) * BANK], core.bank(b), ALU.mult),
                        ev, sig), k_of=src, banks=(pair, pair + 1))
                for _ in run:
                    pass
                core.feat.release(core.pe.latest)
            terms.append(tmp)
        core.merged_ok = core.pool.run(lambda e: e.tensor_tensor(core.merged[:, j, :], terms[0], terms[1], ALU.add),
                                       core.dve.latest, unit_free)
        tmp_free = list(tmp_free)
        tmp_free[j % 2] = core.merged_ok


def gain_rows(core, ins):
    nc = core.nc
    scratch = nc.dram_tensor("gain_rows", (2, D), F32, kind="Internal").ap()
    rows = core.view(GM_ROW + 1024, 256)[0:DT, :].rearrange("p (n c) -> p n c", n=2)
    core.claim(0)
    turned = core.turns([(core.bank(0)[0:DT, n * P:(n + 1) * P], core.mod_v[:, at:at + DT, 0])
                         for n, at in enumerate((2 * DT, 5 * DT))], core.mod_ok)
    ev = core.dve.run(lambda e: e.tensor_copy(core.view(GM_ROW + 1024, 256)[0:DT, :], core.bank(0)[0:DT, 0:256]),
                      turned)
    core.freed(0, 1, ev)
    stored = Transfers(nc, "dma_gain_store").start(core.sp, scratch.rearrange("n (j c) -> j n c", c=P), rows, ev)
    core.gm_row, core.gf_row = core.view(GM_ROW, D), core.view(GF_ROW, D)
    back = Transfers(nc, "dma_gain_rows")
    back.start(core.sp, core.gm_row, scratch[0].partition_broadcast(P), stored, core.everything())
    core.gains_ok = back.start(core.sp, core.gf_row, scratch[1].partition_broadcast(P))
    core.ffn_scale = core.small[:, 96:104]
    a = core.dve.run(lambda e: e.tensor_scalar(core.ffn_scale, core.mod_v[:, 4 * DT:5 * DT, 0], 1.0, None, ALU.add))
    core.ffn_ok = core.dve.run(lambda e: e.tensor_tensor(core.ffn_scale, core.ffn_scale, core.col("norm_ffn", 0, 8),
                                                         ALU.mult), a)


def project_out(core, ins, w_out_ok, w_out):
    nc, pe, dve, act, sp = core.nc, core.pe, core.dve, core.act, core.sp
    core.x_dram = nc.dram_tensor("x_after_mixer", (T, D), F32, kind="Internal").ap()
    core.xn_dram = nc.dram_tensor("x_normed", (T, D), F32, kind="Internal").ap()
    x_src = ins["x"].rearrange("a (t p) d -> (a t) p d", p=P)
    core.xn = core.view(HT, TT * D).rearrange("p (t d) -> p t d", t=TT)
    xt = [core.view(XT + 1024 * i, D) for i in range(2)]
    ht_free = core.everything()
    dma_x = [Transfers(nc, f"dma_x_again{i}") for i in range(2)]
    dma_st = [Transfers(nc, f"dma_x_store{i}") for i in range(2)]
    core.xn_stored = Transfers(nc, "dma_xn_store")
    landed = [dma_x[i].start(sp, xt[i], x_src[i], ht_free) for i in range(2)]
    sums = core.small[:, 104:112]
    for t in range(TT):
        xn = core.xn[:, t, :]
        for half in range(2):
            b = (2 * t + half) % 8
            cols = slice(half * BANK, (half + 1) * BANK)
            core.claim(b)
            mm = core.matmuls(core.bank(b), [(core.merged[:, k, t * P:(t + 1) * P], w_out[:, k, cols])
                                             for k in range(DT)], w_out_ok, core.merged_ok)
            ev = dve.run(lambda e: e.tensor_tensor(xn[:, cols], core.bank(b), core.gm_row[:, cols], ALU.mult), mm,
                         core.gains_ok, ht_free)
            core.freed(b, 1, ev)
        x1 = dve.run(lambda e: e.tensor_tensor(xt[t % 2], xt[t % 2], xn, ALU.add), landed[t % 2])
        st = dma_st[t % 2].start(sp, core.x_dram[t * P:(t + 1) * P, :], xt[t % 2], x1)
        sq = act.run(lambda e: e.activation(xn, xt[t % 2], ACT.Square, accum_out=sums[:, t:t + 1]), x1)
        ev = row_scale(core, sums[:, t:t + 1], D, sq)
        core.xn_ok = dve.run(lambda e: e.tensor_scalar(xn, xt[t % 2], sums[:, t:t + 1], None, ALU.mult), ev)
        core.xn_stored.start(sp, core.xn_dram[t * P:(t + 1) * P, :], xn, core.xn_ok)
        if t + 2 < TT:
            landed[t % 2] = dma_x[t % 2].start(sp, xt[t % 2], x_src[t + 2], st, core.xn_ok)
    core.x_stored = [d.done() for d in dma_st]


STAGED = [8192 + 2048 * i for i in range(8)]
XS, XST, HID, CUT_W, HIDT, YE, XSF = 0, 2048, 6144, 24576, 36864, 40960, 43008
H2T, TOPK = 45056, 50176


def expert_loads(ins):
    gate, up, down = (ins[f"expert_w_{n}"][0] for n in ("gate", "up", "down"))
    loads = []
    for e in range(NE):
        for c in range(FF // BANK):
            for w in (gate, up):
                loads += [feature_tile(w[e][r:r + BANK, :], c * BANK, BANK) for r in range(0, D, BANK)]
        for r in range(0, FF, 2 * P):
            loads.append(feature_tile(down[e][r:r + 2 * P, :], 0, D))
    w_in = ins["w_in_2"][0]
    loads += [feature_tile(w_in[r:r + BANK, :], 0, BANK) for r in range(0, D, BANK)]
    loads.append(feature_tile(w_in, AW, 2 * KW))
    return loads


def route(core, ins, router, router_ok):
    pe, dve, act, pool = core.pe, core.dve, core.act, core.pool
    core.stage("route")
    shift = core.mod_v[:, 3 * DT:4 * DT, 0]
    h2 = [core.view(H2T + 1024 * i, T) for i in range(2)]
    h2_free = [core.everything()] * 2
    core.claim(6, 2)
    for j in range(DT):
        ev = turn_and_modulate(core, core.xn, TT, j, 2 * (j % 3), h2[j % 2], core.ffn_scale[:, j:j + 1],
                               shift[:, j:j + 1], core.xn_ok, core.ffn_ok, h2_free[j % 2])
        pe.after(ev, router_ok)
        for half in range(2):
            mm = pe.engine.matmul(core.bank(6 + half)[0:NE, :], router[:, j, :],
                                  h2[j % 2][:, half * BANK:(half + 1) * BANK], start=(j == 0), stop=(j == DT - 1))
        h2_free = list(h2_free)
        h2_free[j % 2] = pe.mark(mm)
    work = core.view(47104, T)[0:NE, :]
    logits = dve.run(lambda e: e.tensor_copy(work, core.bank(6, T)[0:NE, :]), pe.latest)
    core.freed(6, 2, logits)
    core.claim(0)
    turned = core.turns([(core.bank(0)[:, t * NE:(t + 1) * NE], work[:, t * P:(t + 1) * P]) for t in range(TT)],
                        logits)
    aff = core.view(TOPK + 416, TT * NE)
    by_token = lambda ap: ap.rearrange("p (t e) -> p t e", t=TT)
    lo = core.bank(0, TT * NE)
    peak = core.small[:, 112:120]
    wide = lambda ap: ap.rearrange("p (t a) -> p t a", a=1).broadcast_to([P, TT, NE])
    ev = dve.run(lambda e: e.tensor_reduce(peak, by_token(lo), AX.X, ALU.max), turned)
    ev = dve.run(lambda e: e.tensor_tensor(by_token(aff), by_token(lo), wide(peak), ALU.subtract))
    core.freed(0, 1, ev)
    ev = act.run(lambda e: e.activation(aff, aff, ACT.Exp), ev)
    dve.run(lambda e: e.tensor_reduce(peak, by_token(aff), AX.X, ALU.add), ev)
    dve.run(lambda e: e.reciprocal(peak, peak))
    ev = dve.run(lambda e: e.tensor_tensor(by_token(aff), by_token(aff), wide(peak), ALU.mult))
    core.claim(0, 2)
    turned = core.turns([(core.bank(0, T)[0:NE, t * P:(t + 1) * P], by_token(aff)[:, t, :]) for t in range(TT)], ev)
    ev = dve.run(lambda e: e.tensor_copy(work, core.bank(0, T)[0:NE, :]), turned)
    core.freed(0, 2, ev)
    best = core.view(TOPK, CAP)[0:NE, :]
    which = core.view(TOPK + 128, CAP).bitcast(U32)[0:NE, :]
    as_float = core.view(TOPK + 256, CAP)[0:NE, :]
    for r in range(CAP // 8):
        eight = slice(8 * r, 8 * r + 8)
        dve.run(lambda e: e.max(best[:, eight], work))
        dve.run(lambda e: e.max_index(which[:, eight], best[:, eight], work))
        dve.run(lambda e: e.match_replace(work, best[:, eight], work, NEG))
    ev = dve.run(lambda e: e.tensor_copy(as_float, which))
    core.claim(2)
    turned = core.turns([(core.bank(2)[:, 0:NE], best), (core.bank(2)[:, NE:2 * NE], as_float)], ev)
    core.gate = core.view(TOPK + 384, NE)
    core.index = core.view(TOPK + 400, NE).bitcast(U32)
    dve.run(lambda e: e.tensor_copy(core.gate, core.bank(2)[:, 0:NE]), turned)
    core.routed = dve.run(lambda e: e.tensor_copy(core.index, core.bank(2)[:, NE:2 * NE]))
    core.freed(2, 1, core.routed)


def experts(core, ins):
    nc, pe, dve, act, pool = core.nc, core.pe, core.dve, core.act, core.pool
    core.stage("experts")
    shift = core.mod_v[:, 3 * DT:4 * DT, 0]
    area_free = [core.everything(), core.x_stored, core.xn_stored.done()]
    dma_xs = [Transfers(nc, f"dma_gather{i}") for i in range(2)]
    dma_ye = [Transfers(nc, f"dma_scatter{i}") for i in range(2)]
    xs = [core.view(XS + 1024 * i, D) for i in range(2)]
    xsT = [core.split(f"xsT{i}", XST + 2048 * i, D).rearrange("p (k c) -> p k c", k=DT) for i in range(2)]
    xsF = core.view(XSF, D).rearrange("p (k c) -> p k c", k=DT)
    hid = core.view(HID, FF)
    hidT = core.split("hidT", HIDT, FF).rearrange("p (k c) -> p k c", k=FF // P)
    ye = [core.view(YE + 1024 * i, D) for i in range(2)]
    lanes = [(act, dve)] * 7 + [(act, pool)]
    weights = SplitRing(core, core.expert, [core.split(f"expert_w{i}", CUT_W + 4096 * i, 2048) for i in range(3)],
                        lanes, 24 * NE, area_free)
    xs_free, xsT_free, ye_free = [area_free] * 2, [area_free] * 2, [area_free] * 2
    xsT_ok, gathered = [None, area_free], [None] * 2
    hid_free, hidT_free = area_free, area_free
    scattered = core.x_stored

    def gather(x):
        i = x % 2
        pool.after(core.routed, core.xn_stored.done(), xs_free[i])
        nc.gpsimd.indirect_dma_start(xs[i], None, core.xn_dram,
                                     bass.IndirectOffsetOnAxis(ap=core.index[:, x:x + 1], axis=0)
                                     ).then_inc(dma_xs[i].sem, 16)
        dma_xs[i].count += 16
        gathered[i] = dma_xs[i].done()

    def turn_inputs(x):
        i = x % 2
        core.claim(4, 2)
        turned = core.turns([(core.bank(4, D)[:, j * P:(j + 1) * P], xs[i][:, j * P:(j + 1) * P])
                             for j in range(DT)], gathered[i])
        xs_free[i] = turned
        for j in range(DT):
            part = core.bank(4, D)[:, j * P:(j + 1) * P]
            if j >= DT // 2:
                dve.run(lambda e: e.tensor_scalar(xsF[:, j, :], part, core.ffn_scale[:, j:j + 1], shift[:, j:j + 1],
                                                  ALU.mult, ALU.add), turned, xsT_ok[1 - i])
            else:
                act.run(lambda e: e.activation(xsF[:, j, :], part, ACT.Identity, bias=shift[:, j:j + 1],
                                               scale=core.ffn_scale[:, j:j + 1]), turned, xsT_ok[1 - i])
        core.freed(4, 2, [dve.latest, act.latest])
        xsT_ok[i] = core.cut(xsT[i], xsF, act, dve, dve.latest, xsT_free[i])

    def turn_hidden(c, ready):
        b = 4 + c % 2
        core.claim(b)
        turned = core.turns([(core.bank(b)[:, k * P:(k + 1) * P], hid[:, (4 * c + k) * P:(4 * c + k + 1) * P])
                             for k in range(4)], ready)
        both = core.cut(hidT[:, 4 * c:4 * c + 4, :], core.bank(b).rearrange("p (k c) -> p k c", k=4), act, dve,
                        turned, hidT_free)
        core.freed(b, 1, both)
        return both

    gather(0)
    gather(1)
    turn_inputs(0)
    for x in range(NE):
        i = x % 2
        hid_ok, hidT_ok = [None] * 4, [None] * 4
        for c in range(FF // BANK):
            cols = slice(c * BANK, (c + 1) * BANK)
            made = []
            for n in range(2):
                b = 2 * (c % 2) + n
                core.claim(b)
                for r in range(2):
                    w, ready = weights.take()
                    w = w.rearrange("p (k n) -> p k n", k=4)
                    pe.after(ready, xsT_ok[i])
                    mm = pe.mark(core.products(core.bank(b), [(xsT[i][:, 4 * r + k, :], w[:, k, :])
                                                              for k in range(4)], first=(r == 0), last=(r == 1)))
                    weights.release(mm)
                made.append(mm)
            s = act.run(lambda e: e.activation(hid[:, cols], core.bank(2 * (c % 2)), ACT.Silu), made[0], hid_free)
            core.freed(2 * (c % 2), 1, s)
            hid_ok[c] = dve.run(lambda e: e.tensor_tensor(hid[:, cols], hid[:, cols], core.bank(2 * (c % 2) + 1),
                                                          ALU.mult), s, made[1])
            core.freed(2 * (c % 2) + 1, 1, hid_ok[c])
            if c:
                hidT_ok[c - 1] = turn_hidden(c - 1, hid_ok[c - 1])
        xsT_free[i] = mm
        if x + 1 < NE:
            turn_inputs(x + 1)
        if x + 2 < NE:
            gather(x + 2)
        core.claim(6, 2)
        for c in range(8):
            if c == 3:
                hidT_ok[3] = turn_hidden(3, hid_ok[3])
                hid_free = [pe.latest]
            w, ready = weights.take()
            w = w.rearrange("p (k n) -> p k n", k=2)
            pe.after(ready, hidT_ok[c // 2])
            for half in range(2):
                mm = core.products(core.bank(6 + half), [(hidT[:, 2 * c + k, :], w[:, k, half * BANK:(half + 1) * BANK])
                                                         for k in range(2)], first=(c == 0), last=(c == 7))
            ev = pe.mark(mm)
            weights.release(ev)
        hidT_free = ev
        for half in range(2):
            cols = slice(half * BANK, (half + 1) * BANK)
            out = dve.run(lambda e: e.scalar_tensor_tensor(
                out=ye[i][:, cols], in0=core.bank(6 + half), scalar=core.gate[:, x:x + 1], in1=core.gf_row[:, cols],
                op0=ALU.mult, op1=ALU.mult), ev, ye_free[i], core.gains_ok)
        core.freed(6, 2, out)
        pool.after(out, scattered)
        nc.gpsimd.indirect_dma_start(core.x_dram, bass.IndirectOffsetOnAxis(ap=core.index[:, x:x + 1], axis=0),
                                     ye[i], None, compute_op=ALU.add).then_inc(dma_ye[i].sem, 16)
        dma_ye[i].count += 16
        scattered = ye_free[i] = dma_ye[i].done()
    core.scattered = scattered


H1_HIGH, H1_LOW, X2, JUNK, FINAL_ROW = 0, 24576, 32768, 40960, 43008
WQ, WKV, QK, SQ, ROPED, R1, R2, GAIN, ROPE, VB = (32768, 40960, 45056, 45696, 46336, 46976, 47296, 47616, 48256,
                                                   49792)
QKT, LRU_RING, BLOCKS, LRU_OUT, LRU_W, LRU_TMP = 8192, 14336, 17408, 19456, 32768, 40960
PROB, PROBT, OATT, ATT, LRUT = 32768, 34816, 36864, 0, 24576
WOUT_F, WOUT_P, XN3, X3 = 40960, 8192, 32768, 40960
H3, ACTT, UP_RING, UP_PARTS, CONV, G_ROW = 0, 16384, 32768, 35840, (39936, 49152, 50176), 0
FGROUP = 8


def second_start(core, ins):
    nc, pe, dve, act, sp = core.nc, core.pe, core.dve, core.act, core.sp
    core.stage("second")
    gone = core.everything()
    x2 = core.view(X2, TT * D).rearrange("p (t d) -> p t d", t=TT)
    core.xb_dram = nc.dram_tensor("x_second", (T, D), F32, kind="Internal").ap()
    final_row = core.view(FINAL_ROW, D)
    rows = Transfers(nc, "dma_second_rows")
    rows.start(sp, final_row, ins["final_norm_w"].partition_broadcast(P), gone)
    core.gain_row = core.view(GAIN, (QH + KVH) * HD)
    gains = core.gain_row.rearrange("p (h c) -> p h c", c=HD)
    for h in range(QH + KVH):
        rows.start(sp, gains[:, h, :], ins["q_norm_g_2" if h < QH else "k_norm_g_2"][0].partition_broadcast(P))
    core.rope = core.view(ROPE, TT * HD)
    core.rows_in = rows.start(sp, core.rope, ins["rope_table"])
    core.blocks = core.view(BLOCKS, 16 * P).rearrange("p (w m j) -> p w m j", w=4, m=LT)
    cleared = dve.run(lambda e: e.memset(core.view(BLOCKS, 16 * P), 0.0), gone)
    w_in = ins["w_in_2"][0]
    core.lru_ring = Ring(nc, sp, "dma_lru", [core.view(LRU_RING + 1024 * i, 1024) for i in range(3)],
                         [feature_tile(w_in, at + c * P) for c in range(LT) for at in (CC_XR, CC_YR)], [gone] * 3)
    blocks = Transfers(nc, "dma_blocks")
    for n, name in enumerate(("wa_f_2", "wx_f_2", "wa_b_2", "wx_b_2")):
        src = ins[name][0].rearrange("(m s) i j -> s i m j", s=2)
        for s in range(2):
            core.blocks_in = blocks.start(sp, core.blocks[s * 64:(s + 1) * 64, n, :, s * 64:(s + 1) * 64], src[s],
                                          cleared)
    dma_x2 = [Transfers(nc, f"dma_x2_{i}") for i in range(2)]
    x2_src = core.x_dram.rearrange("(t p) d -> p t d", p=P)
    x2_in = [dma_x2[i].start(sp, x2[:, 4 * i:4 * i + 4, :], x2_src[:, 4 * i:4 * i + 4, :], core.scattered, gone)
             for i in range(2)]
    sums = core.small[:, 120:128]
    sums2 = core.small[:, 128:136]
    junk = core.view(JUNK, D)
    core.xb_stored = Transfers(nc, "dma_xb_store")
    for i in range(2):
        tiles = range(4 * i, 4 * i + 4)
        part, part2 = sums[:, 4 * i:4 * i + 4], sums2[:, 4 * i:4 * i + 4]
        for t in tiles:
            ev = act.run(lambda e: e.activation(junk, x2[:, t, :], ACT.Square, accum_out=sums[:, t:t + 1]), x2_in[i],
                         gone)
        row_scale(core, part, D, ev)
        for t in tiles:
            ev = dve.run(lambda e: e.scalar_tensor_tensor(out=x2[:, t, :], in0=x2[:, t, :], scalar=sums[:, t:t + 1],
                                                          in1=final_row, op0=ALU.mult, op1=ALU.mult), core.rows_in)
            core.xb_stored.start(sp, core.xb_dram[t * P:(t + 1) * P, :], x2[:, t, :], ev)
            ev = act.run(lambda e: e.activation(junk, x2[:, t, :], ACT.Square, accum_out=sums2[:, t:t + 1]), ev)
        row_scale(core, part2, D, ev)
        for t in tiles:
            ready = dve.run(lambda e: e.tensor_scalar(x2[:, t, :], x2[:, t, :], sums2[:, t:t + 1], None, ALU.mult),
                            core.xb_stored.done())
    core.h1T = core.split("h1T", H1_HIGH, DT * T, apart=H1_LOW).rearrange("p (j t) -> p j t", j=DT)
    for j in range(DT):
        core.h1_ok = turn_and_cut(core, x2, j, 2 * (j % 4), core.h1T[:, j, :], core.col("norm1", j), ready, gone)


def second_heads(core, ins):
    nc, pe, dve, act = core.nc, core.pe, core.dve, core.act
    n_heads = QH + KVH
    turned_all = core.pe.latest
    wq, wkv = core.split_tiles("wq", WQ, 2, DT // 2 * AW), core.split("wkv", WKV, DT * 2 * KW)
    w_ok = []
    for n, part in enumerate((*wq, wkv)):
        slot, landed = core.expert.take()
        w_ok.append(core.cut(part, slot, act, dve, landed, turned_all, core.h1_ok))
    wq = [w.rearrange("p (k n) -> p k n", k=DT // 2) for w in wq]
    wkv = wkv.rearrange("p (k n) -> p k n", k=DT)
    core.qkT = core.view(QKT, 5 * T).rearrange("p (i t) -> p i t", i=5)
    core.vb = core.view(VB, TT * KW).rearrange("p (t n) -> p t n", t=TT)
    qk, sq, roped = core.view(QK, 640), core.view(SQ, 640), core.view(ROPED, 640)
    r1, r2 = core.view(R1, 320), core.view(R2, 320)
    sums = core.small[:, 136:146]
    ev_gain = dve.run(lambda e: e.tensor_scalar(core.gain_row[:, 0:AW], core.gain_row[:, 0:AW], HD ** -0.5, None,
                                                ALU.mult), core.rows_in)
    by_head = lambda ap: ap.rearrange("p (h c) -> p h c", c=HD)
    parts = lambda ap: ap.rearrange("p (h a s c) -> p h a s c", a=2, s=2, c=HD // 4)
    flat = lambda ap: ap.rearrange("p (h a c) -> p h a c", a=2, c=HD // 4)
    roped_free = None
    turns_free = [core.h1_ok, w_ok]
    for t in range(TT):
        tok = slice(t * P, (t + 1) * P)
        b = 2 * (t % 2)
        core.claim(b, 2)
        pe.after(w_ok, core.h1_ok)
        core.products(core.bank(b), [(core.h1T[:, k, tok], wq[k // 4][:, k % 4, :]) for k in range(DT)])
        mm = pe.mark(core.products(core.bank(b + 1, 2 * KW), [(core.h1T[:, k, tok], wkv[:, k, :])
                                                              for k in range(DT)]))
        both = core.bank(b, n_heads * HD)
        ev = act.run(lambda e: e.activation(sq, both, ACT.Square), mm)
        act.run(lambda e: e.activation(core.vb[:, t, :], core.bank(b + 1)[:, KW:2 * KW], ACT.Copy), turns_free)
        ev = dve.run(lambda e: e.tensor_reduce(sums, by_head(sq), AX.X, ALU.add), ev)
        ev = row_scale(core, sums, HD, ev)
        dve.run(lambda e: e.tensor_tensor(
            by_head(qk), by_head(both), sums.rearrange("p (h a) -> p h a", a=1).broadcast_to([P, n_heads, HD]),
            ALU.mult), ev)
        core.freed(b, 2, [dve.latest, act.latest])
        ev = dve.run(lambda e: e.tensor_tensor(qk, qk, core.gain_row, ALU.mult), ev_gain)
        table = core.rope[:, t * HD:(t + 1) * HD].rearrange("p (f a c) -> p f a c", f=2, a=2)
        paired = roped[:, 0:AW].rearrange("p (i s a z c) -> p s i a z c", s=2, a=2, z=2, c=HD // 4)
        keys = roped[:, AW:AW + KW].rearrange("p (s a z c) -> p s a z c", a=2, z=2, c=HD // 4)
        for a in range(2):
            angle = lambda f: table[:, f, a, :].rearrange("p (o c) -> p o c", o=1).broadcast_to(
                [P, n_heads, HD // 4])
            lo, hi = parts(qk)[:, :, a, 0, :], parts(qk)[:, :, a, 1, :]
            t1, t2 = flat(r1)[:, :, a, :], flat(r2)[:, :, a, :]
            queries = lambda ap: ap[:, 0:QH, :].rearrange("p (s i) c -> p s i c", s=2)
            for z, first, second, op in ((0, lo, hi, ALU.subtract), (1, hi, lo, ALU.add)):
                dve.run(lambda e: e.tensor_tensor(t1, first, angle(0), ALU.mult))
                dve.run(lambda e: e.tensor_tensor(t2, second, angle(1), ALU.mult))
                dve.run(lambda e: e.tensor_tensor(paired[:, :, :, a, z, :], queries(t1), queries(t2), op), roped_free)
                ready = dve.run(lambda e: e.tensor_tensor(keys[:, :, a, z, :], t1[:, QH:, :], t2[:, QH:, :], op))
        core.claim(4, 2)
        turned = core.turns([(core.bank(4, T)[:, i * P:(i + 1) * P], roped[:, i * P:(i + 1) * P]) for i in range(5)],
                            ready)
        roped_free = turned
        core.qk_ok = act.run(lambda e: e.activation(core.qkT[:, :, tok], core.bank(4, 5 * P).rearrange(
            "p (i t) -> p i t", i=5), ACT.Copy), turned, w_ok)
        core.freed(4, 2, core.qk_ok)


def lru_rates(core):
    dve, act = core.dve, core.act
    lam = core.small[:, 0:8]
    rate, minus, z, s, s2 = (core.small[:, 8 * n:8 * n + 8] for n in (1, 2, 3, 4, 5))
    for d, name in enumerate(("lam_f", "lam_b")):
        dve.run(lambda e: e.tensor_copy(lam[:, 4 * d:4 * d + 4], core.col(name, 0, 4)))
    ev = dve.run(lambda e: e.tensor_scalar(z, lam, -1.0, None, ALU.mult))
    ev = dve.run(lambda e: e.tensor_tensor(z, z, lam, ALU.max))
    ev = act.run(lambda e: e.activation(z, z, ACT.Exp, scale=-1.0), ev)
    dve.run(lambda e: e.tensor_scalar(s, z, 2.0, None, ALU.add), ev)
    dve.run(lambda e: e.reciprocal(s, s))
    dve.run(lambda e: e.tensor_tensor(s, s, z, ALU.mult))
    dve.run(lambda e: e.tensor_tensor(s2, s, s, ALU.mult))
    dve.run(lambda e: e.memset(z, 1.0 / 19))
    for n in range(17, 0, -2):
        dve.run(lambda e: e.tensor_tensor(z, z, s2, ALU.mult))
        dve.run(lambda e: e.tensor_scalar(z, z, 1.0 / n, None, ALU.add))
    dve.run(lambda e: e.tensor_tensor(z, z, s, ALU.mult))
    dve.run(lambda e: e.tensor_scalar(z, z, 2.0, None, ALU.mult))
    dve.run(lambda e: e.tensor_scalar(rate, lam, 0.0, None, ALU.min))
    dve.run(lambda e: e.tensor_tensor(rate, rate, z, ALU.subtract))
    dve.run(lambda e: e.tensor_scalar(rate, rate, LRU_C, None, ALU.mult))
    core.rates_ok = dve.run(lambda e: e.tensor_scalar(minus, rate, -1.0, None, ALU.mult))
    core.rate, core.minus_rate = rate, minus


def lru(core):
    pe, dve, act, pool = core.pe, core.dve, core.act, core.pool
    core.stage("lru")
    gone = core.everything()
    weights = SplitRing(core, core.lru_ring, [core.split(f"lru_w{i}", LRU_W + 2048 * i, 1024) for i in range(4)],
                        [(act, pool)], 2 * LT, gone)
    tile = lambda n: core.view(LRU_TMP + T * n, T)
    xc_of, yr_of = [tile(0), tile(1)], [tile(2), tile(3)]
    a, tanh, b, h = (tile(n) for n in (4, 5, 6, 7))
    core.lru_out = core.view(LRU_OUT, LT * T).rearrange("p (c t) -> p c t", c=LT)
    xc_free, yr_free, xc_ok, yr_ok = [gone] * 2, [gone] * 2, [None] * 2, [None] * 2

    def project(c):
        i = c % 2
        for pair in (0, 2):
            w, ready = weights.take()
            w = w.rearrange("p (k n) -> p k n", k=DT)
            core.claim(pair, 2)
            pe.after(ready, core.h1_ok)
            for half in range(2):
                mm = core.products(core.bank(pair + half), [(w[:, k, :], core.h1T[:, k, half * BANK:(half + 1) * BANK])
                                                            for k in range(DT)])
            mm = pe.mark(mm)
            weights.release(mm)
            if pair == 0:
                xc, x = xc_of[i], core.bank(0, T)
                tap = lambda n: core.col("lru_conv_w", 4 * n + c)
                ev = act.run(lambda e: e.activation(xc, x, ACT.Identity, bias=core.col("lru_conv_b", c), scale=tap(2)),
                             mm, xc_free[i])
                for n, shift in ((0, 2), (1, 1)):
                    dve.run(lambda e: e.scalar_tensor_tensor(out=xc[:, shift:T], in0=x[:, 0:T - shift], scalar=tap(n),
                                                             in1=xc[:, shift:T], op0=ALU.mult, op1=ALU.add), ev)
                xc_ok[i] = dve.run(lambda e: e.scalar_tensor_tensor(
                    out=xc[:, 0:T - 1], in0=x[:, 1:T], scalar=tap(3), in1=xc[:, 0:T - 1], op0=ALU.mult, op1=ALU.add))
                core.freed(0, 2, xc_ok[i])
            else:
                yr_ok[i] = act.run(lambda e: e.activation(yr_of[i], core.bank(2, T), ACT.Gelu_apprx_tanh), mm,
                                   yr_free[i])
                core.freed(2, 2, yr_ok[i])

    def recur(c):
        i = c % 2
        xc, out = xc_of[i], core.lru_out[:, c, :]
        for d in range(2):
            for n, pair in ((0, 4), (1, 6)):
                core.claim(pair, 2)
                pe.after(xc_ok[i], core.blocks_in)
                for half in range(2):
                    mm = pe.engine.matmul(core.bank(pair + half), core.blocks[:, 2 * d + n, c, :],
                                          xc[:, half * BANK:(half + 1) * BANK], start=True, stop=True)
                gate = pe.mark(mm)
                bias = core.col(("ba_", "bx_")[n] + "fb"[d], c)
                ev = act.run(lambda e: e.activation((tanh, b)[n], core.bank(pair, T), ACT.Sigmoid, bias=bias), gate,
                             dve.latest)
                core.freed(pair, 2, ev)
            at = 4 * d + c
            act.run(lambda e: e.activation(a, tanh, ACT.Exp, scale=core.rate[:, at:at + 1]), core.rates_ok)
            ev = act.run(lambda e: e.activation(tanh, tanh, ACT.Tanh, scale=core.minus_rate[:, at:at + 1]))
            dve.run(lambda e: e.tensor_tensor(b, b, xc, ALU.mult), ev)
            dve.run(lambda e: e.tensor_tensor(h, a, a, ALU.mult))
            ev = dve.run(lambda e: e.scalar_tensor_tensor(out=tanh, in0=h, scalar=1.0, in1=tanh, op0=ALU.add,
                                                          op1=ALU.mult))
            act.run(lambda e: e.activation(tanh, tanh, ACT.Sqrt), ev)
            first = 0 if d == 0 else T - 1
            dve.run(lambda e: e.memset(tanh[:, first:first + 1], 1.0), act.latest)
            dve.run(lambda e: e.tensor_tensor(b, b, tanh, ALU.mult))
            if d == 0:
                dve.run(lambda e: e.tensor_tensor_scan(out, a, b, 0.0, ALU.mult, ALU.add), gone)
            else:
                dve.run(lambda e: e.tensor_tensor_scan(h[:, ::-1], a[:, ::-1], b[:, ::-1], 0.0, ALU.mult, ALU.add))
        dve.run(lambda e: e.tensor_tensor(out, out, h, ALU.add))
        core.lru_ok = yr_free[i] = dve.run(lambda e: e.tensor_tensor(out, out, yr_of[i], ALU.mult), yr_ok[i])
        xc_free[i] = [core.lru_ok, pe.latest]

    lru_rates(core)
    project(0)
    for c in range(LT):
        if c + 1 < LT:
            project(c + 1)
        recur(c)


def attention(core):
    pe, dve, act = core.pe, core.dve, core.act
    core.stage("attention")
    gone = core.everything()
    prob = [core.view(PROB + T * i, T) for i in range(2)]
    probT = [core.view(PROBT + T * i, T).rearrange("p (k q) -> p k q", k=TT) for i in range(2)]
    o = core.view(OATT, TT * AW).rearrange("p (t n) -> p t n", t=TT)
    units = [(t, h) for t in range(TT) for h in range(QH)]
    core.lruT = core.split_tiles("lruT", LRUT, LT, T)
    for c in range(LT):
        core.lru_ok = core.cut(core.lruT[c], core.lru_out[:, c, :], act, core.pool, gone)
    w_out = core.ins["w_out_2"][0]
    core.w_out_in = [Transfers(core.nc, f"dma_w_out2_{r}").start(
        core.sp, tiled(core.view(WOUT_F + 2048 * r, 2048), 2),
        w_out[r * 2 * P:(r + 1) * 2 * P, :].rearrange("(k p) n -> p k n", p=P), gone) for r in range(4)]
    peak = [core.small[:, 48 + i:49 + i] for i in range(2)]
    total = [core.small[:, 50 + i:51 + i] for i in range(4)]
    prob_free, probT_free, exp_ok, probT_ok = [gone] * 2, [gone] * 2, [None] * 2, [None] * 2

    def scores(n):
        t, h = units[n]
        i, lo = n % 2, HD * (h // 4)
        tile = h % 4
        core.claim(2 * i, 2)
        pe.after(core.qk_ok)
        for half in range(2):
            mm = pe.engine.matmul(core.bank(2 * i + half), core.qkT[lo:lo + HD, tile, t * P:(t + 1) * P],
                                  core.qkT[lo:lo + HD, 4, half * BANK:(half + 1) * BANK], start=True, stop=True)
        ev = pe.mark(mm)
        dve.run(lambda e: e.tensor_reduce(peak[i], core.bank(2 * i, T), AX.X, ALU.max), ev, exp_ok[i])
        ev = dve.run(lambda e: e.tensor_scalar(peak[i], peak[i], -1.0, None, ALU.mult))
        exp_ok[i] = act.run(lambda e: e.activation(prob[i], core.bank(2 * i, T), ACT.Exp, bias=peak[i],
                                                   accum_out=total[n % 4]), ev, prob_free[i])
        core.freed(2 * i, 2, exp_ok[i])

    def turn(n):
        i = n % 2
        core.claim(4, 2)
        turned = core.turns([(core.bank(4, T)[:, k * P:(k + 1) * P], prob[i][:, k * P:(k + 1) * P])
                             for k in range(TT)], exp_ok[i])
        prob_free[i] = turned
        half = lambda k: core.view(PROBT + T * i + BANK * k, BANK)
        a = act.run(lambda e: e.activation(half(0), core.bank(4), ACT.Copy), turned, probT_free[i])
        b = dve.run(lambda e: e.tensor_copy(half(1), core.bank(5)), turned, probT_free[i])
        core.freed(4, 1, a)
        core.freed(5, 1, b)
        probT_ok[i] = [a, b]

    def mix(n):
        t, h = units[n]
        i, g = n % 2, h // 4
        b = 6 + i
        core.claim(b)
        pe.after(probT_ok[i])
        for k in range(TT):
            mm = pe.engine.matmul(core.bank(b, HD), probT[i][:, k, :], core.vb[:, k, g * HD:(g + 1) * HD],
                                  start=(k == 0), stop=(k == TT - 1))
        ev = probT_free[i] = pe.mark(mm)
        dve.run(lambda e: e.reciprocal(total[n % 4], total[n % 4]), exp_ok[i])
        core.o_ok = dve.run(lambda e: e.tensor_scalar(o[:, t, h * HD:(h + 1) * HD], core.bank(b, HD), total[n % 4],
                                                      None, ALU.mult), ev)
        core.freed(b, 1, core.o_ok)

    scores(0)
    for n in range(len(units)):
        if n + 1 < len(units):
            scores(n + 1)
        if n:
            mix(n - 1)
        turn(n)
    mix(len(units) - 1)
    core.attT = core.split("attT", ATT, 4 * T).rearrange("p (j t) -> p j t", j=4)
    for j in range(4):
        b = 2 * (j % 2)
        core.claim(b, 2)
        turned = core.turns([(core.bank(b, T)[:, t * P:(t + 1) * P], o[:, t, j * P:(j + 1) * P]) for t in range(TT)],
                            core.o_ok)
        core.att_ok = core.cut(core.attT[:, j, :], core.bank(b, T), act, dve, turned)
        core.freed(b, 2, core.att_ok)


def second_out(core):
    nc, pe, dve, act, pool, sp = core.nc, core.pe, core.dve, core.act, core.pool, core.sp
    core.stage("second_out")
    gone = core.everything()
    w = [part.rearrange("p (k n) -> p k n", k=2) for part in core.split_tiles("w_out_2_", WOUT_P, 4, 2 * D)]
    w_ok = []
    for r in range(4):
        w_ok.append(core.cut(w[r], tiled(core.view(WOUT_F + 2048 * r, 2048), 2), act,
                             dve, core.w_out_in[r], gone))
    xn3 = core.view(XN3, TT * D).rearrange("p (t d) -> p t d", t=TT)
    core.x3 = core.view(X3, TT * D).rearrange("p (t d) -> p t d", t=TT)
    landed = [Transfers(nc, f"dma_xb{r}").start(sp, core.x3[:, 2 * r:2 * r + 2, :], core.xb_dram[
        r * 2 * P:(r + 1) * 2 * P, :].rearrange("(t p) d -> p t d", p=P), w_ok[r], core.xb_stored.done())
        for r in range(4)]
    sums = core.small[:, 56:64]
    for t in range(TT):
        tok = slice(t * P, (t + 1) * P)
        xt, xn = core.x3[:, t, :], xn3[:, t, :]
        src = lambda k: core.attT[:, k, tok] if k < 4 else core.lruT[k - 4][:, tok]
        pe.after(core.att_ok, core.lru_ok)
        b = 2 * (t % 4)
        core.claim(b, 2)
        mms = []
        order = range(DT)
        for half in range(2):
            cols = slice(half * BANK, (half + 1) * BANK)
            for k in order:
                pe.after(w_ok[k // 2])
                mm = core.products(core.bank(b + half), [(src(k), w[k // 2][:, k % 2, cols])], first=(k == 0), last=(k == DT - 1))
            mm = pe.mark(mm)
            ev = dve.run(lambda e: e.tensor_tensor(xt[:, cols], xt[:, cols], core.bank(b + half), ALU.add), mm,
                         landed[t // 2])
            core.freed(b + half, 1, ev)
        sq = act.run(lambda e: e.activation(xn, xt, ACT.Square, accum_out=sums[:, t:t + 1]), ev, gone)
        ev = row_scale(core, sums[:, t:t + 1], D, sq)
        ready = dve.run(lambda e: e.tensor_scalar(xn, xt, sums[:, t:t + 1], None, ALU.mult), ev)
    core.h3T = core.split("h3T", H3, DT * T).rearrange("p (j t) -> p j t", j=DT)
    mixed = pe.latest
    for j in range(DT):
        core.h3_ok = turn_and_cut(core, xn3, j, 2 * (j % 4), core.h3T[:, j, :], core.col("norm2", j), ready, mixed)


def ffn_loads(ins):
    up, down = ins["w_up_2"][0], ins["w_down_2"][0]
    loads = []
    for g in range(0, FT, FGROUP):
        for f in range(g, g + FGROUP):
            loads += [feature_tile(up, f * P), feature_tile(up, DFF + f * P)]
        for half in range(2):
            for k in range(g, g + FGROUP, 2):
                loads.append(feature_tile(down[k * P:(k + 2) * P, :], half * BANK, BANK))
    return loads


def ffn(core, ins, out):
    nc, pe, dve, act, pool, sp = core.nc, core.pe, core.dve, core.act, core.pool, core.sp
    core.stage("ffn")
    turned = pe.latest
    ring = Ring(nc, sp, "dma_ffn", [core.view(UP_RING + 1024 * i, 1024) for i in range(3)], ffn_loads(ins),
                [turned] * 3)
    parts = [core.split(f"ffn_w{i}", UP_PARTS + 2048 * i, 1024) for i in range(2)]
    weights = SplitRing(core, ring, parts, [(act, dve)], len(ring.loads), turned)
    actT = core.split_tiles("actT", ACTT, FGROUP, T)
    conv = [core.view(at, T) for at in CONV]
    conv_free = [core.everything()] * 3
    act_free = turned
    used = 0
    sums = core.small[:, 64:72]
    dma_out = [Transfers(nc, f"dma_out{i}") for i in range(2)]
    g_row = core.view(G_ROW, D)
    y = [core.view(G_ROW + D * (i + 1), D) for i in range(2)]
    for g in range(0, FT, FGROUP):
        for f in range(g, g + FGROUP):
            made = []
            for n in range(2):
                i, pair = used % 3, 2 * (used % 4)
                used += 1
                w, ready = weights.take()
                w = w.rearrange("p (k n) -> p k n", k=DT)
                core.claim(pair, 2)
                pe.after(ready, core.h3_ok)
                for half in range(2):
                    mm = core.products(core.bank(pair + half), [(w[:, k, :], core.h3T[:, k, half * BANK:(half + 1) * BANK])
                                                                for k in range(DT)])
                mm = pe.mark(mm)
                weights.release(mm)
                u, c, at = core.bank(pair, T), conv[i], n * FT + f
                ev = act.run(lambda e: e.activation(c, u, ACT.Identity, bias=core.col("up_conv_b", at),
                                                    scale=core.col("up_conv_w01", 2 * FT + at)), mm, conv_free[i])
                dve.run(lambda e: e.scalar_tensor_tensor(out=c[:, 1:T], in0=u[:, 0:T - 1],
                                                         scalar=core.col("up_conv_w01", at), in1=c[:, 1:T],
                                                         op0=ALU.mult, op1=ALU.add), ev)
                ev = dve.run(lambda e: e.scalar_tensor_tensor(out=c[:, 0:T - 1], in0=u[:, 1:T],
                                                              scalar=core.col("up_conv_w2", at), in1=c[:, 0:T - 1],
                                                              op0=ALU.mult, op1=ALU.add))
                core.freed(pair, 2, ev)
                if n == 0:
                    ev = act.run(lambda e: e.activation(c, c, ACT.Gelu_apprx_tanh), ev)
                made.append((ev, i))
            (gate_ok, gi), (value_ok, vi) = made
            ev = dve.run(lambda e: e.tensor_tensor(conv[vi], conv[gi], conv[vi], ALU.mult), gate_ok, value_ok)
            act_ok = core.cut(actT[f - g], conv[vi], act, pool, ev, act_free)
            conv_free[gi], conv_free[vi] = ev, act_ok
        last_group = g + FGROUP == FT
        if last_group:
            rows_in = Transfers(nc, "dma_final_row").start(sp, g_row, ins["final_g_2"].partition_broadcast(P), mm)
            y_free = [mm] * 2
        for half in range(2):
            cols = slice(half * BANK, (half + 1) * BANK)
            ends = [None] * TT
            for kk in range(FGROUP // 2):
                w, ready = weights.take()
                w = w.rearrange("p (k n) -> p k n", k=2)
                pe.after(ready, act_ok)
                last = kk == FGROUP // 2 - 1
                for t in range(TT):
                    if kk == 0:
                        core.claim(t)
                    mm = core.products(core.bank(t), [(actT[2 * kk + k][:, t * P:(t + 1) * P], w[:, k, :])
                                                      for k in range(2)], first=(kk == 0), last=last)
                    if last:
                        ends[t] = pe.mark(mm)
                if not last:
                    pe.mark(mm)
                weights.release(pe.latest)
            act_free = pe.latest
            for t in range(TT):
                xt = core.x3[:, t, :]
                ev = dve.run(lambda e: e.tensor_tensor(xt[:, cols], xt[:, cols], core.bank(t), ALU.add), ends[t])
                core.freed(t, 1, ev)
                if half and last_group:
                    yt = y[t % 2]
                    sq = act.run(lambda e: e.activation(yt, xt, ACT.Square, accum_out=sums[:, t:t + 1]), ev,
                                 y_free[t % 2])
                    row_scale(core, sums[:, t:t + 1], D, sq)
                    ev = dve.run(lambda e: e.scalar_tensor_tensor(out=yt, in0=xt, scalar=sums[:, t:t + 1],
                                                                  in1=g_row, op0=ALU.mult, op1=ALU.mult), rows_in)
                    y_free[t % 2] = dma_out[t % 2].start(sp, out[0, t * P:(t + 1) * P, :], yt, ev)
    sp.after(y_free)


def build_block_pair(nc, ins, out, upto=99):
    core = Core(nc)
    core.gate_free = None
    core.ins = ins
    start(core, ins)
    if upto <= 1:
        return core
    core.stage("values")
    values(core)
    hgrn(core)
    if upto <= 2:
        return core
    core.u_ok = core.act.latest
    core.gate_free = core.raw_free[0]
    core.stage("sgu")
    for part in [sgu_values(core)] + [ada_chunk(core, core.wide, c, 4 + c % 2) for c in range(4, 12)] + [
            hgrn_gates(core)]:
        for _ in part:
            pass
    merge(core, ins)
    core.stage("out")
    w_out = core.view(WOUT, DT * D).rearrange("p (k n) -> p k n", k=DT)
    w_out_ok = Transfers(nc, "dma_w_out").start(core.sp, w_out, ins["w_out"][0].rearrange("(k p) n -> p k n", p=P),
                                                core.everything())
    gain_rows(core, ins)
    core.expert = Ring(nc, core.sp, "dma_expert", [core.view(at, 2048) for at in STAGED], expert_loads(ins),
                       [core.everything()] * 8)
    router = core.view(TOPK + 544, DT * NE).rearrange("p (k e) -> p k e", k=DT)
    router_ok = Transfers(nc, "dma_router").start(core.sp, router,
                                                  ins["router_w"][0].rearrange("(k p) e -> p k e", p=P))
    project_out(core, ins, w_out_ok, w_out)
    if upto <= 3:
        core.sp.after(core.x_stored, core.xn_stored.done())
        return core
    route(core, ins, router, router_ok)
    if upto <= 4:
        return core
    experts(core, ins)
    if upto <= 5:
        core.sp.after(core.scattered)
        return core
    second_start(core, ins)
    second_heads(core, ins)
    if upto <= 6:
        return core
    lru(core)
    if upto <= 7:
        return core
    attention(core)
    gone = core.everything()
    if upto <= 8:
        return core
    second_out(core)
    if upto <= 9:
        return core
    ffn(core, ins, out)
    return core


def kernel(**inputs):
    import concourse.bacc as bacc
    from concourse.bass_utils import run_bass_kernel_spmd

    nc = bacc.Bacc("TRN2", target_bir_lowering=False, num_devices=1)
    arrays, ins = {}, {}
    for name, a in list(inputs.items()) + list(shape_constants().items()):
        a = np.ascontiguousarray(a)
        arrays[f"in_{name}"] = a
        ins[name] = nc.dram_tensor(f"in_{name}", a.shape, mybir.dt.from_np(a.dtype), kind="ExternalInput").ap()
    out = nc.dram_tensor("out", (1, T, D), F32, kind="ExternalOutput").ap()
    build_block_pair(nc, ins, out)
    r = run_bass_kernel_spmd(nc, [arrays], core_ids=[0])
    return r.results[0]["out"]
```

```python
import numpy as np

import concourse.bass as bass
from concourse import mybir

F32 = mybir.dt.float32
F32R = mybir.dt.float32r
U32 = mybir.dt.uint32
U8 = mybir.dt.uint8
ALU = mybir.AluOpType
ACT = mybir.ActivationFunctionType
AX = mybir.AxisListType

P = 128
D = 1024
T = 1024
DT = D // P
TT = T // P
BANK = 512
EPS = 1e-6

CTX = 256
HEADS = 4
WIDTH = 512
CHUNK = 128
LEVELS = [1, 2, 4, 8, 16, 32, 64]
NCH = T // CHUNK
GROUPS = 4
COL_Q, COL_FF, COL_FB, COL_V, COL_G, COL_U, COL_SV = (i * WIDTH for i in range(7))
COL_GA, COL_GB = 7 * WIDTH, 7 * WIDTH + D

NE = 16
CAP = 2 * T // NE
FF = 2048
ARENA = 51660
NEG = -1.0

QH, KVH, HD = 8, 2, 64
AW = QH * HD
KW = KVH * HD
LW = D - AW
LT = LW // P
CC_XR = AW + 2 * KW
CC_YR = CC_XR + LW
DFF = 3 * D
FT = DFF // P
LRU_C = 8.0


class Lane:

    def __init__(self, nc, engine, name, in_turn):
        self.nc, self.engine, self.name, self.in_turn = nc, engine, name, in_turn
        self.seen = {}
        self.sem, self.count, self.latest = None, 0, None

    def stage(self, name):
        self.label = f"{self.name}_{name}"
        self.sem, self.count = self.nc.alloc_semaphore(self.label), 0

    def after(self, *events):
        for event in events:
            if event is None:
                continue
            if isinstance(event, list):
                self.after(*event)
                continue
            sem, value, name = event
            if value > self.seen.get(name, 0):
                self.engine.wait_ge(sem, value)
                self.seen[name] = value
        return self.engine

    def mark(self, instruction):
        self.count += 1
        instruction.then_inc(self.sem, 1)
        self.latest = (self.sem, self.count, self.label)
        return self.latest

    def run(self, issue, *events):
        self.after(*events)
        if self.in_turn:
            self.after(self.latest)
        return self.mark(issue(self.engine))


class Transfers:

    def __init__(self, nc, name):
        self.sem, self.count, self.name = nc.alloc_semaphore(name), 0, name

    def start(self, lane, out, in_, *events):
        lane.after(*events).dma_start(out, in_).then_inc(self.sem, 16)
        self.count += 16
        return self.done()

    def done(self):
        return (self.sem, self.count, self.name)


class Ring:

    def __init__(self, nc, lane, name, slots, loads, free):
        self.lane, self.slots, self.loads = lane, slots, loads
        self.transfers = [Transfers(nc, f"{name}{i}") for i in range(len(slots))]
        self.issued = self.taken = 0
        for i in range(min(len(free), len(loads))):
            self.load(free[i])

    def load(self, *events):
        if self.issued < len(self.loads):
            i = self.issued % len(self.slots)
            out, in_ = self.loads[self.issued](self.slots[i])
            self.issued += 1
            self.transfers[i].start(self.lane, out, in_, *events)

    def take(self):
        assert self.taken < self.issued
        i = self.taken % len(self.slots)
        self.taken += 1
        return self.slots[i], self.transfers[i].done()

    def release(self, event):
        self.load(event)


class Core:

    def __init__(self, nc):
        self.nc = nc
        self.pe = Lane(nc, nc.tensor, "pe", False)
        self.dve = Lane(nc, nc.vector, "dve", True)
        self.act = Lane(nc, nc.scalar, "act", True)
        self.pool = Lane(nc, nc.gpsimd, "pool", True)
        self.sp = Lane(nc, nc.sync, "sp", False)
        self.ident = self.sb("ident", P)
        self.ones = self.sb("ones", P)
        self.masks = self.sb("masks", 15 * P, U8)
        self.vec = self.sb("vec", 4 * P)
        self.mod = self.sb("mod", 96)
        self.small = self.sb("small", 192)
        self.arena_at = nc.sbuf_base
        self.arena = self.sb("arena", ARENA)
        self.psum = nc.alloc_psum_tensor("psum", [P, 8 * BANK], F32)
        self.bank_free = [None] * 8
        self.where = {}

    def sb(self, name, n, dt=F32):
        return self.nc.alloc_sbuf_tensor(name, [P, n], dt)

    def stage(self, name):
        for lane in (self.pe, self.dve, self.act, self.pool):
            lane.stage(name)

    def everything(self):
        return [lane.latest for lane in (self.pe, self.dve, self.act, self.pool)]

    def view(self, at, n):
        assert at + n <= ARENA, (at, n)
        return self.arena[:, at:at + n]

    def rounded(self, name, at, n):
        assert at + n <= ARENA, (at, n)
        return self.nc.alloc_sbuf_tensor_at(name, [P, n], F32R, offset=self.arena_at + 4 * at)[:, :]

    def split(self, name, at, n, apart=None):
        return Parts(self.rounded(f"{name}_high", at, n),
                     self.rounded(f"{name}_low", at + n if apart is None else apart, n))

    def split_tiles(self, name, at, count, n):
        return [self.split(f"{name}{i}", at + i * n, n, apart=at + (count + i) * n) for i in range(count)]

    def cut(self, parts, value, high_lane, low_lane, *events):
        if high_lane is self.act:
            high = self.act.run(lambda e: e.activation(parts.high, value, ACT.Copy), *events)
        else:
            high = high_lane.run(lambda e: e.tensor_copy(parts.high, value), *events)
        low = low_lane.run(lambda e: e.tensor_tensor(parts.low, value, parts.high.bitcast(F32), ALU.subtract), high)
        return [high, low]

    def bank(self, b, n=BANK):
        return self.psum[:, b * BANK:b * BANK + n]

    def col(self, name, i=0, n=1):
        return self.vec[:, self.where[name] + i:self.where[name] + i + n]

    def claim(self, b, n=1):
        self.pe.after(*self.bank_free[b:b + n])

    def freed(self, b, n, event):
        for i in range(b, b + n):
            self.bank_free[i] = event
        return event

    def matmuls(self, out, pairs, *events):
        self.pe.after(*events)
        for n, (lhsT, rhs) in enumerate(pairs):
            mm = self.pe.engine.matmul(out, lhsT, rhs, start=(n == 0), stop=(n == len(pairs) - 1))
        return self.pe.mark(mm)

    def products(self, out, pairs, first=True, last=True):
        for n, (a, b) in enumerate(pairs):
            for m, (x, y) in enumerate(((a.high, b.high), (a.low, b.high), (a.high, b.low))):
                mm = self.pe.engine.matmul(out, x, y, start=(first and n == 0 and m == 0),
                                           stop=(last and n == len(pairs) - 1 and m == 2))
        return mm

    def turns(self, outs_ins, *events):
        self.pe.after(*events)
        for out, in_ in outs_ins:
            tr = self.pe.engine.transpose(out, in_, self.ident[0:in_.shape[0], 0:in_.shape[0]])
        return self.pe.mark(tr)


class Parts:

    def __init__(self, high, low):
        self.high, self.low = high, low

    def __getitem__(self, at):
        return Parts(self.high[at], self.low[at])

    def rearrange(self, pattern, **sizes):
        return Parts(self.high.rearrange(pattern, **sizes), self.low.rearrange(pattern, **sizes))


class SplitRing:

    def __init__(self, core, ring, parts, lanes, limit, free):
        self.core, self.ring, self.parts, self.lanes, self.limit = core, ring, parts, lanes, limit
        self.cuts, self.ready, self.taken = 0, [None] * len(parts), 0
        for _ in range(len(parts)):
            self.prepare(free)

    def prepare(self, *free):
        if self.cuts < self.limit:
            i = self.cuts % len(self.parts)
            high_lane, low_lane = self.lanes[self.cuts % len(self.lanes)]
            slot, landed = self.ring.take()
            n = self.parts[i].high.shape[1]
            self.ready[i] = self.core.cut(self.parts[i], slot[:, 0:n], high_lane, low_lane, landed, *free)
            self.ring.release(self.ready[i])
            self.cuts += 1

    def take(self):
        i = self.taken % len(self.parts)
        self.taken += 1
        return self.parts[i], self.ready[i]

    def release(self, event):
        self.prepare(event)


def tiled(slot, k):
    return slot.rearrange("p (k n) -> p k n", k=k)


def feature_tile(w, at, width=P):
    k = w.shape[0] // P
    src = w.rearrange("(k p) n -> p k n", p=P)[:, :, at:at + width]
    return lambda slot: (tiled(slot[:, 0:k * width], k), src)


def shape_constants():
    j, i = np.meshgrid(np.arange(P), np.arange(P), indexing="ij")
    masks = [j == i]
    for h in LEVELS:
        same = j // (2 * h) == i // (2 * h)
        masks.append(same & (j // h % 2 == 0) & (i // h % 2 == 1))
    for h in LEVELS:
        same = j // (2 * h) == i // (2 * h)
        masks.append(same & (j // h % 2 == 1) & (i // h % 2 == 0))
    masks = np.stack(masks, 1).astype(np.float32).reshape(P, -1)
    quarter = HD // 4
    inverse = (np.float32(1.0) / np.float32(10000.0) ** (np.arange(0, HD // 2, 2, dtype=np.float32)
                                                         / np.float32(HD // 2))).astype(np.float32)
    token = np.arange(T)
    angles = np.stack([(token // 64).astype(np.float32)[:, None] * inverse,
                       (token % 64).astype(np.float32)[:, None] * inverse], 1).astype(np.float32)
    rope = np.stack([np.cos(angles), np.sin(angles)], 1).astype(np.float32)
    rope = rope.reshape(TT, P, 4 * quarter).transpose(1, 0, 2).reshape(P, -1)
    return {
        "identity": np.eye(P, dtype=np.float32),
        "pair_masks": masks,
        "rope_table": np.ascontiguousarray(rope),
    }


def row_scale(core, sums, n, *events):
    a = core.dve.run(lambda e: e.tensor_scalar(sums, sums, 1.0 / n, EPS, ALU.mult, ALU.add), *events)
    b = core.act.run(lambda e: e.activation(sums, sums, ACT.Sqrt), a)
    return core.dve.run(lambda e: e.reciprocal(sums, sums), b)


def norm_rows(core, tok, n_tiles, sums, junk, landed):
    for t in range(n_tiles):
        ev = core.act.run(lambda e: e.activation(junk, tok[:, t, :], ACT.Square, accum_out=sums[:, t:t + 1]),
                          landed[t])
    ready = row_scale(core, sums, D, ev)
    return [core.dve.run(lambda e: e.tensor_scalar(tok[:, t, :], tok[:, t, :], sums[:, t:t + 1], None, ALU.mult),
                         ready) for t in range(n_tiles)]


def turn_and_modulate(core, tok, n_tiles, j, b, out, scale, shift, *events):
    core.claim(b, 2)
    turned = core.turns([(core.bank(b, D)[:, t * P:(t + 1) * P], tok[:, t, j * P:(j + 1) * P])
                         for t in range(n_tiles)], *events)
    ev = core.act.run(lambda e: e.activation(out, core.bank(b, n_tiles * P), ACT.Identity, bias=shift, scale=scale),
                      turned)
    return core.freed(b, 2, ev)


def turn_and_cut(core, tok, j, b, out, scale, *events, scales=None):
    core.claim(b, 2)
    core.pe.after(*events)
    for t in range(TT):
        part, rows = core.bank(b, T)[:, t * P:(t + 1) * P], tok[:, t, j * P:(j + 1) * P]
        if scales is None:
            turn = core.pe.engine.transpose(part, rows, core.ident[:, :])
        else:
            turn = core.pe.engine.matmul(part, rows, scales[:, t, :], start=True, stop=True)
    turned = core.pe.mark(turn)
    ev = core.act.run(lambda e: e.activation(out.high, core.bank(b, T), ACT.Copy, scale=scale), turned)
    ev = core.dve.run(lambda e: e.scalar_tensor_tensor(out=out.low, in0=core.bank(b, T), scalar=scale,
                                                       in1=out.high.bitcast(F32), op0=ALU.mult, op1=ALU.subtract), ev)
    return core.freed(b, 2, ev)


HT, RING_A, WIDE, OT, YB = 0, 8192, 16384, 20480, 24576
VV, RAW, UNIT, KRT, SALL, VCTX = 28672, 32768, 39936, 46080, 47104, 48128
BSB, WST, S0, KC = 49152, 49664, 50176, 50432
MERGE_PARTS, MERGE_RING, MERGE_TMP, OT_HIGH, UT_HIGH, HT_HIGH, MERGED = (
    RING_A, RING_A + 4096, (RING_A + 7168, 49152), WIDE, VV, RAW, 40960)
WOUT, GM_ROW, XT = OT_HIGH, YB + 2048, YB
ADA_REST = [34816 + 4096 * i for i in range(3)]


def start(core, ins):
    nc, dve, act, sp = core.nc, core.dve, core.act, core.sp
    core.stage("start")
    rows = core.view(38912, 4 * P).rearrange("p (n c) -> p n c", n=4)
    cleared = dve.run(lambda e: e.memset(core.view(38912, 4 * P), 0.0))
    dve.run(lambda e: e.memset(core.ones[:, :], 1.0))
    core.eps = core.small[:, 184:185]
    dve.run(lambda e: e.memset(core.eps, EPS))
    first = Transfers(nc, "dma_constants")
    first.start(sp, core.ident[:, :], ins["identity"])
    masks_f = core.view(RING_A, 15 * P)
    first.start(sp, masks_f, ins["pair_masks"])
    by_rows = lambda name: ins[name].rearrange("a (r p) -> (a r) p", p=P)
    pairs_of_blocks = lambda name: ins[name].rearrange("a (r h) j -> (a r) (h j)", h=2)
    vectors = [
        (0, "c", by_rows("c")), (0, "c_ctx", ins["c_ctx"].rearrange("(r p) -> r p", p=P)),
        (0, "norm_mix", by_rows("norm_mix_w")), (0, "ada_b", by_rows("ada_b")),
        (0, "lb", ins["hgrn_lb_logits"].rearrange("a b (r p) -> (a b r) p", p=P)),
        (0, "hgrn_norm", by_rows("hgrn_norm_w")), (0, "sgu_norm", by_rows("sgu_norm_w")),
        (0, "norm_ffn", by_rows("norm_ffn_w")), (1, "norm1", by_rows("norm1_g_2")),
        (1, "lru_conv_w", ins["lru_conv_w_2"].rearrange("a w (r p) -> (a w r) p", p=P)),
        (1, "lru_conv_b", by_rows("lru_conv_b_2")), (1, "ba_f", pairs_of_blocks("ba_f_2")),
        (1, "bx_f", pairs_of_blocks("bx_f_2")), (1, "ba_b", pairs_of_blocks("ba_b_2")),
        (1, "bx_b", pairs_of_blocks("bx_b_2")), (1, "lam_f", by_rows("lam_f_2")),
        (1, "lam_b", by_rows("lam_b_2")), (1, "norm2", by_rows("norm2_g_2")),
        (1, "up_conv_b", by_rows("up_conv_b_2")),
        (2, "up_conv_w01", ins["up_conv_w_2"][:, 0:2, :].rearrange("a w (r p) -> (a w r) p", p=P)),
        (3, "up_conv_w2", ins["up_conv_w_2"][:, 2:3, :].rearrange("a w (r p) -> (a w r) p", p=P)),
    ]
    used = [0] * 4
    for t, name, src in vectors:
        n = src.shape[0]
        first.start(sp, rows[used[t]:used[t] + n, t, :], src, cleared)
        core.where[name] = t * P + used[t]
        used[t] += n
        assert used[t] <= P
    x_tok = core.view(VV, TT * D).rearrange("p (t d) -> p t d", t=TT)
    ctx_tok = core.view(36864, 2 * D).rearrange("p (t d) -> p t d", t=2)
    w_in = ins["w_in"][0]
    ada_slots = [core.view(at, 4096) for at in (RING_A + 4096, YB, 40960, 45056)]
    ada = Ring(nc, sp, "dma_ada", ada_slots, [feature_tile(ins["ada_w"][0], c * BANK, BANK) for c in range(4)],
               [None] * 4)
    ctx_in = Transfers(nc, "dma_ctx").start(sp, ctx_tok, ins["ctx"].rearrange("a (t p) d -> p (a t) d", p=P))
    x_dram = ins["x"].rearrange("a (t p) d -> p (a t) d", p=P)
    x_in = [Transfers(nc, f"dma_x{i}").start(sp, x_tok[:, 2 * i:2 * i + 2, :], x_dram[:, 2 * i:2 * i + 2, :])
            for i in range(4)]
    core.wide = Ring(nc, sp, "dma_wide", [core.view(WIDE, 4096)],
                     [feature_tile(w_in, COL_V, BANK), feature_tile(w_in, COL_SV, BANK)], [None])
    order = []
    for h in range(HEADS):
        order += [COL_Q + h * P, COL_FF + h * P, COL_FB + h * P]
    order += [COL_U + g * P for g in range(GROUPS)] + [COL_G + h * P for h in range(HEADS)]
    loads = [feature_tile(w_in, at) for at in order]

    turned = core.turns([(core.bank(0)[:, t * P:(t + 1) * P], rows[:, t, :]) for t in range(4)], first.done())
    core.vec_ok = dve.run(lambda e: e.tensor_copy(core.vec[:, :], core.bank(0)), turned)
    core.freed(0, 1, core.vec_ok)
    core.masks_ok = dve.run(lambda e: e.tensor_copy(core.masks[:, :], masks_f))

    silu_c = core.small[:, 0:16].rearrange("p (k s) -> p k s", s=2)
    act.run(lambda e: e.activation(silu_c[:, :, 0], core.col("c", 0, 8), ACT.Silu), core.vec_ok)
    core.silu_ok = act.run(lambda e: e.activation(silu_c[:, :, 1], core.col("c_ctx", 0, 8), ACT.Silu))
    core.silu_c = silu_c
    core.ada_rows_free = None
    core.mod_v = core.mod[:, :].rearrange("p (j s) -> p j s", s=2)

    for c in range(4):
        for _ in ada_chunk(core, ada, c, c % 2):
            pass
    junk = core.view(39424, D)
    ctx_n = norm_rows(core, ctx_tok, 2, core.small[:, 16:18], junk, [ctx_in] * 2)
    x_n = norm_rows(core, x_tok, TT, core.small[:, 24:32], junk, [x_in[t // 2] for t in range(TT)])
    mix_scale = core.small[:, 32:48].rearrange("p (j s) -> p j s", s=2)
    for s in range(2):
        a = dve.run(lambda e: e.tensor_scalar(mix_scale[:, :, s], core.mod_v[:, 8:16, s], 1.0, None, ALU.add))
        ok = dve.run(lambda e: e.tensor_tensor(mix_scale[:, :, s], mix_scale[:, :, s], core.col("norm_mix", 0, 8),
                                               ALU.mult), a)
    core.hT = core.view(HT, DT * T).rearrange("p (j t) -> p j t", j=DT)
    core.hcT = core.view(YB, DT * CTX).rearrange("p (j t) -> p j t", j=DT)
    for j in range(DT):
        turn_and_modulate(core, ctx_tok, 2, j, 2 + 2 * (j % 3), core.hcT[:, j, :],
                                       mix_scale[:, j, 1:2], core.mod_v[:, j, 1:2], ctx_n, ok)
    for j in range(DT):
        core.h_ok = turn_and_modulate(core, x_tok, TT, j, 2 + 2 * (j % 3), core.hT[:, j, :],
                                      mix_scale[:, j, 0:1], core.mod_v[:, j, 0:1], x_n, ok)

    low, e0, e1 = core.small[:, 48:56], core.small[:, 56:64], core.small[:, 64:72]
    core.low, core.span = low, core.small[:, 72:80]
    for d in range(2):
        l0, l1, sl = core.col("lb", 8 * d, 4), core.col("lb", 8 * d + 4, 4), slice(4 * d, 4 * d + 4)
        dve.run(lambda e: e.tensor_tensor(low[:, sl], l0, l1, ALU.max))
        dve.run(lambda e: e.tensor_tensor(e0[:, sl], l0, low[:, sl], ALU.subtract))
        a = dve.run(lambda e: e.tensor_tensor(e1[:, sl], l1, low[:, sl], ALU.subtract))
    b = act.run(lambda e: e.activation(core.small[:, 56:72], core.small[:, 56:72], ACT.Exp), a)
    dve.run(lambda e: e.tensor_tensor(low, e0, e1, ALU.add), b)
    dve.run(lambda e: e.reciprocal(low, low))
    dve.run(lambda e: e.tensor_tensor(low, low, e0, ALU.mult))
    core.low_ok = dve.run(lambda e: e.tensor_scalar(core.span, low, -1.0, 1.0, ALU.mult, ALU.add))

    core.score = [core.view(UNIT + 3072 * d + 2048, NCH * CHUNK) for d in range(2)]
    for d in range(2):
        core.score_free = dve.run(lambda e: e.memset(core.score[d], 0.0), core.pe.latest, act.latest)

    sgu_rows = core.view(UNIT, GROUPS * P).rearrange("p (g s) -> p g s", g=GROUPS)
    core.sgu_wT = core.view(WST, GROUPS * P).rearrange("p (g t) -> p g t", g=GROUPS)
    core.sgu_bias = core.view(BSB, GROUPS * P)
    dma_sgu = Transfers(nc, "dma_sgu")
    dma_sgu.start(sp, sgu_rows, ins["sgu_w"][0].rearrange("g t s -> t g s"), core.everything())
    landed = dma_sgu.start(sp, core.sgu_bias, ins["sgu_b"].rearrange("a g t -> (a g t)").partition_broadcast(P))
    slots = [core.view(RING_A + 1024 * i, 1024) for i in range(8)]
    core.feat = Ring(nc, sp, "dma_feature", slots, loads, [core.masks_ok] * 4 + [core.pe.latest] * 4)
    core.sgu_rows, core.sgu_in = sgu_rows, landed


def turn_spatial(core):
    core.claim(0)
    turned = core.turns([(core.bank(0)[:, g * P:(g + 1) * P], core.sgu_rows[:, g, :]) for g in range(GROUPS)],
                        core.sgu_in)
    core.sgu_ok = core.dve.run(lambda e: e.tensor_copy(core.view(WST, GROUPS * P), core.bank(0)), turned)
    core.freed(0, 1, core.sgu_ok)


def ada_chunk(core, ring, c, b):
    slot, landed = ring.take()
    w = tiled(slot, DT)
    core.pe.after(landed, core.silu_ok)
    core.claim(b)
    for k in range(DT):
        mm = core.pe.engine.matmul(core.bank(b)[0:2, :], core.silu_c[:, k, :], w[:, k, :], start=(k == 0),
                                   stop=(k == DT - 1))
        if k < DT - 1:
            yield
    summed = core.pe.mark(mm)
    ring.release(summed)
    rows = core.view(KC, BANK)[0:2, :]
    ev = core.dve.run(lambda e: e.tensor_copy(rows, core.bank(b)[0:2, :]), summed, core.ada_rows_free)
    yield
    out = core.bank(b, 8).rearrange("p (m s) -> p m s", s=2)
    core.ada_rows_free = turned = core.turns([(out[:, m, :], rows[:, m * P:(m + 1) * P]) for m in range(4)], ev)
    for s in range(2):
        ev = core.dve.run(lambda e: e.tensor_tensor(core.mod_v[:, 4 * c:4 * c + 4, s], out[:, :, s],
                                                    core.col("ada_b", 4 * c, 4), ALU.add), turned)
    core.freed(b, 1, ev)
    core.mod_ok = ev
    yield


def values(core):
    core.v = core.view(VV, TT * WIDTH).rearrange("p (t n) -> p t n", t=TT)
    core.vctx = core.view(VCTX, 2 * WIDTH).rearrange("p (t n) -> p t n", t=2)
    slot, landed = core.wide.take()
    w = tiled(slot, DT)
    x_free = core.everything()
    for t in range(TT + 2):
        src, out = (core.hT, core.v[:, t, :]) if t < TT else (core.hcT, core.vctx[:, t - TT, :])
        at = (t % TT if t < TT else t - TT) * P
        b = t % 4
        core.claim(b)
        mm = core.matmuls(core.bank(b), [(src[:, k, at:at + P], w[:, k, :]) for k in range(DT)], landed,
                          core.h_ok)
        if t % 2:
            ev = core.act.run(lambda e: e.activation(out, core.bank(b), ACT.Copy), mm, x_free)
        else:
            ev = core.dve.run(lambda e: e.tensor_copy(out, core.bank(b)), mm, x_free)
        core.freed(b, 1, ev)
    core.wide.release(mm)
    core.v_ok = [core.act.latest, core.dve.latest]


def feature_halves(core, slot, landed, finish):
    w = tiled(slot, DT)
    for half, b in enumerate((6, 7)):
        core.claim(b)
        core.pe.after(landed)
        for k in range(DT):
            mm = core.pe.engine.matmul(core.bank(b), w[:, k, :], core.hT[:, k, half * BANK:(half + 1) * BANK],
                                       start=(k == 0), stop=(k == DT - 1))
            if k < DT - 1:
                yield
        ev = core.pe.mark(mm)
        core.freed(b, 1, finish(half, b, ev))
        yield


def raw_head(core, h):
    r = RAW + 3584 * (h % 2)
    free = core.raw_free[h % 2]
    q = core.view(r, T)
    slot, landed = core.feat.take()
    yield from feature_halves(core, slot, landed, lambda half, b, ev: core.act.run(
        lambda e: e.activation(q[:, half * BANK:(half + 1) * BANK], core.bank(b), ACT.Silu), ev, free))
    core.feat.release(core.pe.latest)
    core.q_ok[h] = core.act.latest
    for d in range(2):
        f, fc = core.view(r + T * (d + 1), T), core.view(r + 3 * T + CTX * d, CTX)
        slot, landed = core.feat.take()
        w = tiled(slot, DT)
        low, span = core.low[:, 4 * d + h:4 * d + h + 1], core.span[:, 4 * d + h:4 * d + h + 1]

        def gate(out, b, n, ev):
            s = core.act.run(lambda e: e.activation(out, core.bank(b, n), ACT.Sigmoid), ev, free)
            core.f_ok[h] = core.pool.run(lambda e: e.tensor_scalar(out, out, span, low, ALU.mult, ALU.add),
                                         s, core.low_ok)
            return s
        yield from feature_halves(core, slot, landed, lambda half, b, ev: gate(
            f[:, half * BANK:(half + 1) * BANK], b, BANK, ev))
        b = 6
        core.claim(b)
        for k in range(DT):
            mm = core.pe.engine.matmul(core.bank(b, CTX), w[:, k, :], core.hcT[:, k, :], start=(k == 0),
                                       stop=(k == DT - 1))
            if k < DT - 1:
                yield
        ev = core.pe.mark(mm)
        core.feat.release(ev)
        core.freed(b, 1, gate(fc, b, CTX, ev))
        yield


def halves(ap, h):
    return ap.rearrange("p (n s h) -> p n s h", s=2, h=h)


def decay_step(core, lane, way, h, decay, key, query, *events):
    d = halves(decay, h)
    ends = h - 1 if way == 0 else 0
    old, new = (0, 1) if way == 0 else (1, 0)
    n = d.shape[1]
    k = halves(key, h)
    ev = lane.run(lambda e: e.tensor_tensor(k[:, :, old, :], k[:, :, old, :],
                                            d[:, :, new, ends:ends + 1].broadcast_to([P, n, h]), ALU.mult), *events)
    if query is not None:
        q = halves(query, h)
        ev = lane.run(lambda e: e.tensor_tensor(q[:, :, new, :], q[:, :, new, :],
                                                d[:, :, old, ends:ends + 1].broadcast_to([P, n, h]), ALU.mult))
    at = d[:, :, new, ends:ends + 1]
    return lane.run(lambda e: e.tensor_tensor(at, at, d[:, :, old, ends:ends + 1], ALU.mult), ev)


def head_scan(core, h, fill):
    pe, dve, act, pool = core.pe, core.dve, core.act, core.pool
    r = RAW + 3584 * (h % 2)
    q = core.view(r, T)
    f = [core.view(r + T * (d + 1), T) for d in range(2)]
    fc = [core.view(r + 3 * T + CTX * d, CTX) for d in range(2)]
    key = [core.view(UNIT + 3072 * d, T) for d in range(2)]
    query = [core.view(UNIT + 3072 * d + 1024, T) for d in range(2)]
    key_c = [core.view(KC + CTX * d, CTX) for d in range(2)]
    krt = core.view(KRT, NCH * P).rearrange("p (c k) -> p c k", c=NCH)
    states = core.view(SALL, NCH * P).rearrange("p (c v) -> p c v", c=NCH)
    s0 = [core.view(S0 + P * d, P) for d in range(2)]
    head_cols = slice(h * P, (h + 1) * P)
    ready, ready_c = [None] * 2, [None] * 2
    for d in range(2):
        dve.run(lambda e: e.tensor_scalar(key[d], f[d], -1.0, 1.0, ALU.mult, ALU.add), core.f_ok[h],
                core.unit_free[d])
        ready[d] = dve.run(lambda e: e.tensor_tensor(query[d], q, f[d], ALU.mult), core.q_ok[h])
    for d in range(2):
        ev = pool.run(lambda e: e.tensor_scalar(key_c[d], fc[d], -1.0, 1.0, ALU.mult, ALU.add), core.kc_free)
        for lv in LEVELS:
            ev = decay_step(core, pool, d, lv, fc[d], key_c[d], None, ev)
        ready_c[d] = ev
    for n in range(len(LEVELS) + 1):
        for d in range(2):
            b = 2 * d
            core.claim(b, 2)
            pe.after(ready[d])
            rhs = q if n == 0 else query[d]
            for c in range(NCH):
                at = slice(c * CHUNK, (c + 1) * CHUNK)
                mm = pe.engine.matmul(core.bank(b, T)[:, at], key[d][:, at], rhs[:, at], start=True, stop=True)
            paired = pe.mark(mm)
            m = 0 if n == 0 else n + (len(LEVELS) if d else 0)
            mask = core.masks[:, m * P:(m + 1) * P].rearrange("p (a i) -> p a i", a=1).broadcast_to([P, NCH, P])
            ev = dve.run(lambda e: e.copy_predicated(
                core.score[d].rearrange("p (c i) -> p c i", c=NCH), mask,
                core.bank(b, T).rearrange("p (c i) -> p c i", c=NCH)), paired, core.score_free)
            core.freed(b, 2, ev)
            if n > 0:
                ready[d] = decay_step(core, dve, d, LEVELS[n - 1], f[d], key[d], query[d], paired)
            fill(3)
    core.claim(4, 2)
    order_c = [[0, 1], [1, 0]]
    turned = core.turns([(core.bank(4)[:, (2 * d + c) * P:(2 * d + c + 1) * P], key_c[d][:, c * P:(c + 1) * P])
                         for d in range(2) for c in range(2)], ready_c[1], ready_c[0])
    core.kc_free = turned
    kr_ok = act.run(lambda e: e.activation(core.view(KRT, 4 * P), core.bank(4), ACT.Copy), turned, core.krt_free)
    core.freed(4, 1, kr_ok)
    fill(2)
    pe.after(kr_ok, core.v_ok)
    for d in range(2):
        for c in range(2):
            mm = pe.engine.matmul(core.bank(5)[:, (2 * d + c) * P:(2 * d + c + 1) * P], krt[:, 2 * d + c, :],
                                  core.vctx[:, c, head_cols], start=True, stop=True)
    u_ok = pe.mark(mm)
    for d in range(2):
        a, z = order_c[d]
        part = lambda c: core.bank(5)[:, (2 * d + c) * P:(2 * d + c + 1) * P]
        dve.run(lambda e: e.tensor_copy(s0[d], part(a)), u_ok)
        last = z * P + (P - 1 if d == 0 else 0)
        ev = dve.run(lambda e: e.scalar_tensor_tensor(out=s0[d], in0=s0[d], scalar=fc[d][:, last:last + 1],
                                                      in1=part(z), op0=ALU.mult, op1=ALU.add), ready_c[d])
    core.freed(5, 1, ev)
    fill(2)
    oT = core.view(OT + T * h, T)
    for d in range(2):
        core.claim(4, 2)
        turned = core.turns([(core.bank(4, T)[:, c * P:(c + 1) * P], key[d][:, c * P:(c + 1) * P])
                             for c in range(NCH)], ready[d])
        ev = act.run(lambda e: e.activation(core.view(KRT, T), core.bank(4, T), ACT.Copy), turned, u_ok)
        core.freed(4, 2, ev)
        fill(3)
        core.claim(4, 2)
        pe.after(ev)
        for c in range(NCH):
            mm = pe.engine.matmul(core.bank(4, T)[:, c * P:(c + 1) * P], krt[:, c, :], core.v[:, c, head_cols],
                                  start=True, stop=True)
        u_ok = pe.mark(mm)
        seq = list(range(NCH)) if d == 0 else list(range(NCH))[::-1]
        ev = dve.run(lambda e: e.tensor_copy(states[:, seq[0], :], s0[d]), core.states_free)
        for c, nxt in zip(seq, seq[1:]):
            last = c * P + (P - 1 if d == 0 else 0)
            ev = dve.run(lambda e: e.scalar_tensor_tensor(
                out=states[:, nxt, :], in0=states[:, c, :], scalar=f[d][:, last:last + 1],
                in1=core.bank(4, T)[:, c * P:(c + 1) * P], op0=ALU.mult, op1=ALU.add), u_ok)
        core.freed(4, 2, ev)
        fill(4)
        b = 2 * d
        core.claim(b, 2)
        pe.after(ev)
        for c in range(NCH):
            at = slice(c * CHUNK, (c + 1) * CHUNK)
            pe.engine.matmul(core.bank(b, T)[:, at], core.v[:, c, head_cols], core.score[d][:, at], start=True,
                             stop=False)
            mm = pe.engine.matmul(core.bank(b, T)[:, at], states[:, c, :], query[d][:, at], start=False, stop=True)
        done = pe.mark(mm)
        core.states_free = core.krt_free = done
        core.unit_free[d] = done
        if d == 0:
            ev = act.run(lambda e: e.activation(oT, core.bank(b, T), ACT.Copy), done)
        else:
            ev = dve.run(lambda e: e.tensor_tensor(oT, oT, core.bank(b, T), ALU.add), done, ev0)
        ev0 = ev
        core.freed(b, 2, ev)
    core.score_free = done
    core.raw_free[h % 2] = [done, dve.latest, pool.latest]
    square = query[1]
    sq = act.run(lambda e: e.activation(square, oT, ACT.Square), ev)
    core.claim(4, 2)
    pe.after(sq)
    for c in range(NCH):
        mm = pe.engine.matmul(core.bank(4)[:, c:c + 1], square[:, c * P:(c + 1) * P], core.ones[:, 0:1], start=True,
                              stop=True)
    summed = pe.mark(mm)
    rs = core.small[:, 80:88]
    ev = dve.run(lambda e: e.tensor_copy(rs, core.bank(4, NCH)), summed)
    core.freed(4, 1, ev)
    ev = row_scale(core, rs, P, ev)
    fill(4)
    diag = key[1]
    ev = dve.run(lambda e: e.tensor_tensor(
        diag.rearrange("p (c i) -> p c i", c=NCH),
        core.ident[:, :].rearrange("p (a i) -> p a i", a=1).broadcast_to([P, NCH, P]),
        rs.rearrange("p (c a) -> p c a", a=1).broadcast_to([P, NCH, P]), ALU.mult), ev, core.unit_free[1])
    core.claim(4, 2)
    pe.after(ev)
    for half in range(2):
        mm = pe.engine.matmul(core.bank(4 + half), core.ones[:, :], diag[:, half * BANK:(half + 1) * BANK],
                              start=True, stop=True)
    spread = pe.mark(mm)
    core.unit_free[1] = spread
    ev = dve.run(lambda e: e.tensor_tensor(oT, oT, core.bank(4, T), ALU.mult), spread)
    core.freed(4, 2, ev)


def hgrn(core):
    core.stage("hgrn")
    core.raw_free = [core.everything(), core.everything()]
    core.unit_free = [core.everything(), core.everything()]
    core.q_ok, core.f_ok = {}, {}
    core.kc_free = core.krt_free = core.states_free = core.everything()
    for _ in raw_head(core, 0):
        pass
    for h in range(HEADS):
        other = raw_head(core, h + 1) if h + 1 < HEADS else sgu_gates(core)

        def fill(n):
            for _ in range(n):
                next(other, None)
        head_scan(core, h, fill)
        for _ in other:
            pass


def sgu_gates(core):
    core.uT = core.view(YB, GROUPS * T).rearrange("p (g t) -> p g t", g=GROUPS)
    for g in range(GROUPS):
        slot, landed = core.feat.take()
        yield from feature_halves(core, slot, landed, lambda half, b, ev: core.act.run(
            lambda e: e.activation(core.uT[:, g, half * BANK:(half + 1) * BANK], core.bank(b), ACT.Gelu_apprx_tanh),
            ev))
        core.feat.release(core.pe.latest)



def sgu_values(core):
    nw = lambda g: core.col("sgu_norm", g)
    slot, landed = core.wide.take()
    w = tiled(slot, DT)
    gv, squares = core.view(RAW, WIDTH), core.view(RAW + WIDTH, WIDTH)
    sums = core.small[:, 88:92]
    by_group = lambda ap: ap.rearrange("p (g c) -> p g c", g=GROUPS)
    gv_free = core.raw_free[0]
    for t in range(TT):
        core.claim(6)
        core.pe.after(landed)
        for k in range(DT):
            mm = core.pe.engine.matmul(core.bank(6), core.hT[:, k, t * P:(t + 1) * P], w[:, k, :], start=(k == 0),
                                       stop=(k == DT - 1))
        ev = core.pe.mark(mm)
        if t == TT - 1:
            core.wide.release(ev)
        ev = core.act.run(lambda e: e.activation(gv, core.bank(6), ACT.Gelu_apprx_tanh), ev, gv_free)
        core.freed(6, 1, ev)
        sq = core.act.run(lambda e: e.activation(squares, gv, ACT.Square))
        ev = core.dve.run(lambda e: e.tensor_reduce(sums, by_group(squares), AX.X, ALU.add), sq)
        ev = row_scale(core, sums, P, ev)
        ev = core.dve.run(lambda e: e.tensor_tensor(
            by_group(squares), by_group(gv), sums.rearrange("p (g a) -> p g a", a=1).broadcast_to([P, GROUPS, P]),
            ALU.mult))
        yield
        core.claim(7)
        core.pe.after(ev, core.sgu_ok)
        for g in range(GROUPS):
            mm = core.pe.engine.matmul(core.bank(7)[:, g * P:(g + 1) * P], squares[:, g * P:(g + 1) * P],
                                       core.sgu_wT[:, g, :], start=True, stop=True)
        mixed = core.pe.mark(mm)
        gv_free = [mixed, ev]
        tmp = core.view(RAW + 2 * WIDTH, WIDTH)
        for g in range(GROUPS):
            core.dve.run(lambda e: e.scalar_tensor_tensor(
                out=tmp[:, g * P:(g + 1) * P], in0=core.bank(7)[:, g * P:(g + 1) * P], scalar=nw(g),
                in1=core.sgu_bias[:, g * P:(g + 1) * P], op0=ALU.mult, op1=ALU.add), mixed)
        core.freed(7, 1, core.dve.latest)
        ut = core.uT[:, :, t * P:(t + 1) * P]
        core.dve.run(lambda e: e.tensor_tensor(ut, ut, by_group(tmp), ALU.mult), core.u_ok)


def hgrn_gates(core):
    tmp = core.view(RAW + 3 * WIDTH, BANK)
    for h in range(HEADS):
        slot, landed = core.feat.take()

        def gate(half, b, ev):
            s = core.act.run(lambda e: e.activation(tmp, core.bank(b), ACT.Silu), ev, core.gate_free)
            o = core.view(OT + T * h + half * BANK, BANK)
            core.gate_free = core.dve.run(lambda e: e.scalar_tensor_tensor(
                out=o, in0=o, scalar=core.col("hgrn_norm", h), in1=tmp, op0=ALU.mult, op1=ALU.mult), s)
            return s
        yield from feature_halves(core, slot, landed, gate)
        core.feat.release(core.pe.latest)


def merge_loads(ins):
    loads = []
    for at, branch in ((COL_GA, "a"), (COL_GB, "b")):
        for j in range(0, DT, 2):
            loads += [feature_tile(ins["w_in"][0], at + (j + i) * P) for i in range(2)]
            loads.append(feature_tile(ins[f"w_branch_{branch}"][0], j * P, 2 * P))
    return loads


def cut_tiles(core, name, high, low, count, value, *events):
    tiles = [core.split(f"{name}{i}", high + i * T, T, apart=low + i * T) for i in range(count)]
    return tiles, [core.cut(tile, value[:, i, :], core.act, core.dve, *events) for i, tile in enumerate(tiles)]


def merge(core, ins, ring):
    pe, dve, act = core.pe, core.dve, core.act
    core.stage("merge")
    gone = core.everything()
    weights = SplitRing(core, ring, [core.split(f"merge_w{i}", MERGE_PARTS + 2048 * i, T) for i in range(2)],
                        [(act, dve)], len(ring.loads), gone)
    hT, h_ok = cut_tiles(core, "hT_", HT_HIGH, HT, DT, core.hT, gone)
    oT, o_ok = cut_tiles(core, "oT_", OT_HIGH, OT, HEADS,
                         core.view(OT, HEADS * T).rearrange("p (k t) -> p k t", k=HEADS), gone)
    uT, u_ok = cut_tiles(core, "uT_", UT_HIGH, YB, GROUPS, core.uT, gone)
    core.merged = core.view(MERGED, DT * T).rearrange("p (j t) -> p j t", j=DT)
    tmp = [core.view(at, T) for at in MERGE_TMP]
    tmp_free = [gone] * 2

    def product(pair, w, src, src_ok):
        core.claim(pair, 2)
        for half in range(2):
            for k in range(len(src)):
                pe.after(src_ok[k])
                mm = core.products(core.bank(pair + half), [(w[:, k, :], src[k][:, half * BANK:(half + 1) * BANK])],
                                   first=(k == 0), last=(k == len(src) - 1))
        return pe.mark(mm)

    for n, (src, src_ok) in enumerate(((oT, o_ok), (uT, u_ok))):
        for j in range(0, DT, 2):
            gates = []
            for i in range(2):
                w, ready = weights.take()
                pe.after(ready)
                mm = product(2 * i, w.rearrange("p (k n) -> p k n", k=DT), hT, h_ok)
                weights.release(mm)
                gates.append(act.run(lambda e: e.activation(tmp[i], core.bank(2 * i, T), ACT.Sigmoid), mm,
                                     tmp_free[i]))
                core.freed(2 * i, 2, gates[i])
            w, ready = weights.take()
            w = w.rearrange("p (k n) -> p k n", k=4)
            pe.after(ready)
            for i in range(2):
                mm = product(4 + 2 * i, w[:, :, i * P:(i + 1) * P], src, src_ok)
                if i:
                    weights.release(mm)
                out = tmp[i] if n else core.merged[:, j + i, :]
                ev = dve.run(lambda e: e.tensor_tensor(out, tmp[i], core.bank(4 + 2 * i, T), ALU.mult), mm, gates[i],
                             gone)
                core.freed(4 + 2 * i, 2, ev)
                if n:
                    ev = dve.run(lambda e: e.tensor_tensor(core.merged[:, j + i, :], core.merged[:, j + i, :], tmp[i],
                                                           ALU.add))
                tmp_free[i] = core.merged_ok = ev
        if n == 0:
            core.w_out = core.view(WOUT, DT * D).rearrange("p (k n) -> p k n", k=DT)
            core.w_out_ok = Transfers(core.nc, "dma_w_out").start(
                core.sp, core.w_out, ins["w_out"][0].rearrange("(k p) n -> p k n", p=P), mm)


def gain_rows(core):
    nc = core.nc
    core.gain_dram = nc.dram_tensor("gain_rows", (2, D), F32, kind="Internal").ap()
    rows = core.view(S0, 256)[0:DT, :].rearrange("p (n c) -> p n c", n=2)
    core.claim(0)
    turned = core.turns([(core.bank(0)[0:DT, n * P:(n + 1) * P], core.mod_v[:, at:at + DT, 0])
                         for n, at in enumerate((2 * DT, 5 * DT))], core.mod_ok)
    ev = core.dve.run(lambda e: e.tensor_copy(core.view(S0, 256)[0:DT, :], core.bank(0)[0:DT, 0:256]), turned)
    core.freed(0, 1, ev)
    core.gains_stored = Transfers(nc, "dma_gain_store").start(
        core.sp, core.gain_dram.rearrange("n (j c) -> j n c", c=P), rows, ev)
    core.ffn_scale = core.small[:, 96:104]
    a = core.dve.run(lambda e: e.tensor_scalar(core.ffn_scale, core.mod_v[:, 4 * DT:5 * DT, 0], 1.0, None, ALU.add))
    core.ffn_ok = core.dve.run(lambda e: e.tensor_tensor(core.ffn_scale, core.ffn_scale, core.col("norm_ffn", 0, 8),
                                                         ALU.mult), a)


def gain_row(core, name, n, at):
    row = core.view(at, D)
    return row, Transfers(core.nc, name).start(core.sp, row, core.gain_dram[n].partition_broadcast(P),
                                               core.gains_stored, core.everything())


def project_out(core, ins):
    nc, pe, dve, act, sp = core.nc, core.pe, core.dve, core.act, core.sp
    core.x_dram = nc.dram_tensor("x_after_mixer", (T, D), F32, kind="Internal").ap()
    core.xn_dram = nc.dram_tensor("x_normed", (T, D), F32, kind="Internal").ap()
    x_src = ins["x"].rearrange("a (t p) d -> (a t) p d", p=P)
    core.xn = core.view(HT, TT * D).rearrange("p (t d) -> p t d", t=TT)
    xt = [core.view(XT + 1024 * i, D) for i in range(2)]
    ht_free = core.everything()
    gm_row, gm_ok = gain_row(core, "dma_gain_row_m", 0, GM_ROW)
    dma_x = [Transfers(nc, f"dma_x_again{i}") for i in range(2)]
    dma_st = [Transfers(nc, f"dma_x_store{i}") for i in range(2)]
    core.xn_stored = Transfers(nc, "dma_xn_store")
    landed = [dma_x[i].start(sp, xt[i], x_src[i], ht_free) for i in range(2)]
    sums = core.small[:, 104:112]
    for t in range(TT):
        xn = core.xn[:, t, :]
        for half in range(2):
            b = (2 * t + half) % 8
            cols = slice(half * BANK, (half + 1) * BANK)
            core.claim(b)
            mm = core.matmuls(core.bank(b), [(core.merged[:, k, t * P:(t + 1) * P], core.w_out[:, k, cols])
                                             for k in range(DT)], core.w_out_ok, core.merged_ok)
            ev = dve.run(lambda e: e.tensor_tensor(xn[:, cols], core.bank(b), gm_row[:, cols], ALU.mult), mm,
                         gm_ok, ht_free)
            core.freed(b, 1, ev)
        x1 = dve.run(lambda e: e.tensor_tensor(xt[t % 2], xt[t % 2], xn, ALU.add), landed[t % 2])
        st = dma_st[t % 2].start(sp, core.x_dram[t * P:(t + 1) * P, :], xt[t % 2], x1)
        sq = act.run(lambda e: e.activation(xn, xt[t % 2], ACT.Square, accum_out=sums[:, t:t + 1]), x1)
        ev = row_scale(core, sums[:, t:t + 1], D, sq)
        core.xn_ok = dve.run(lambda e: e.tensor_scalar(xn, xt[t % 2], sums[:, t:t + 1], None, ALU.mult), ev)
        core.xn_stored.start(sp, core.xn_dram[t * P:(t + 1) * P, :], xn, core.xn_ok)
        if t + 2 < TT:
            landed[t % 2] = dma_x[t % 2].start(sp, xt[t % 2], x_src[t + 2], st, core.xn_ok)
    core.x_stored = [d.done() for d in dma_st]
    for _ in range(4):
        core.expert.load(core.everything())


STAGED = [8192 + 2048 * i for i in range(8)]
GF_ROW, XS, XST, HID, CUT_W, HIDT, YE, XSF = 48128, 0, 2048, 6144, 24576, 36864, 40960, 43008
H2T, TOPK = 45056, 50176


def expert_loads(ins):
    gate, up, down = (ins[f"expert_w_{n}"][0] for n in ("gate", "up", "down"))
    loads = []
    for e in range(NE):
        for c in range(FF // BANK):
            for w in (gate, up):
                loads += [feature_tile(w[e][r:r + BANK, :], c * BANK, BANK) for r in range(0, D, BANK)]
        for r in range(0, FF, 2 * P):
            loads.append(feature_tile(down[e][r:r + 2 * P, :], 0, D))
    w_in = ins["w_in_2"][0]
    loads += [feature_tile(w_in[r:r + BANK, :], 0, BANK) for r in range(0, D, BANK)]
    loads.append(feature_tile(w_in, AW, 2 * KW))
    return loads


def route(core, ins, router, router_ok):
    pe, dve, act, pool = core.pe, core.dve, core.act, core.pool
    core.stage("route")
    shift = core.mod_v[:, 3 * DT:4 * DT, 0]
    h2 = [core.view(H2T + 1024 * i, T) for i in range(2)]
    h2_free = [core.everything()] * 2
    core.claim(6, 2)
    for j in range(DT):
        ev = turn_and_modulate(core, core.xn, TT, j, 2 * (j % 3), h2[j % 2], core.ffn_scale[:, j:j + 1],
                               shift[:, j:j + 1], core.xn_ok, core.ffn_ok, h2_free[j % 2])
        pe.after(ev, router_ok)
        for half in range(2):
            mm = pe.engine.matmul(core.bank(6 + half)[0:NE, :], router[:, j, :],
                                  h2[j % 2][:, half * BANK:(half + 1) * BANK], start=(j == 0), stop=(j == DT - 1))
        h2_free = list(h2_free)
        h2_free[j % 2] = pe.mark(mm)
    work = core.view(47104, T)[0:NE, :]
    logits = dve.run(lambda e: e.tensor_copy(work, core.bank(6, T)[0:NE, :]), pe.latest)
    core.freed(6, 2, logits)
    core.claim(0)
    turned = core.turns([(core.bank(0)[:, t * NE:(t + 1) * NE], work[:, t * P:(t + 1) * P]) for t in range(TT)],
                        logits)
    aff = core.view(TOPK + 416, TT * NE)
    by_token = lambda ap: ap.rearrange("p (t e) -> p t e", t=TT)
    lo = core.bank(0, TT * NE)
    peak = core.small[:, 112:120]
    wide = lambda ap: ap.rearrange("p (t a) -> p t a", a=1).broadcast_to([P, TT, NE])
    ev = dve.run(lambda e: e.tensor_reduce(peak, by_token(lo), AX.X, ALU.max), turned)
    ev = dve.run(lambda e: e.tensor_tensor(by_token(aff), by_token(lo), wide(peak), ALU.subtract))
    core.freed(0, 1, ev)
    ev = act.run(lambda e: e.activation(aff, aff, ACT.Exp), ev)
    dve.run(lambda e: e.tensor_reduce(peak, by_token(aff), AX.X, ALU.add), ev)
    dve.run(lambda e: e.reciprocal(peak, peak))
    ev = dve.run(lambda e: e.tensor_tensor(by_token(aff), by_token(aff), wide(peak), ALU.mult))
    core.claim(0, 2)
    turned = core.turns([(core.bank(0, T)[0:NE, t * P:(t + 1) * P], by_token(aff)[:, t, :]) for t in range(TT)], ev)
    ev = dve.run(lambda e: e.tensor_copy(work, core.bank(0, T)[0:NE, :]), turned)
    core.freed(0, 2, ev)
    best = core.view(TOPK, CAP)[0:NE, :]
    which = core.view(TOPK + 128, CAP).bitcast(U32)[0:NE, :]
    as_float = core.view(TOPK + 256, CAP)[0:NE, :]
    for r in range(CAP // 8):
        eight = slice(8 * r, 8 * r + 8)
        dve.run(lambda e: e.max(best[:, eight], work))
        dve.run(lambda e: e.max_index(which[:, eight], best[:, eight], work))
        dve.run(lambda e: e.match_replace(work, best[:, eight], work, NEG))
    ev = dve.run(lambda e: e.tensor_copy(as_float, which))
    core.claim(2)
    turned = core.turns([(core.bank(2)[:, 0:NE], best), (core.bank(2)[:, NE:2 * NE], as_float)], ev)
    core.gate = core.view(TOPK + 384, NE)
    core.index = core.view(TOPK + 400, NE).bitcast(U32)
    dve.run(lambda e: e.tensor_copy(core.gate, core.bank(2)[:, 0:NE]), turned)
    core.routed = dve.run(lambda e: e.tensor_copy(core.index, core.bank(2)[:, NE:2 * NE]))
    core.freed(2, 1, core.routed)


def experts(core, ins):
    nc, pe, dve, act, pool = core.nc, core.pe, core.dve, core.act, core.pool
    core.stage("experts")
    shift = core.mod_v[:, 3 * DT:4 * DT, 0]
    area_free = [core.everything(), core.x_stored, core.xn_stored.done()]
    gf_row, gf_ok = gain_row(core, "dma_gain_row_f", 1, GF_ROW)
    dma_xs = [Transfers(nc, f"dma_gather{i}") for i in range(2)]
    dma_ye = [Transfers(nc, f"dma_scatter{i}") for i in range(2)]
    xs = [core.view(XS + 1024 * i, D) for i in range(2)]
    xsT = [core.split(f"xsT{i}", XST + 2048 * i, D).rearrange("p (k c) -> p k c", k=DT) for i in range(2)]
    xsF = core.view(XSF, D).rearrange("p (k c) -> p k c", k=DT)
    hid = core.view(HID, FF)
    hidT = core.split("hidT", HIDT, FF).rearrange("p (k c) -> p k c", k=FF // P)
    ye = [core.view(YE + 1024 * i, D) for i in range(2)]
    lanes = [(act, dve)] * 7 + [(act, pool)]
    weights = SplitRing(core, core.expert, [core.split(f"expert_w{i}", CUT_W + 4096 * i, 2048) for i in range(3)],
                        lanes, 24 * NE, area_free)
    xs_free, xsT_free, ye_free = [area_free] * 2, [area_free] * 2, [area_free] * 2
    xsT_ok, gathered = [None, area_free], [None] * 2
    hid_free, hidT_free = area_free, area_free
    scattered = core.x_stored

    def gather(x):
        i = x % 2
        pool.after(core.routed, core.xn_stored.done(), xs_free[i])
        nc.gpsimd.indirect_dma_start(xs[i], None, core.xn_dram,
                                     bass.IndirectOffsetOnAxis(ap=core.index[:, x:x + 1], axis=0)
                                     ).then_inc(dma_xs[i].sem, 16)
        dma_xs[i].count += 16
        gathered[i] = dma_xs[i].done()

    def turn_inputs(x):
        i = x % 2
        core.claim(4, 2)
        turned = core.turns([(core.bank(4, D)[:, j * P:(j + 1) * P], xs[i][:, j * P:(j + 1) * P])
                             for j in range(DT)], gathered[i])
        xs_free[i] = turned
        for j in range(DT):
            part = core.bank(4, D)[:, j * P:(j + 1) * P]
            if j >= DT // 2:
                dve.run(lambda e: e.tensor_scalar(xsF[:, j, :], part, core.ffn_scale[:, j:j + 1], shift[:, j:j + 1],
                                                  ALU.mult, ALU.add), turned, xsT_ok[1 - i])
            else:
                act.run(lambda e: e.activation(xsF[:, j, :], part, ACT.Identity, bias=shift[:, j:j + 1],
                                               scale=core.ffn_scale[:, j:j + 1]), turned, xsT_ok[1 - i])
        core.freed(4, 2, [dve.latest, act.latest])
        xsT_ok[i] = core.cut(xsT[i], xsF, act, dve, dve.latest, xsT_free[i])

    def turn_hidden(c, ready):
        b = 4 + c % 2
        core.claim(b)
        turned = core.turns([(core.bank(b)[:, k * P:(k + 1) * P], hid[:, (4 * c + k) * P:(4 * c + k + 1) * P])
                             for k in range(4)], ready)
        both = core.cut(hidT[:, 4 * c:4 * c + 4, :], core.bank(b).rearrange("p (k c) -> p k c", k=4), act, dve,
                        turned, hidT_free)
        core.freed(b, 1, both)
        return both

    gather(0)
    gather(1)
    turn_inputs(0)
    for x in range(NE):
        i = x % 2
        hid_ok, hidT_ok = [None] * 4, [None] * 4
        for c in range(FF // BANK):
            cols = slice(c * BANK, (c + 1) * BANK)
            made = []
            for n in range(2):
                b = 2 * (c % 2) + n
                core.claim(b)
                for r in range(2):
                    w, ready = weights.take()
                    w = w.rearrange("p (k n) -> p k n", k=4)
                    pe.after(ready, xsT_ok[i])
                    mm = pe.mark(core.products(core.bank(b), [(xsT[i][:, 4 * r + k, :], w[:, k, :])
                                                              for k in range(4)], first=(r == 0), last=(r == 1)))
                    weights.release(mm)
                made.append(mm)
            s = act.run(lambda e: e.activation(hid[:, cols], core.bank(2 * (c % 2)), ACT.Silu), made[0], hid_free)
            core.freed(2 * (c % 2), 1, s)
            hid_ok[c] = dve.run(lambda e: e.tensor_tensor(hid[:, cols], hid[:, cols], core.bank(2 * (c % 2) + 1),
                                                          ALU.mult), s, made[1])
            core.freed(2 * (c % 2) + 1, 1, hid_ok[c])
            if c:
                hidT_ok[c - 1] = turn_hidden(c - 1, hid_ok[c - 1])
        xsT_free[i] = mm
        core.claim(6, 2)
        for c in range(8):
            if c == 2 and x + 1 < NE:
                turn_inputs(x + 1)
            if c == 2 and x + 2 < NE:
                gather(x + 2)
            if c == 4:
                hidT_ok[3] = turn_hidden(3, hid_ok[3])
                hid_free = [pe.latest]
            w, ready = weights.take()
            w = w.rearrange("p (k n) -> p k n", k=2)
            pe.after(ready, hidT_ok[c // 2])
            for half in range(2):
                mm = core.products(core.bank(6 + half), [(hidT[:, 2 * c + k, :], w[:, k, half * BANK:(half + 1) * BANK])
                                                         for k in range(2)], first=(c == 0), last=(c == 7))
            ev = pe.mark(mm)
            weights.release(ev)
        hidT_free = ev
        for half in range(2):
            cols = slice(half * BANK, (half + 1) * BANK)
            out = dve.run(lambda e: e.scalar_tensor_tensor(
                out=ye[i][:, cols], in0=core.bank(6 + half), scalar=core.gate[:, x:x + 1], in1=gf_row[:, cols],
                op0=ALU.mult, op1=ALU.mult), ev, ye_free[i], gf_ok)
        core.freed(6, 2, out)
        pool.after(out, scattered)
        nc.gpsimd.indirect_dma_start(core.x_dram, bass.IndirectOffsetOnAxis(ap=core.index[:, x:x + 1], axis=0),
                                     ye[i], None, compute_op=ALU.add).then_inc(dma_ye[i].sem, 16)
        dma_ye[i].count += 16
        scattered = ye_free[i] = dma_ye[i].done()
    core.scattered = scattered


H1_HIGH, H1_LOW, X2, JUNK, FINAL_ROW, DIAG = 0, 24576, 32768, 40960, 43008, 44032
WQ, WKV, QK, SQ, ROPED, R1, R2, GAIN, ROPE, VB = (32768, 40960, 45056, 45696, 46336, 46976, 47296, 47616, 48256,
                                                   49792)
QKT, LRU_RING, BLOCKS, LRU_OUT, LRU_W, LRU_TMP = 8192, 14336, 17408, 19456, 32768, 36864
QK_HIGH, PROB, PROBT, OATT, ATT, LRUT = 0, 32768, 34816, 36864, 0, 24576
WOUT_F, WOUT_P, XN3, X3 = 40960, 8192, 32768, 40960
H3, ACTT, UP_RING, UP_PARTS, CONV, G_ROW = 0, 16384, 32768, 35840, (39936, 49152, 50176), 0
FGROUP = 8


def second_start(core, ins):
    nc, pe, dve, act, sp = core.nc, core.pe, core.dve, core.act, core.sp
    core.stage("second")
    gone = core.everything()
    x2 = core.view(X2, TT * D).rearrange("p (t d) -> p t d", t=TT)
    core.xb_dram = nc.dram_tensor("x_second", (T, D), F32, kind="Internal").ap()
    final_row = core.view(FINAL_ROW, D)
    core.final_in = Transfers(nc, "dma_final_row_1").start(sp, final_row,
                                                           ins["final_norm_w"].partition_broadcast(P), gone)
    dma_x2 = [Transfers(nc, f"dma_x2_{i}") for i in range(4)]
    x2_src = core.x_dram.rearrange("(t p) d -> p t d", p=P)
    x2_in = [dma_x2[i].start(sp, x2[:, 2 * i:2 * i + 2, :], x2_src[:, 2 * i:2 * i + 2, :], core.scattered, gone)
             for i in range(4)]
    rows = Transfers(nc, "dma_second_rows")
    core.gain_row = core.view(GAIN, (QH + KVH) * HD)
    gains = core.gain_row.rearrange("p (h c) -> p h c", c=HD)
    for h in range(QH + KVH):
        rows.start(sp, gains[:, h, :], ins["q_norm_g_2" if h < QH else "k_norm_g_2"][0].partition_broadcast(P))
    core.rope = core.view(ROPE, TT * HD)
    core.rows_in = rows.start(sp, core.rope, ins["rope_table"])
    core.blocks = core.view(BLOCKS, 16 * P).rearrange("p (w m j) -> p w m j", w=4, m=LT)
    cleared = dve.run(lambda e: e.memset(core.view(BLOCKS, 16 * P), 0.0), gone)
    w_in = ins["w_in_2"][0]
    core.lru_ring = Ring(nc, sp, "dma_lru", [core.view(LRU_RING + 1024 * i, 1024) for i in range(3)],
                         [feature_tile(w_in, at + c * P) for c in range(LT) for at in (CC_XR, CC_YR)], [gone] * 3)
    blocks = Transfers(nc, "dma_blocks")
    for n, name in enumerate(("wa_f_2", "wx_f_2", "wa_b_2", "wx_b_2")):
        src = ins[name][0].rearrange("(m s) i j -> s i m j", s=2)
        for s in range(2):
            core.blocks_in = blocks.start(sp, core.blocks[s * 64:(s + 1) * 64, n, :, s * 64:(s + 1) * 64], src[s],
                                          cleared)
    sums = core.small[:, 120:128]
    sums2 = core.small[:, 128:136]
    junk = core.view(JUNK, D)
    core.xb_stored = Transfers(nc, "dma_xb_store")
    diagonals = core.view(DIAG, TT * P).rearrange("p (t i) -> p t i", t=TT)
    for t in range(TT):
        ev = act.run(lambda e: e.activation(junk, x2[:, t, :], ACT.Square, accum_out=sums[:, t:t + 1]), x2_in[t // 2], gone)
        if t % 2 == 0:
            continue
        row_scale(core, sums[:, t - 1:t + 1], D, ev)
        for u in (t - 1, t):
            ev = dve.run(lambda e: e.scalar_tensor_tensor(out=x2[:, u, :], in0=x2[:, u, :], scalar=sums[:, u:u + 1],
                                                          in1=final_row, op0=ALU.mult, op1=ALU.mult), core.final_in)
            core.xb_stored.start(sp, core.xb_dram[u * P:(u + 1) * P, :], x2[:, u, :], ev)
            ev = act.run(lambda e: e.activation(junk, x2[:, u, :], ACT.Square, accum_out=sums2[:, u:u + 1]), ev)
        row_scale(core, sums2[:, t - 1:t + 1], D, ev)
        for u in (t - 1, t):
            ready = dve.run(lambda e: e.tensor_scalar(diagonals[:, u, :], core.ident[:, :], sums2[:, u:u + 1], None,
                                                      ALU.mult), gone)
    core.h1T = core.split("h1T", H1_HIGH, DT * T, apart=H1_LOW).rearrange("p (j t) -> p j t", j=DT)
    for j in range(DT):
        core.h1_ok = turn_and_cut(core, x2, j, 2 * (j % 4), core.h1T[:, j, :], core.col("norm1", j), ready, gone,
                                  scales=diagonals)


def second_heads(core, ins):
    nc, pe, dve, act = core.nc, core.pe, core.dve, core.act
    n_heads = QH + KVH
    turned_all = core.pe.latest
    wq, wkv = core.split_tiles("wq", WQ, 2, DT // 2 * AW), core.split("wkv", WKV, DT * 2 * KW)
    w_ok = []
    for n, part in enumerate((*wq, wkv)):
        slot, landed = core.expert.take()
        w_ok.append(core.cut(part, slot, act, dve, landed, turned_all, core.h1_ok, core.xb_stored.done()))
    wq = [w.rearrange("p (k n) -> p k n", k=DT // 2) for w in wq]
    wkv = wkv.rearrange("p (k n) -> p k n", k=DT)
    core.qkT = core.view(QKT, 5 * T).rearrange("p (i t) -> p i t", i=5)
    core.vb = core.view(VB, TT * KW).rearrange("p (t n) -> p t n", t=TT)
    qk, sq, roped = core.view(QK, 640), core.view(SQ, 640), core.view(ROPED, 640)
    r1, r2 = core.view(R1, 320), core.view(R2, 320)
    sums = core.small[:, 136:146]
    ev_gain = dve.run(lambda e: e.tensor_scalar(core.gain_row[:, 0:AW], core.gain_row[:, 0:AW], HD ** -0.5, None,
                                                ALU.mult), core.rows_in)
    by_head = lambda ap: ap.rearrange("p (h c) -> p h c", c=HD)
    parts = lambda ap: ap.rearrange("p (h a s c) -> p h a s c", a=2, s=2, c=HD // 4)
    flat = lambda ap: ap.rearrange("p (h a c) -> p h a c", a=2, c=HD // 4)
    roped_free = None
    turns_free = [core.h1_ok, w_ok]
    def project(t):
        tok = slice(t * P, (t + 1) * P)
        b = 2 * (t % 2)
        core.claim(b, 2)
        pe.after(w_ok, core.h1_ok)
        core.products(core.bank(b), [(core.h1T[:, k, tok], wq[k // 4][:, k % 4, :]) for k in range(DT)])
        return pe.mark(core.products(core.bank(b + 1, 2 * KW), [(core.h1T[:, k, tok], wkv[:, k, :])
                                                                for k in range(DT)]))

    projected = project(0)
    for t in range(TT):
        tok = slice(t * P, (t + 1) * P)
        b = 2 * (t % 2)
        both = core.bank(b, n_heads * HD)
        ev = act.run(lambda e: e.activation(sq, both, ACT.Square), projected)
        act.run(lambda e: e.activation(core.vb[:, t, :], core.bank(b + 1)[:, KW:2 * KW], ACT.Copy), turns_free)
        ev = dve.run(lambda e: e.tensor_reduce(sums, by_head(sq), AX.X, ALU.add), ev)
        ev = row_scale(core, sums, HD, ev)
        dve.run(lambda e: e.tensor_tensor(
            by_head(qk), by_head(both), sums.rearrange("p (h a) -> p h a", a=1).broadcast_to([P, n_heads, HD]),
            ALU.mult), ev)
        core.freed(b, 2, [dve.latest, act.latest])
        ev = dve.run(lambda e: e.tensor_tensor(qk, qk, core.gain_row, ALU.mult), ev_gain)
        table = core.rope[:, t * HD:(t + 1) * HD].rearrange("p (f a c) -> p f a c", f=2, a=2)
        paired = roped[:, 0:AW].rearrange("p (i s a z c) -> p s i a z c", s=2, a=2, z=2, c=HD // 4)
        keys = roped[:, AW:AW + KW].rearrange("p (s a z c) -> p s a z c", a=2, z=2, c=HD // 4)
        for a in range(2):
            angle = lambda f: table[:, f, a, :].rearrange("p (o c) -> p o c", o=1).broadcast_to(
                [P, n_heads, HD // 4])
            lo, hi = parts(qk)[:, :, a, 0, :], parts(qk)[:, :, a, 1, :]
            t1, t2 = flat(r1)[:, :, a, :], flat(r2)[:, :, a, :]
            queries = lambda ap: ap[:, 0:QH, :].rearrange("p (s i) c -> p s i c", s=2)
            for z, first, second, op in ((0, lo, hi, ALU.subtract), (1, hi, lo, ALU.add)):
                dve.run(lambda e: e.tensor_tensor(t1, first, angle(0), ALU.mult))
                dve.run(lambda e: e.tensor_tensor(t2, second, angle(1), ALU.mult))
                dve.run(lambda e: e.tensor_tensor(paired[:, :, :, a, z, :], queries(t1), queries(t2), op), roped_free)
                ready = dve.run(lambda e: e.tensor_tensor(keys[:, :, a, z, :], t1[:, QH:, :], t2[:, QH:, :], op))
        if t + 1 < TT:
            projected = project(t + 1)
        core.claim(4, 2)
        turned = core.turns([(core.bank(4, T)[:, i * P:(i + 1) * P], roped[:, i * P:(i + 1) * P]) for i in range(5)],
                            ready)
        roped_free = turned
        core.qk_ok = act.run(lambda e: e.activation(core.qkT[:, :, tok], core.bank(4, 5 * P).rearrange(
            "p (i t) -> p i t", i=5), ACT.Copy), turned, w_ok)
        core.freed(4, 2, core.qk_ok)


def lru_rates(core):
    dve, act = core.dve, core.act
    lam = core.small[:, 0:8]
    rate, minus, z, s, s2 = (core.small[:, 8 * n:8 * n + 8] for n in (1, 2, 3, 4, 5))
    for d, name in enumerate(("lam_f", "lam_b")):
        dve.run(lambda e: e.tensor_copy(lam[:, 4 * d:4 * d + 4], core.col(name, 0, 4)))
    ev = dve.run(lambda e: e.tensor_scalar(z, lam, -1.0, None, ALU.mult))
    ev = dve.run(lambda e: e.tensor_tensor(z, z, lam, ALU.max))
    ev = act.run(lambda e: e.activation(z, z, ACT.Exp, scale=-1.0), ev)
    dve.run(lambda e: e.tensor_scalar(s, z, 2.0, None, ALU.add), ev)
    dve.run(lambda e: e.reciprocal(s, s))
    dve.run(lambda e: e.tensor_tensor(s, s, z, ALU.mult))
    dve.run(lambda e: e.tensor_tensor(s2, s, s, ALU.mult))
    dve.run(lambda e: e.memset(z, 1.0 / 19))
    for n in range(17, 0, -2):
        dve.run(lambda e: e.tensor_tensor(z, z, s2, ALU.mult))
        dve.run(lambda e: e.tensor_scalar(z, z, 1.0 / n, None, ALU.add))
    dve.run(lambda e: e.tensor_tensor(z, z, s, ALU.mult))
    dve.run(lambda e: e.tensor_scalar(z, z, 2.0, None, ALU.mult))
    dve.run(lambda e: e.tensor_scalar(rate, lam, 0.0, None, ALU.min))
    dve.run(lambda e: e.tensor_tensor(rate, rate, z, ALU.subtract))
    dve.run(lambda e: e.tensor_scalar(rate, rate, LRU_C, None, ALU.mult))
    core.rates_ok = dve.run(lambda e: e.tensor_scalar(minus, rate, -1.0, None, ALU.mult))
    core.rate, core.minus_rate = rate, minus


def lru(core):
    pe, dve, act, pool = core.pe, core.dve, core.act, core.pool
    core.stage("lru")
    gone = core.everything()
    weights = SplitRing(core, core.lru_ring, [core.split(f"lru_w{i}", LRU_W + 2048 * i, 1024) for i in range(2)],
                        [(act, pool)], 2 * LT, gone)
    tile = lambda n: core.view(LRU_TMP + T * n, T)
    xc_of, yr_of = [tile(0), tile(1)], [tile(2), tile(3)]
    a_of, tanh_of, b_of = [tile(4), tile(5)], [tile(6), tile(7)], [tile(8), tile(9)]
    h = tile(10)
    unit_free, gates_ok = [gone] * 2, [None] * 2
    core.lru_out = core.view(LRU_OUT, LT * T).rearrange("p (c t) -> p c t", c=LT)
    xc_free, yr_free, xc_ok, yr_ok = [gone] * 2, [gone] * 2, [None] * 2, [None] * 2

    def project(c):
        i = c % 2
        for pair in (0, 2):
            w, ready = weights.take()
            w = w.rearrange("p (k n) -> p k n", k=DT)
            core.claim(pair, 2)
            pe.after(ready, core.h1_ok)
            for half in range(2):
                mm = core.products(core.bank(pair + half), [(w[:, k, :], core.h1T[:, k, half * BANK:(half + 1) * BANK])
                                                            for k in range(DT)])
            mm = pe.mark(mm)
            weights.release(mm)
            if pair == 0:
                xc, x = xc_of[i], core.bank(0, T)
                tap = lambda n: core.col("lru_conv_w", 4 * n + c)
                ev = act.run(lambda e: e.activation(xc, x, ACT.Identity, bias=core.col("lru_conv_b", c), scale=tap(2)),
                             mm, xc_free[i])
                for n, shift in ((0, 2), (1, 1)):
                    dve.run(lambda e: e.scalar_tensor_tensor(out=xc[:, shift:T], in0=x[:, 0:T - shift], scalar=tap(n),
                                                             in1=xc[:, shift:T], op0=ALU.mult, op1=ALU.add), ev)
                xc_ok[i] = dve.run(lambda e: e.scalar_tensor_tensor(
                    out=xc[:, 0:T - 1], in0=x[:, 1:T], scalar=tap(3), in1=xc[:, 0:T - 1], op0=ALU.mult, op1=ALU.add))
                core.freed(0, 2, xc_ok[i])
            else:
                yr_ok[i] = act.run(lambda e: e.activation(yr_of[i], core.bank(2, T), ACT.Gelu_apprx_tanh), mm,
                                   yr_free[i])
                core.freed(2, 2, yr_ok[i])

    def gates(u):
        c, d = divmod(u, 2)
        i = c % 2
        a, tanh, b = a_of[u % 2], tanh_of[u % 2], b_of[u % 2]
        for n, pair in ((0, 4), (1, 6)):
            core.claim(pair, 2)
            pe.after(xc_ok[i], core.blocks_in)
            for half in range(2):
                mm = pe.engine.matmul(core.bank(pair + half), core.blocks[:, 2 * d + n, c, :],
                                      xc_of[i][:, half * BANK:(half + 1) * BANK], start=True, stop=True)
            gate = pe.mark(mm)
            bias = core.col(("ba_", "bx_")[n] + "fb"[d], c)
            ev = act.run(lambda e: e.activation((tanh, b)[n], core.bank(pair, T), ACT.Sigmoid, bias=bias), gate,
                         unit_free[u % 2])
            core.freed(pair, 2, ev)
        at = 4 * d + c
        act.run(lambda e: e.activation(a, tanh, ACT.Exp, scale=core.rate[:, at:at + 1]), core.rates_ok)
        gates_ok[u % 2] = act.run(lambda e: e.activation(tanh, tanh, ACT.Tanh, scale=core.minus_rate[:, at:at + 1]))

    def recur(u):
        c, d = divmod(u, 2)
        i = c % 2
        a, tanh, b = a_of[u % 2], tanh_of[u % 2], b_of[u % 2]
        xc, out = xc_of[i], core.lru_out[:, c, :]
        dve.run(lambda e: e.tensor_tensor(h, a, a, ALU.mult), gates_ok[u % 2])
        ev = dve.run(lambda e: e.scalar_tensor_tensor(out=tanh, in0=h, scalar=1.0, in1=tanh, op0=ALU.add,
                                                      op1=ALU.mult))
        root = act.run(lambda e: e.activation(tanh, tanh, ACT.Sqrt), ev)
        dve.run(lambda e: e.tensor_tensor(b, b, xc, ALU.mult))
        first = 0 if d == 0 else T - 1
        dve.run(lambda e: e.memset(tanh[:, first:first + 1], 1.0), root)
        dve.run(lambda e: e.tensor_tensor(b, b, tanh, ALU.mult))
        if d == 0:
            unit_free[0] = dve.run(lambda e: e.tensor_tensor_scan(out, a, b, 0.0, ALU.mult, ALU.add), gone)
        else:
            unit_free[1] = dve.run(lambda e: e.tensor_tensor_scan(h[:, ::-1], a[:, ::-1], b[:, ::-1], 0.0, ALU.mult,
                                                                  ALU.add))
            dve.run(lambda e: e.tensor_tensor(out, out, h, ALU.add))
            core.lru_ok = yr_free[i] = dve.run(lambda e: e.tensor_tensor(out, out, yr_of[i], ALU.mult), yr_ok[i])
            xc_free[i] = [core.lru_ok, pe.latest]

    lru_rates(core)
    project(0)
    gates(0)
    for u in range(2 * LT):
        if u % 2 == 0 and u // 2 + 1 < LT:
            project(u // 2 + 1)
        if u // 2 + 2 == LT and u % 2 == 0:
            core.qk = []
            for n in range(5):
                core.qk.append(core.split(f"qk{n}", QK_HIGH + n * T, T, apart=QKT + n * T))
                core.qk_ok = core.cut(core.qk[n], core.qkT[:, n, :], pool, pool, core.qk_ok, pe.latest)
        if u + 1 < 2 * LT:
            gates(u + 1)
        recur(u)


def attention(core):
    pe, dve, act = core.pe, core.dve, core.act
    core.stage("attention")
    gone = core.everything()
    prob = [core.view(PROB + T * i, T) for i in range(2)]
    probT = [core.view(PROBT + T * i, T).rearrange("p (k q) -> p k q", k=TT) for i in range(2)]
    o = core.view(OATT, TT * AW).rearrange("p (t n) -> p t n", t=TT)
    units = [(t, h) for t in range(TT) for h in range(QH)]
    core.lruT = core.split_tiles("lruT", LRUT, LT, T)
    for c in range(LT):
        core.lru_ok = core.cut(core.lruT[c], core.lru_out[:, c, :], act, core.pool, gone)
    w_out = core.ins["w_out_2"][0]
    core.w_out_in = [Transfers(core.nc, f"dma_w_out2_{r}").start(
        core.sp, tiled(core.view(WOUT_F + 2048 * r, 2048), 2),
        w_out[r * 2 * P:(r + 1) * 2 * P, :].rearrange("(k p) n -> p k n", p=P), gone) for r in range(4)]
    peak = [core.small[:, 48 + i:49 + i] for i in range(2)]
    total = [core.small[:, 50 + i:51 + i] for i in range(4)]
    prob_free, probT_free, exp_ok, probT_ok = [gone] * 2, [gone] * 2, [None] * 2, [None] * 2

    def scores(n):
        t, h = units[n]
        i, lo = n % 2, HD * (h // 4)
        tile = h % 4
        core.claim(2 * i, 2)
        pe.after(core.qk_ok)
        for half in range(2):
            mm = core.products(core.bank(2 * i + half), [(core.qk[tile][lo:lo + HD, t * P:(t + 1) * P],
                                                          core.qk[4][lo:lo + HD, half * BANK:(half + 1) * BANK])])
        ev = pe.mark(mm)
        dve.run(lambda e: e.tensor_reduce(peak[i], core.bank(2 * i, T), AX.X, ALU.max), ev, exp_ok[i])
        ev = dve.run(lambda e: e.tensor_scalar(peak[i], peak[i], -1.0, None, ALU.mult))
        exp_ok[i] = act.run(lambda e: e.activation(prob[i], core.bank(2 * i, T), ACT.Exp, bias=peak[i],
                                                   accum_out=total[n % 4]), ev, prob_free[i])
        core.freed(2 * i, 2, exp_ok[i])

    def turn(n):
        i = n % 2
        core.claim(4, 2)
        turned = core.turns([(core.bank(4, T)[:, k * P:(k + 1) * P], prob[i][:, k * P:(k + 1) * P])
                             for k in range(TT)], exp_ok[i])
        prob_free[i] = turned
        half = lambda k: core.view(PROBT + T * i + BANK * k, BANK)
        a = act.run(lambda e: e.activation(half(0), core.bank(4), ACT.Copy), turned, probT_free[i])
        b = dve.run(lambda e: e.tensor_copy(half(1), core.bank(5)), turned, probT_free[i])
        core.freed(4, 1, a)
        core.freed(5, 1, b)
        probT_ok[i] = [a, b]

    def mix(n):
        t, h = units[n]
        i, g = n % 2, h // 4
        b = 6 + i
        core.claim(b)
        pe.after(probT_ok[i])
        for k in range(TT):
            mm = pe.engine.matmul(core.bank(b, HD), probT[i][:, k, :], core.vb[:, k, g * HD:(g + 1) * HD],
                                  start=(k == 0), stop=(k == TT - 1))
        ev = probT_free[i] = pe.mark(mm)
        dve.run(lambda e: e.reciprocal(total[n % 4], total[n % 4]), exp_ok[i])
        core.o_ok = dve.run(lambda e: e.tensor_scalar(o[:, t, h * HD:(h + 1) * HD], core.bank(b, HD), total[n % 4],
                                                      None, ALU.mult), ev)
        core.freed(b, 1, core.o_ok)

    scores(0)
    scores(1)
    for n in range(len(units)):
        turn(n)
        if n + 2 < len(units):
            scores(n + 2)
        mix(n)
    core.attT = core.split("attT", ATT, 4 * T).rearrange("p (j t) -> p j t", j=4)
    for j in range(4):
        b = 2 * (j % 2)
        core.claim(b, 2)
        turned = core.turns([(core.bank(b, T)[:, t * P:(t + 1) * P], o[:, t, j * P:(j + 1) * P]) for t in range(TT)],
                            core.o_ok)
        core.att_ok = core.cut(core.attT[:, j, :], core.bank(b, T), act, dve, turned)
        core.freed(b, 2, core.att_ok)


def second_out(core):
    nc, pe, dve, act, pool, sp = core.nc, core.pe, core.dve, core.act, core.pool, core.sp
    core.stage("second_out")
    gone = core.everything()
    w = [part.rearrange("p (k n) -> p k n", k=2) for part in core.split_tiles("w_out_2_", WOUT_P, 4, 2 * D)]
    w_ok = []
    for r in range(4):
        w_ok.append(core.cut(w[r], tiled(core.view(WOUT_F + 2048 * r, 2048), 2), act,
                             dve, core.w_out_in[r], gone))
    xn3 = core.view(XN3, TT * D).rearrange("p (t d) -> p t d", t=TT)
    core.x3 = core.view(X3, TT * D).rearrange("p (t d) -> p t d", t=TT)
    landed = [Transfers(nc, f"dma_xb{r}").start(sp, core.x3[:, 2 * r:2 * r + 2, :], core.xb_dram[
        r * 2 * P:(r + 1) * 2 * P, :].rearrange("(t p) d -> p t d", p=P), w_ok[r], core.xb_stored.done())
        for r in range(4)]
    sums = core.small[:, 56:64]
    for t in range(TT):
        tok = slice(t * P, (t + 1) * P)
        xt, xn = core.x3[:, t, :], xn3[:, t, :]
        src = lambda k: core.attT[:, k, tok] if k < 4 else core.lruT[k - 4][:, tok]
        pe.after(core.att_ok, core.lru_ok)
        b = 2 * (t % 4)
        core.claim(b, 2)
        for half in range(2):
            cols = slice(half * BANK, (half + 1) * BANK)
            for k in range(DT):
                pe.after(w_ok[k // 2])
                mm = core.products(core.bank(b + half), [(src(k), w[k // 2][:, k % 2, cols])], first=(k == 0),
                                   last=(k == DT - 1))
            mm = pe.mark(mm)
            ev = dve.run(lambda e: e.tensor_tensor(xt[:, cols], xt[:, cols], core.bank(b + half), ALU.add), mm,
                         landed[t // 2])
            core.freed(b + half, 1, ev)
        sq = act.run(lambda e: e.activation(xn, xt, ACT.Square, accum_out=sums[:, t:t + 1]), ev, gone)
        ev = row_scale(core, sums[:, t:t + 1], D, sq)
        ready = dve.run(lambda e: e.tensor_scalar(xn, xt, sums[:, t:t + 1], None, ALU.mult), ev)
    core.h3T = core.split("h3T", H3, DT * T).rearrange("p (j t) -> p j t", j=DT)
    mixed = pe.latest
    for j in range(DT):
        core.h3_ok = turn_and_cut(core, xn3, j, 2 * (j % 4), core.h3T[:, j, :], core.col("norm2", j), ready, mixed)


def ffn_loads(ins):
    up, down = ins["w_up_2"][0], ins["w_down_2"][0]
    loads = []
    for g in range(0, FT, FGROUP):
        for f in range(g, g + FGROUP):
            loads += [feature_tile(up, f * P), feature_tile(up, DFF + f * P)]
        for half in range(2):
            for k in range(g, g + FGROUP, 2):
                loads.append(feature_tile(down[k * P:(k + 2) * P, :], half * BANK, BANK))
    return loads


def ffn(core, ins, out):
    nc, pe, dve, act, pool, sp = core.nc, core.pe, core.dve, core.act, core.pool, core.sp
    core.stage("ffn")
    turned = pe.latest
    ring = Ring(nc, sp, "dma_ffn", [core.view(UP_RING + 1024 * i, 1024) for i in range(3)], ffn_loads(ins),
                [turned] * 3)
    parts = [core.split(f"ffn_w{i}", UP_PARTS + 2048 * i, 1024) for i in range(2)]
    weights = SplitRing(core, ring, parts, [(act, dve)], len(ring.loads), turned)
    actT = core.split_tiles("actT", ACTT, FGROUP, T)
    conv = [core.view(at, T) for at in CONV]
    conv_free = [core.everything()] * 3
    act_free, act_ok = turned, [None] * FGROUP
    used = 0
    sums = core.small[:, 64:72]
    dma_out = [Transfers(nc, f"dma_out{i}") for i in range(4)]
    g_row = core.view(G_ROW, D)
    y = [core.view(G_ROW + D * (i + 1), D) for i in range(4)]
    junk, squared = core.view(G_ROW + 5 * D, D), []

    def finish(pair, squared):
        row_scale(core, sums[:, pair:pair + 2], D, squared)
        for t in (pair, pair + 1):
            i = t % 4
            ev = dve.run(lambda e: e.scalar_tensor_tensor(out=y[i], in0=core.x3[:, t, :], scalar=sums[:, t:t + 1],
                                                          in1=g_row, op0=ALU.mult, op1=ALU.mult), rows_in, y_free[i])
            y_free[i] = dma_out[i].start(sp, out[0, t * P:(t + 1) * P, :], y[i], ev)

    for g in range(0, FT, FGROUP):
        for f in range(g, g + FGROUP):
            made = []
            for n in range(2):
                i, pair = used % 3, 2 * (used % 4)
                used += 1
                w, ready = weights.take()
                w = w.rearrange("p (k n) -> p k n", k=DT)
                core.claim(pair, 2)
                pe.after(ready, core.h3_ok)
                for half in range(2):
                    mm = core.products(core.bank(pair + half), [
                        (w[:, k, :], core.h3T[:, k, half * BANK:(half + 1) * BANK]) for k in range(DT)])
                mm = pe.mark(mm)
                weights.release(mm)
                u, c, at = core.bank(pair, T), conv[i], n * FT + f
                ev = act.run(lambda e: e.activation(c, u, ACT.Identity, bias=core.col("up_conv_b", at),
                                                    scale=core.col("up_conv_w01", 2 * FT + at)), mm, conv_free[i])
                dve.run(lambda e: e.scalar_tensor_tensor(out=c[:, 1:T], in0=u[:, 0:T - 1],
                                                         scalar=core.col("up_conv_w01", at), in1=c[:, 1:T],
                                                         op0=ALU.mult, op1=ALU.add), ev)
                ev = dve.run(lambda e: e.scalar_tensor_tensor(out=c[:, 0:T - 1], in0=u[:, 1:T],
                                                              scalar=core.col("up_conv_w2", at), in1=c[:, 0:T - 1],
                                                              op0=ALU.mult, op1=ALU.add))
                core.freed(pair, 2, ev)
                if n == 0:
                    ev = act.run(lambda e: e.activation(c, c, ACT.Gelu_apprx_tanh), ev)
                made.append((ev, i))
            (gate_ok, gi), (value_ok, vi) = made
            ev = dve.run(lambda e: e.tensor_tensor(conv[vi], conv[gi], conv[vi], ALU.mult), gate_ok, value_ok)
            act_ok[f - g] = core.cut(actT[f - g], conv[vi], act, pool, ev, act_free)
            conv_free[gi], conv_free[vi] = ev, act_ok[f - g]
        last_group = g + FGROUP == FT
        if last_group:
            rows_in = Transfers(nc, "dma_final_row").start(sp, g_row, ins["final_g_2"].partition_broadcast(P), mm)
            y_free = [mm] * 4
        for half in range(2):
            cols = slice(half * BANK, (half + 1) * BANK)
            ends = [None] * TT
            for kk in range(FGROUP // 2):
                w, ready = weights.take()
                w = w.rearrange("p (k n) -> p k n", k=2)
                pe.after(ready, act_ok[2 * kk], act_ok[2 * kk + 1])
                last = kk == FGROUP // 2 - 1
                for t in range(TT):
                    if kk == 0:
                        core.claim(t)
                    mm = core.products(core.bank(t), [(actT[2 * kk + k][:, t * P:(t + 1) * P], w[:, k, :])
                                                      for k in range(2)], first=(kk == 0), last=last)
                    if last:
                        ends[t] = pe.mark(mm)
                if not last:
                    pe.mark(mm)
                weights.release(pe.latest)
            act_free = pe.latest
            for t in range(TT):
                xt = core.x3[:, t, :]
                ev = dve.run(lambda e: e.tensor_tensor(xt[:, cols], xt[:, cols], core.bank(t), ALU.add), ends[t])
                core.freed(t, 1, ev)
                if half and last_group:
                    squared.append(act.run(lambda e: e.activation(junk, xt, ACT.Square, accum_out=sums[:, t:t + 1]),
                                           ev, y_free[0] if t == 0 else None))
                    if t % 2 and t > 1:
                        finish(t - 3, squared[t - 2])
    finish(TT - 2, squared[TT - 1])
    sp.after(y_free)


def build_block_pair(nc, ins, out):
    core = Core(nc)
    core.gate_free = None
    core.ins = ins
    start(core, ins)
    core.stage("values")
    values(core)
    turn_spatial(core)
    hgrn(core)
    core.u_ok = core.act.latest
    core.gate_free = core.raw_free[0]
    core.stage("sgu")
    scanned = core.everything()
    ada = Ring(nc, core.sp, "dma_ada_rest", [core.view(at, 4096) for at in ADA_REST],
               [feature_tile(ins["ada_w"][0], c * BANK, BANK) for c in range(4, 12)], [scanned] * 3)
    merge_ring = Ring(nc, core.sp, "dma_merge", [core.view(MERGE_RING + 1024 * i, 1024) for i in range(3)],
                      merge_loads(ins), [scanned] * 3)
    chunks = iter(range(4, 12))
    for _ in sgu_values(core):
        c = next(chunks)
        for _ in ada_chunk(core, ada, c, 4 + c % 2):
            pass
    for _ in hgrn_gates(core):
        pass
    gain_rows(core)
    router = core.view(TOPK + 544, DT * NE).rearrange("p (k e) -> p k e", k=DT)
    router_ok = Transfers(nc, "dma_router").start(core.sp, router,
                                                  ins["router_w"][0].rearrange("(k p) e -> p k e", p=P),
                                                  core.everything())
    merge(core, ins, merge_ring)
    core.stage("out")
    core.expert = Ring(nc, core.sp, "dma_expert", [core.view(at, 2048) for at in STAGED], expert_loads(ins),
                       [core.everything()] * 4)
    project_out(core, ins)
    route(core, ins, router, router_ok)
    experts(core, ins)
    second_start(core, ins)
    second_heads(core, ins)
    lru(core)
    attention(core)
    second_out(core)
    ffn(core, ins, out)


def kernel(**inputs):
    import concourse.bacc as bacc
    from concourse.bass_utils import run_bass_kernel_spmd

    nc = bacc.Bacc("TRN2", target_bir_lowering=False, num_devices=1)
    arrays, ins = {}, {}
    for name, a in list(inputs.items()) + list(shape_constants().items()):
        a = np.ascontiguousarray(a)
        arrays[f"in_{name}"] = a
        ins[name] = nc.dram_tensor(f"in_{name}", a.shape, mybir.dt.from_np(a.dtype), kind="ExternalInput").ap()
    out = nc.dram_tensor("out", (1, T, D), F32, kind="ExternalOutput").ap()
    build_block_pair(nc, ins, out)
    r = run_bass_kernel_spmd(nc, [arrays], core_ids=[0])
    return r.results[0]["out"]
```
